# Optimizing a Trainium2 kernel written in Bass

```python
import jax, jax.numpy as jnp
from jax import lax
import numpy as np

D_MODEL = 1024
BATCH = 1
SEQ = 1024
DEPTH = 1
DEC_BATCH = 8
DEC_SEQ = 4
PAST_LEN = 2048
PAGE_SIZE = 128

MIX_WIDTH = D_MODEL
GROUP_WIDTH = MIX_WIDTH // 4
HEAD_DIM = 64
GLA_HEADS = GROUP_WIDTH // HEAD_DIM
GLA_RANK = 16
GLA_TAU = 16.0
GLA_CHUNK = 64
FOX_HEADS = GROUP_WIDTH // HEAD_DIM
FOX_QBLOCK = 128
FORGET_BIAS = 3.0
CONV_CH = GROUP_WIDTH
CONV_WIDTH = 31
POOL_CH = GROUP_WIDTH
POOL_WINDOWS = (2, 4, 8, 16)
POOL_GROUPS = 4
POOL_GC = POOL_CH // POOL_GROUPS
POOL_MAX = 16
MOE_GROUPS = 4
EXPERTS_PER_GROUP = 4
N_EXPERTS = MOE_GROUPS * EXPERTS_PER_GROUP
TOP_K_INNER = 2
D_EXPERT = D_MODEL // 2
EPS = 1e-6

IN_SIZES = (GROUP_WIDTH, GROUP_WIDTH, GROUP_WIDTH, GROUP_WIDTH, GLA_RANK,
            GROUP_WIDTH, GROUP_WIDTH, GROUP_WIDTH, FOX_HEADS,
            CONV_CH, CONV_CH, POOL_CH)
IN_SPLITS = tuple(sum(IN_SIZES[:i + 1]) for i in range(len(IN_SIZES) - 1))
N_IN = sum(IN_SIZES)

kernel_name = 'hybrid_gla_fox_conv_pool_hmoe_step'

F32 = jnp.float32

def rms_norm(x, g):
    xf = x.astype(F32)
    y = xf * lax.rsqrt(jnp.mean(xf * xf, axis=-1, keepdims=True) + EPS)
    return (y * g.astype(F32)).astype(x.dtype)

def layer_norm(x, g, b):
    xf = x.astype(F32)
    mu = jnp.mean(xf, axis=-1, keepdims=True)
    var = jnp.mean(jnp.square(xf - mu), axis=-1, keepdims=True)
    y = (xf - mu) * lax.rsqrt(var + EPS) * g.astype(F32) + b.astype(F32)
    return y.astype(x.dtype)

def gla_chunk_step(S, inp):
    q, k, v, la = inp
    C = q.shape[2]
    b = jnp.cumsum(la, axis=2)
    inter = jnp.einsum('bhtd,bhde->bhte', q * jnp.exp(b), S)
    causal = jnp.tril(jnp.ones((C, C), dtype=bool))
    diff = b[:, :, :, None, :] - b[:, :, None, :, :]
    decay = jnp.exp(jnp.where(causal[:, :, None], diff, -jnp.inf))
    A = jnp.einsum('bhtd,bhsd,bhtsd->bhts', q, k, decay)
    o = inter + jnp.einsum('bhts,bhse->bhte', A, v)
    b_last = b[:, :, -1:, :]
    S_new = jnp.exp(b_last[:, :, 0, :])[..., None] * S + jnp.einsum('bhsd,bhse->bhde', k * jnp.exp(b_last - b), v)
    return S_new, o

def gla_run(S0, q, k, v, la):
    B, L, H, dk = q.shape
    C = GLA_CHUNK if L % GLA_CHUNK == 0 else L
    n = L // C

    def to_chunks(t):
        t = t.astype(F32).transpose(0, 2, 1, 3).reshape(B, H, n, C, t.shape[-1])
        return jnp.moveaxis(t, 2, 0)

    S, o = lax.scan(gla_chunk_step, S0.astype(F32),
                    (to_chunks(q * (dk ** -0.5)), to_chunks(k), to_chunks(v), to_chunks(la)))
    o = jnp.moveaxis(o, 0, 2).reshape(B, H, L, -1).transpose(0, 2, 1, 3)
    return o, S

def fox_attend(q, cq, qpos, k_all, v_all, c_allT):
    s = jnp.einsum('bqhd,bkhd->bhqk', q, k_all).astype(F32) * (HEAD_DIM ** -0.5)
    s = s + jnp.swapaxes(cq, 1, 2)[..., None] - c_allT[:, :, None, :]
    mask = jnp.arange(k_all.shape[1])[None, :] <= qpos[:, None]
    p = jax.nn.softmax(jnp.where(mask, s, -jnp.inf), axis=-1)
    return jnp.einsum('bhqk,bkhd->bqhd', p.astype(v_all.dtype), v_all)

def fox_run(q, k, v, log_f, past):
    if past is None:
        k_all, v_all, lf_all, P = k, v, log_f, 0
    else:
        kp, vp, lfp = past
        k_all = jnp.concatenate([kp, k], axis=1)
        v_all = jnp.concatenate([vp, v], axis=1)
        lf_all = jnp.concatenate([lfp.astype(F32), log_f], axis=1)
        P = kp.shape[1]
    c_all = jnp.cumsum(lf_all.astype(F32), axis=1)
    c_allT = jnp.swapaxes(c_all, 1, 2)
    cq = c_all[:, P:]
    B, L, H, dh = q.shape
    qpos = P + jnp.arange(L)
    if L % FOX_QBLOCK == 0 and L > FOX_QBLOCK:
        nb = L // FOX_QBLOCK
        qb = jnp.moveaxis(q.reshape(B, nb, FOX_QBLOCK, H, dh), 1, 0)
        cb = jnp.moveaxis(cq.reshape(B, nb, FOX_QBLOCK, H), 1, 0)
        pb = qpos.reshape(nb, FOX_QBLOCK)
        o = lax.map(lambda a: fox_attend(a[0], a[1], a[2], k_all, v_all, c_allT), (qb, cb, pb))
        o = jnp.moveaxis(o, 0, 1).reshape(B, L, H, dh)
    else:
        o = fox_attend(q, cq, qpos, k_all, v_all, c_allT)
    return o

def causal_dwconv(u_ext, w, b):
    y = lax.conv_general_dilated(u_ext, w[:, None, :], window_strides=(1,), padding='VALID',
                                 dimension_numbers=('NWC', 'WIO', 'NWC'),
                                 feature_group_count=u_ext.shape[-1])
    return y + b

def pool_mix(u, prefix, start, pool_w, pool_scale):
    B, L, _ = u.shape
    ext = jnp.concatenate([prefix.astype(u.dtype), u], axis=1)
    cs = jnp.cumsum(ext.astype(F32), axis=1)
    cs0 = jnp.concatenate([jnp.zeros((B, 1, POOL_CH), F32), cs], axis=1)
    pos = start + jnp.arange(L)
    means = []
    for g, w in enumerate(POOL_WINDOWS):
        sl = slice(g * POOL_GC, (g + 1) * POOL_GC)
        win_sum = cs0[:, POOL_MAX:POOL_MAX + L, sl] - cs0[:, POOL_MAX - w:POOL_MAX - w + L, sl]
        cnt = jnp.minimum(w, pos + 1).astype(F32)
        means.append(win_sum / cnt[None, :, None])
    d = (jnp.concatenate(means, axis=-1) - u.astype(F32)).reshape(B, L, POOL_GROUPS, POOL_GC)
    y = jnp.einsum('blgc,gcd->blgd', d, pool_w.astype(F32)).reshape(B, L, POOL_CH) * pool_scale.astype(F32)
    return y.astype(u.dtype), ext[:, -(POOL_MAX - 1):]

def hier_moe(h, wg, bg, we, be, w_gate, w_up, w_down):
    B, L, D = h.shape
    hf = h.reshape(B * L, D)
    g_logits = (hf @ wg + bg).astype(F32)
    _, g_idx = lax.top_k(g_logits, 1)
    p_group = jnp.take_along_axis(jax.nn.softmax(g_logits, axis=-1), g_idx, axis=-1)
    e_logits = (hf @ we + be).astype(F32).reshape(-1, MOE_GROUPS, EXPERTS_PER_GROUP)
    e_in = jnp.take_along_axis(e_logits, g_idx[:, :, None], axis=1)[:, 0]
    top_v, top_i = lax.top_k(e_in, TOP_K_INNER)
    gate = jax.nn.softmax(top_v, axis=-1) * p_group
    e_idx = g_idx * EXPERTS_PER_GROUP + top_i
    combine = jnp.sum(jax.nn.one_hot(e_idx, N_EXPERTS, dtype=F32) * gate[..., None], axis=1).astype(h.dtype)
    y = jnp.zeros_like(hf)
    for e in range(N_EXPERTS):
        he = jax.nn.silu(hf @ w_gate[e]) * (hf @ w_up[e])
        y = y + combine[:, e:e + 1] * (he @ w_down[e])
    return y.reshape(B, L, D)

def layer(x, p, gla_s0, conv_prefix, pool_prefix, fox_past, start):
    bsz, seq_len, _ = x.shape
    h = rms_norm(x, p['norm1_g'])
    z = h @ p['w_in']
    (g_q, g_k, g_v, g_g, g_a, f_q, f_k, f_v, f_f, c_a, c_b, p_u) = jnp.split(z, IN_SPLITS, axis=-1)

    def gheads(t):
        return t.reshape(bsz, seq_len, GLA_HEADS, HEAD_DIM)

    def fheads(t):
        return t.reshape(bsz, seq_len, FOX_HEADS, HEAD_DIM)

    log_alpha = jax.nn.log_sigmoid((g_a @ p['gla_w_a2'] + p['gla_b_a']).astype(F32)) / GLA_TAU
    o_gla, gla_state = gla_run(gla_s0, gheads(g_q), gheads(g_k), gheads(g_v), gheads(log_alpha))
    o_gla = rms_norm(o_gla.astype(x.dtype), p['gla_norm_g'].reshape(GLA_HEADS, HEAD_DIM)) * jax.nn.silu(gheads(g_g))
    o_gla = o_gla.reshape(bsz, seq_len, GROUP_WIDTH)

    fq = rms_norm(fheads(f_q), p['fox_q_norm_g'])
    fk = rms_norm(fheads(f_k), p['fox_k_norm_g'])
    fv = fheads(f_v)
    log_f = jax.nn.log_sigmoid((f_f + p['fox_b_f']).astype(F32))
    o_fox = fox_run(fq, fk, fv, log_f, fox_past).reshape(bsz, seq_len, GROUP_WIDTH)

    u = c_a * jax.nn.sigmoid(c_b)
    u_ext = jnp.concatenate([conv_prefix.astype(u.dtype), u], axis=1)
    o_conv = jax.nn.silu(layer_norm(causal_dwconv(u_ext, p['conv_w'], p['conv_b']), p['conv_ln_g'], p['conv_ln_b']))
    conv_state = u_ext[:, -(CONV_WIDTH - 1):]

    o_pool, pool_state = pool_mix(p_u, pool_prefix, start, p['pool_w'], p['pool_scale'])

    mix = jnp.concatenate([o_gla, o_fox, o_conv.astype(x.dtype), o_pool], axis=-1)
    x = x + mix @ p['w_out']
    x = x + hier_moe(rms_norm(x, p['norm2_g']), p['router_wg'], p['router_bg'], p['router_we'], p['router_be'],
                     p['exp_w_gate'], p['exp_w_up'], p['exp_w_down'])
    return x, (fk, fv, log_f.astype(x.dtype), gla_state.astype(x.dtype), conv_state, pool_state)

def setup_inputs(seed: int = 0) -> dict:
    key = jax.random.key(seed)
    ks = iter(jax.random.split(key, 48))

    def nrm(shape, scale):
        return jax.random.normal(next(ks), shape, F32) * scale

    n_pages = PAST_LEN // PAGE_SIZE
    n_used = DEC_BATCH * n_pages
    n_pool = n_used + max(1, n_used // 4)
    return {
        'x_prompt': nrm((BATCH, SEQ, D_MODEL), 1.0),
        'x_sample': nrm((DEC_BATCH, DEC_SEQ, D_MODEL), 1.0),
        'cache_k': nrm((DEPTH, n_pool, PAGE_SIZE, FOX_HEADS, HEAD_DIM), 1.0),
        'cache_v': nrm((DEPTH, n_pool, PAGE_SIZE, FOX_HEADS, HEAD_DIM), 1.0),
        'cache_logf': jax.nn.log_sigmoid(FORGET_BIAS + nrm((DEPTH, n_pool, PAGE_SIZE, FOX_HEADS), 1.0)),
        'page_table': jax.random.permutation(next(ks), n_pool)[:n_used].reshape(DEC_BATCH, n_pages).astype(jnp.int32),
        'state_gla': nrm((DEPTH, DEC_BATCH, GLA_HEADS, HEAD_DIM, HEAD_DIM), 0.5),
        'state_conv': nrm((DEPTH, DEC_BATCH, CONV_WIDTH - 1, CONV_CH), 0.5),
        'state_pool': nrm((DEPTH, DEC_BATCH, POOL_MAX - 1, POOL_CH), 1.0),
        'norm1_g': 1.0 + nrm((DEPTH, D_MODEL), 0.02),
        'w_in': nrm((DEPTH, D_MODEL, N_IN), D_MODEL ** -0.5),
        'gla_w_a2': nrm((DEPTH, GLA_RANK, GROUP_WIDTH), GLA_RANK ** -0.5),
        'gla_b_a': nrm((DEPTH, GROUP_WIDTH), 0.02),
        'gla_norm_g': 1.0 + nrm((DEPTH, GROUP_WIDTH), 0.02),
        'fox_b_f': FORGET_BIAS + nrm((DEPTH, FOX_HEADS), 0.1),
        'fox_q_norm_g': 1.0 + nrm((DEPTH, HEAD_DIM), 0.02),
        'fox_k_norm_g': 1.0 + nrm((DEPTH, HEAD_DIM), 0.02),
        'conv_w': nrm((DEPTH, CONV_WIDTH, CONV_CH), CONV_WIDTH ** -0.5),
        'conv_b': nrm((DEPTH, CONV_CH), 0.02),
        'conv_ln_g': 1.0 + nrm((DEPTH, CONV_CH), 0.02),
        'conv_ln_b': nrm((DEPTH, CONV_CH), 0.02),
        'pool_w': nrm((DEPTH, POOL_GROUPS, POOL_GC, POOL_GC), POOL_GC ** -0.5),
        'pool_scale': 1.0 + nrm((DEPTH, POOL_CH), 0.1),
        'w_out': nrm((DEPTH, MIX_WIDTH, D_MODEL), MIX_WIDTH ** -0.5),
        'norm2_g': 1.0 + nrm((DEPTH, D_MODEL), 0.02),
        'router_wg': nrm((DEPTH, D_MODEL, MOE_GROUPS), D_MODEL ** -0.5),
        'router_bg': nrm((DEPTH, MOE_GROUPS), 0.01),
        'router_we': nrm((DEPTH, D_MODEL, N_EXPERTS), D_MODEL ** -0.5),
        'router_be': nrm((DEPTH, N_EXPERTS), 0.01),
        'exp_w_gate': nrm((DEPTH, N_EXPERTS, D_MODEL, D_EXPERT), D_MODEL ** -0.5),
        'exp_w_up': nrm((DEPTH, N_EXPERTS, D_MODEL, D_EXPERT), D_MODEL ** -0.5),
        'exp_w_down': nrm((DEPTH, N_EXPERTS, D_EXPERT, D_MODEL), D_EXPERT ** -0.5),
    }

def reference(x_prompt, x_sample, cache_k, cache_v, cache_logf, page_table, state_gla, state_conv, state_pool,
              norm1_g, w_in, gla_w_a2, gla_b_a, gla_norm_g, fox_b_f, fox_q_norm_g, fox_k_norm_g,
              conv_w, conv_b, conv_ln_g, conv_ln_b, pool_w, pool_scale, w_out, norm2_g,
              router_wg, router_bg, router_we, router_be, exp_w_gate, exp_w_up, exp_w_down):
    dec_b, n_pages = page_table.shape
    past = n_pages * PAGE_SIZE
    bsz = x_prompt.shape[0]
    xp, xs = x_prompt, x_sample
    kp_l, vp_l, lfp_l, ks_l, vs_l, lfs_l = [], [], [], [], [], []
    glap_l, glas_l, convp_l, convs_l, poolp_l, pools_l = [], [], [], [], [], []
    for l in range(DEPTH):
        p = {
            'norm1_g': norm1_g[l], 'w_in': w_in[l], 'gla_w_a2': gla_w_a2[l], 'gla_b_a': gla_b_a[l],
            'gla_norm_g': gla_norm_g[l], 'fox_b_f': fox_b_f[l], 'fox_q_norm_g': fox_q_norm_g[l],
            'fox_k_norm_g': fox_k_norm_g[l], 'conv_w': conv_w[l], 'conv_b': conv_b[l],
            'conv_ln_g': conv_ln_g[l], 'conv_ln_b': conv_ln_b[l], 'pool_w': pool_w[l],
            'pool_scale': pool_scale[l], 'w_out': w_out[l], 'norm2_g': norm2_g[l],
            'router_wg': router_wg[l], 'router_bg': router_bg[l], 'router_we': router_we[l],
            'router_be': router_be[l], 'exp_w_gate': exp_w_gate[l], 'exp_w_up': exp_w_up[l],
            'exp_w_down': exp_w_down[l],
        }
        xp, sp = layer(xp, p,
                       jnp.zeros((bsz, GLA_HEADS, HEAD_DIM, HEAD_DIM), F32),
                       jnp.zeros((bsz, CONV_WIDTH - 1, CONV_CH), xp.dtype),
                       jnp.zeros((bsz, POOL_MAX - 1, POOL_CH), xp.dtype),
                       None, 0)
        fox_past = (cache_k[l][page_table].reshape(dec_b, past, FOX_HEADS, HEAD_DIM),
                    cache_v[l][page_table].reshape(dec_b, past, FOX_HEADS, HEAD_DIM),
                    cache_logf[l][page_table].reshape(dec_b, past, FOX_HEADS))
        xs, ss = layer(xs, p, state_gla[l], state_conv[l], state_pool[l], fox_past, past)
        kp_l.append(sp[0]); vp_l.append(sp[1]); lfp_l.append(sp[2])
        glap_l.append(sp[3]); convp_l.append(sp[4]); poolp_l.append(sp[5])
        ks_l.append(ss[0]); vs_l.append(ss[1]); lfs_l.append(ss[2])
        glas_l.append(ss[3]); convs_l.append(ss[4]); pools_l.append(ss[5])
    k_prompt = jnp.stack(kp_l); v_prompt = jnp.stack(vp_l); logf_prompt = jnp.stack(lfp_l)
    k_sample = jnp.stack(ks_l); v_sample = jnp.stack(vs_l); logf_sample = jnp.stack(lfs_l)
    gla_prompt = jnp.stack(glap_l); gla_sample = jnp.stack(glas_l)
    conv_prompt = jnp.stack(convp_l); conv_sample = jnp.stack(convs_l)
    pool_prompt = jnp.stack(poolp_l); pool_sample = jnp.stack(pools_l)
    return (xp, xs, k_prompt, v_prompt, logf_prompt, k_sample, v_sample, logf_sample,
            gla_prompt, gla_sample, conv_prompt, conv_sample, pool_prompt, pool_sample)


_drawn_inputs = setup_inputs


def setup_inputs(seed=0):
    import zlib

    import numpy as np

    out = dict(_drawn_inputs(seed))
    spreads = {}
    factors = {'gla_b_a': 6.604,
     'gla_norm_g': 14.281,
     'fox_q_norm_g': 38.719,
     'conv_b': 3.09,
     'conv_ln_g': 13.762,
     'conv_ln_b': 12.531,
     'router_bg': 12.78,
     'router_be': 21.425,
     'norm2_g': 4.837,
     'cache_logf': 5.244}
    for name, (base, spread) in spreads.items():
        noise = np.random.default_rng([zlib.crc32(name.encode()), seed]).standard_normal(out[name].shape)
        drawn = base * np.exp(spread * noise) if base else spread * noise
        out[name] = __import__('jax').numpy.asarray(drawn.astype(out[name].dtype))
    for name, factor in factors.items():
        out[name] = (out[name] * factor).astype(out[name].dtype)
    return out
```

```python
from contextlib import ExitStack

import concourse.bass as bass
from concourse import mybir
from concourse.bass import ds

F32 = mybir.dt.float32
I32 = mybir.dt.int32
ALU = mybir.AluOpType
ACT = mybir.ActivationFunctionType
AX = mybir.AxisListType

P = 128
D = 1024
KC = D // P
SEQ = 1024
DEC_B, DEC_L = 8, 4
NS = DEC_B * DEC_L
TOK = SEQ + NS
NT = SEQ // P + 1
W = 256
H, HD = 4, 64
RANK = 16
TAU = 16.0
TAPS = 31
PMAX = 16
WINDOWS = (2, 4, 8, 16)
PAGE = 128
NPG = 16
POOLPG = 160
PAST = NPG * PAGE
EPS = 1e-6
NEG = -1e30
NE, NG = 16, 4
DE = 512
SLOT_TILES = (2 * TOK) // P + NE
LEAST_PAIRS = (-(-2 * TOK // P) + 1) // 2
CH = 352
NCH = TOK // CH

GQ, GK, GV, GG, GA, FQ, FK, FV, FF, CA, CB, PU = 0, 256, 512, 768, 1024, 1040, 1296, 1552, 1808, 1812, 2068, 2324
N_IN = PU + W
Z_GROUPS = (GQ, GK, GG, FQ, FK, CA, CB, PU)
ZQ, ZK, ZG, ZFQ, ZFK, ZCA, ZCB, ZPU = range(0, 16, 2)
FROW = 32


class Memory:
    pass


def rows_of(t):
    return P if t < NT - 1 else NS


def constants(nc, m):
    with nc.Block() as block:

        @block.gpsimd
        def _(e):
            for t, v in ((m.ident, 0.0), (m.ones, 1.0), (m.headmean, 0.0), (m.chmean, 1.0 / W),
                         (m.causal, 1.0), (m.strict, 1.0), (m.qmask, 0.0), (m.sampmask, 1.0),
                         (m.newmask, 0.0), (m.carry, 1.0), (m.headsel, 0.0), (m.reset, 1.0),
                         (m.poolw, 0.0), (m.eps, EPS)):
                e.memset(t[:], v)
            e.drain()
            for i in range(2):
                e.memset(m.headmean[64 * i:64 * i + 64, 64 * i:64 * i + 64], 1.0 / HD)
                e.drain()
            e.memset(m.reset[:, 0:SEQ].rearrange("p (c t) -> p c t", t=P)[:, :, 0:1], 0.0)
            e.memset(m.reset[:, SEQ:TOK].rearrange("p (c t) -> p c t", t=DEC_L)[:, :, 0:1], 0.0)
            e.drain()
            e.affine_select(out=m.ident[:], in_=m.ident[:], compare_op=ALU.not_equal, fill=1.0, base=0,
                            pattern=[[-1, P]], channel_multiplier=1)
            e.drain()
            e.affine_select(out=m.causal[:], in_=m.causal[:], compare_op=ALU.is_ge, fill=0.0, base=0,
                            pattern=[[1, P]], channel_multiplier=-1)
            e.drain()
            e.affine_select(out=m.strict[:], in_=m.strict[:], compare_op=ALU.is_gt, fill=0.0, base=0,
                            pattern=[[1, P]], channel_multiplier=-1)
            e.drain()
            e.affine_select(out=m.qmask[:], in_=m.qmask[:], compare_op=ALU.is_ge, fill=NEG, base=0,
                            pattern=[[-1, P]], channel_multiplier=1)
            e.drain()
            e.affine_select(out=m.sampmask[:], in_=m.sampmask[:], compare_op=ALU.is_ge, fill=0.0, base=0,
                            pattern=[[1, NS]], channel_multiplier=-1)
            e.drain()
            e.affine_select(out=m.newmask[HD:], in_=m.newmask[HD:], compare_op=ALU.is_equal, fill=NEG, base=0,
                            pattern=[[1, DEC_B], [-1, DEC_B], [0, DEC_L]], channel_multiplier=0)
            e.drain()
            e.affine_select(out=m.carry[:], in_=m.carry[:], compare_op=ALU.is_gt, fill=0.0, base=0,
                            pattern=[[1, P]], channel_multiplier=-1)
            e.drain()
            e.affine_select(out=m.headsel[0:H], in_=m.headsel[0:H], compare_op=ALU.not_equal, fill=-1.0, base=0,
                            pattern=[[0, DEC_L], [-1, H]], channel_multiplier=1)
            e.drain()
            e.affine_select(out=m.headsel[FROW:FROW + H], in_=m.headsel[FROW:FROW + H], compare_op=ALU.not_equal, fill=1.0, base=0,
                            pattern=[[0, DEC_L], [-1, H]], channel_multiplier=1)
            e.drain()
            e.iota(m.tok_id[:], pattern=[[P, NT]], base=0, channel_multiplier=1)
            e.iota(m.exp_id_i[:], pattern=[[0, NT], [1, NE]], base=0, channel_multiplier=0)
            e.iota(m.tile_id_i[:], pattern=[[1, SLOT_TILES]], base=0, channel_multiplier=0)
            e.iota(m.count_i[:], pattern=[[1, PMAX]], base=1, channel_multiplier=0)
            e.drain()
            e.drain()
            e.affine_select(out=m.sampmask[:], in_=m.sampmask[:], compare_op=ALU.is_ge, fill=0.0, base=0,
                            pattern=[[-DEC_L, DEC_B], [0, DEC_L]], channel_multiplier=1)
            e.drain()
            e.affine_select(out=m.newmask[HD:], in_=m.newmask[HD:], compare_op=ALU.is_ge, fill=NEG, base=0,
                            pattern=[[0, DEC_B], [0, DEC_B], [-DEC_L, DEC_L]], channel_multiplier=1)
            e.drain()
            e.affine_select(out=m.carry[:], in_=m.carry[:], compare_op=ALU.is_ge, fill=0.0, base=0,
                            pattern=[[-NPG, DEC_B], [0, NPG]], channel_multiplier=1)
            e.drain()
            e.tensor_copy(m.exp_id[:], m.exp_id_i[:])
            e.tensor_copy(m.tile_id[:], m.tile_id_i[:])
            e.tensor_copy(m.count[:], m.count_i[:])

        @block.sync
        def _(e):
            loads = [
                (m.g1[:], m.norm1_g[0].rearrange("(p k) -> p k", k=KC)),
                (m.g2[:], m.norm2_g[0].rearrange("(p k) -> p k", k=KC)),
                (m.gla_g[:], m.gla_norm_g[0].rearrange("(c p) -> p c", p=P)),
                (m.gla_b[:], m.gla_b_a[0].rearrange("(c p) -> p c", p=P)),
                (m.cb[:], m.conv_b[0].rearrange("(c p) -> p c", p=P)),
                (m.ln_g[:], m.conv_ln_g[0].rearrange("(c p) -> p c", p=P)),
                (m.ln_b[:], m.conv_ln_b[0].rearrange("(c p) -> p c", p=P)),
                (m.pscale[:], m.pool_scale[0].rearrange("(c p) -> p c", p=P)),
                (m.wa2[:], m.gla_w_a2[0]),
                (m.tapw[:], m.conv_w[0]),
                (m.fb[FROW:FROW + H, :], m.fox_b_f[0].rearrange("(h a) -> h a", a=1)),
                (m.wr[:, :, 0:NG], m.router_wg[0].rearrange("(p k) n -> p k n", k=KC)),
                (m.wr[:, :, NG:NG + NE], m.router_we[0].rearrange("(p k) n -> p k n", k=KC)),
                (m.rb[:, 0:NG], m.router_bg[0].partition_broadcast(P)),
                (m.rb[:, NG:NG + NE], m.router_be[0].partition_broadcast(P)),
                (m.pages[:], m.page_table.rearrange("b g -> (b g)").rearrange("(a n) -> a n", a=1)),
                (m.pages_col[:], m.page_table.rearrange("b g -> (b g)").rearrange("(n a) -> n a", a=1)),
            ]
            for i in range(2):
                loads.append((m.fqg[64 * i:64 * i + 64, :], m.fox_q_norm_g[0].rearrange("(p a) -> p a", a=1)))
                loads.append((m.fkg[64 * i:64 * i + 64, :], m.fox_k_norm_g[0].rearrange("(p a) -> p a", a=1)))
            for to, of in loads:
                e.dma_start(to, of, allow_slow_non_contiguous=True).then_inc(m.s_param, 16)
            m.n_params = len(loads)
            e.wait_ge(m.s_param, 16 * m.n_params)

    with nc.Block() as block:

        @block.sync
        def _(e):
            for g in range(4):
                o = HD * (g % 2)
                e.dma_start(m.poolw[o:o + HD, g // 2, o:o + HD], m.pool_w[0, g]).then_inc(m.s_param, 16)
            e.wait_ge(m.s_param, 16 * (m.n_params + 4))

        @block.vector
        def _(e):
            e.tensor_scalar(m.fqg8[:], m.fqg[:], HD ** -0.5, None, ALU.mult)


def projections(nc, m):
    ctx = ExitStack()
    sb = lambda name, shape: ctx.enter_context(nc.sbuf_tensor(name, shape, F32))
    sem = lambda name: ctx.enter_context(nc.semaphore(name))
    with ctx:
        hT = m.mixT
        zrow = sb("zrow", [P, D])
        xt = sb("xt", [P, 2, D])
        hn = sb("hn", [P, 2, D])
        junk = sb("junk", [P, D])
        ssq = sb("ssq", [P, 2])
        std = sb("std", [P, 2])
        rstd = sb("rstd", [P, 2])
        wv = sb("wv", [P, KC, 2 * W])
        wz = sb("wz", [P, 2, KC, W])
        wsm = sb("wsm", [P, KC, FROW + H])
        ps_t, ps_v, ps_z = m.ps[:, 0:2, :], m.ps[:, 2:4, :], m.ps[:, 4:8, :]

        x_in = [sem(f"x_in{i}") for i in range(2)]
        std_ready, normed, turned, ht_ready = sem("std_ready"), sem("normed"), sem("turned"), sem("ht_ready")
        wv_in, wsm_in = sem("wv_in"), sem("wsm_in")
        v_done, v_out, v_stored = sem("v_done"), sem("v_out"), sem("v_stored")
        wz_in = [sem(f"wz_in{i}") for i in range(2)]
        z_done, z_out = sem("z_done"), sem("z_out")

        w_rows = m.w_in[0].rearrange("(p k) n -> p k n", k=KC)
        NZ = len(Z_GROUPS)

        with nc.Block() as block:

            @block.sync
            def _(e):
                for t in range(NT):
                    r = rows_of(t)
                    if t >= 2:
                        e.wait_ge(normed, t - 1)
                    src = m.x_prompt[0, t * P:(t + 1) * P, :] if t < NT - 1 else m.x_sample.rearrange("b l d -> (b l) d")
                    e.dma_start(xt[0:r, t % 2, :], src).then_inc(x_in[t % 2], 16)
                    if t == 1:
                        e.dma_start(wv[:, :, 0:W], w_rows[:, :, GV:GV + W]).then_inc(wv_in, 16)
                        e.dma_start(wv[:, :, W:2 * W], w_rows[:, :, FV:FV + W]).then_inc(wv_in, 16)
                for g, c in enumerate(Z_GROUPS):
                    if g >= 2:
                        e.wait_ge(z_done, 2 * NCH * (g - 1))
                    e.dma_start(wz[:, g % 2, :, :], w_rows[:, :, c:c + W]).then_inc(wz_in[g % 2], 16)
                for t in range(NT):
                    r = rows_of(t)
                    e.wait_ge(v_out, t + 1)
                    to = m.v_prompt[0, 0, t * P:(t + 1) * P] if t < NT - 1 else m.v_sample[0].rearrange("b l h d -> (b l) h d")
                    e.dma_start(to.rearrange("p h d -> p (h d)"), m.V[0:r, t, W:2 * W]).then_inc(v_stored, 16)
                e.wait_ge(v_stored, 16 * NT)

            @block.gpsimd
            def _(e):
                e.memset(wsm[:], 0.0)
                e.memset(zrow[:], 0.0)
                e.drain()
                for t in range(2 * LEAST_PAIRS, SLOT_TILES):
                    e.dma_start(m.yd[t * P:(t + 1) * P, :], zrow[:, 0:D]).then_inc(m.s_zero_rows, 16)
                e.dma_start(wsm[:, :, 0:RANK], w_rows[:, :, GA:GA + RANK]).then_inc(wsm_in, 16)
                e.dma_start(wsm[:, :, FROW:FROW + H], w_rows[:, :, FF:FF + H]).then_inc(wsm_in, 16)

            @block.scalar
            def _(e):
                def square(t):
                    r = rows_of(t)
                    e.wait_ge(x_in[t % 2], 16 * (t // 2 + 1))
                    e.activation(junk[0:r], xt[0:r, t % 2, :], ACT.Square, scale=D ** -0.5,
                                 accum_out=ssq[0:r, t % 2:t % 2 + 1])
                    e.drain()
                    e.activation(std[0:r, t % 2:t % 2 + 1], ssq[0:r, t % 2:t % 2 + 1], ACT.Sqrt,
                                 bias=m.eps[0:r, :]).then_inc(std_ready, 1)

                square(0)
                for t in range(NT):
                    if t + 1 < NT:
                        square(t + 1)
                    r = rows_of(t)
                    e.wait_ge(v_done, t + 1)
                    e.copy(m.V[0:r, t, :], ps_v[0:r, t % 2, :]).then_inc(v_out, 1)
                for n in range(2 * NZ * NCH):
                    e.wait_ge(z_done, n + 1)
                    e.copy(m.Z[:, n // NCH, n % NCH * CH:(n % NCH + 1) * CH], ps_z[:, n % 4, 0:CH]).then_inc(z_out, 1)
                for n in range(NCH):
                    k = 2 * NZ * NCH + n
                    e.wait_ge(z_done, k + 1)
                    e.copy(m.ZS[:, n * CH:(n + 1) * CH], ps_z[0:FROW + H, k % 4, 0:CH]).then_inc(z_out, 1)

            @block.vector
            def _(e):
                def norm(t):
                    r, b = rows_of(t), t % 2
                    e.wait_ge(std_ready, t + 1)
                    e.reciprocal(rstd[0:r, b:b + 1], std[0:r, b:b + 1])
                    e.drain()
                    if t >= 2:
                        e.wait_ge(turned, t - 1)
                    e.tensor_scalar(hn[0:r, b, :], xt[0:r, b, :], rstd[0:r, b:b + 1], None, ALU.mult).then_inc(normed, 1)

                norm(0)
                for t in range(NT):
                    if t + 1 < NT:
                        norm(t + 1)
                    r = rows_of(t)
                    e.wait_ge(turned, t + 1)
                    for c in range(2):
                        g = m.g1[:, 4 * c:4 * c + 4].unsqueeze(2).broadcast_to([P, 4, r])
                        i = e.tensor_tensor(hT[:, 4 * c:4 * c + 4, t * P:t * P + r],
                                            ps_t[:, c, :].rearrange("p (k t) -> p k t", k=4)[:, :, 0:r], g, ALU.mult)
                    i.then_inc(ht_ready, 1)

            @block.tensor
            def _(e):
                def turn(t):
                    r = rows_of(t)
                    e.wait_ge(normed, t + 1)
                    if t >= 1:
                        e.wait_ge(ht_ready, t)
                    for k in range(KC):
                        i = e.transpose(ps_t[:, k // 4, k % 4 * P:k % 4 * P + r], hn[0:r, t % 2, k:D:KC], m.ident[0:r, 0:r])
                    i.then_inc(turned, 1)

                turn(0)
                e.wait_ge(wv_in, 32)
                for t in range(NT):
                    if t + 1 < NT:
                        turn(t + 1)
                    r = rows_of(t)
                    e.wait_ge(ht_ready, t + 1)
                    if t >= 2:
                        e.wait_ge(v_out, t - 1)
                    for k in range(KC):
                        i = e.matmul(ps_v[0:r, t % 2, :], hT[:, k, t * P:t * P + r], wv[:, k, :],
                                     start=(k == 0), stop=(k == KC - 1))
                    i.then_inc(v_done, 1)
                for n in range(2 * NZ * NCH + NCH):
                    f, c, b = n // NCH, n % NCH, n % 4
                    if f < 2 * NZ:
                        if n % (2 * NCH) == 0:
                            e.wait_ge(wz_in[f // 2 % 2], 16 * (f // 4 + 1))
                        lhs, rows = wz[:, f // 2 % 2, :, f % 2 * P:f % 2 * P + P], P
                    else:
                        if c == 0:
                            e.wait_ge(wsm_in, 32)
                        lhs, rows = wsm, FROW + H
                    if n >= 4:
                        e.wait_ge(z_out, n - 3)
                    for k in range(KC):
                        i = e.matmul(ps_z[0:rows, b, 0:CH], lhs[:, k, :], hT[:, k, c * CH:(c + 1) * CH],
                                     start=(k == 0), stop=(k == KC - 1))
                    i.then_inc(z_done, 1)


def log_sigmoid_act(e, x, t):
    e.activation(t, x, ACT.Abs)
    e.drain()
    e.activation(t, t, ACT.Exp, scale=-1.0)
    e.drain()
    return e.activation(t, t, ACT.Ln, bias=1.0)


def gla_pool_norms(nc, m):
    ctx = ExitStack()
    sb = lambda name, shape: ctx.enter_context(nc.sbuf_tensor(name, shape, F32))
    sem = lambda name: ctx.enter_context(nc.semaphore(name))
    NC = NT - 1 + DEC_B
    QE, KE = m.Z[:, ZQ:ZQ + 2, :], m.Z[:, ZK:ZK + 2, :]
    ps = m.ps
    with ctx:
        la, bsum, tmp = sb("la", [P, 2, TOK]), sb("bsum", [P, 2, TOK]), sb("tmp", [P, 2, TOK])
        mid, last, dlm = sb("mid", [P, 2, NC]), sb("last", [P, 2, NC]), sb("dlm", [P, 2, NC])
        e_mid, e_last, e_dlm = sb("e_mid", [P, 2, NC]), sb("e_last", [P, 2, NC]), sb("e_dlm", [P, 2, NC])
        keT = sb("keT", [P, NT, W])
        at = sb("at", [P, 2, 2, 2, P])
        S, Ssc, Stmp = sb("S", [P, 2, P]), sb("Ssc", [P, 2, P]), sb("Stmp", [P, 2, 4, HD])
        SS = sb("SS", [P, 2, DEC_B, P])
        sq, std, rec = sb("head_sq", [P, 2, CH]), sb("head_std", [P, 2, CH]), sb("head_rec", [P, 2, CH])
        tailT = sb("tailT", [2 * NS, W])
        kout = sb("kout", [P, 2, W])
        pxs, pas, pbs = (sb(n, [P, 2, DEC_B, PMAX + DEC_L]) for n in ("pxs", "pas", "pbs"))
        pst = sb("pst", [DEC_B * (PMAX - 1), W])
        rcount = sb("rcount", [P, 2, PMAX])
        fx = m.ZS
        ft = m.CF
        SSsc = bsum[:].rearrange("p c t -> p (c t)")[:, 0:2 * DEC_B * P].rearrange("p (c b e) -> p c b e", c=2, b=DEC_B)
        vmask = tmp[:].rearrange("p c t -> p (c t)")[0:NS, 0:DEC_B * W].rearrange("p (b e) -> p b e", b=DEC_B)
        pa, pb, px = (m.mixT[:, c:c + 2, 0:PMAX + SEQ] for c in (2, 4, 6))

        n_sq, n_ms, n_std, n_norm = sem("n_sq"), sem("n_ms"), sem("n_std"), sem("n_norm")
        la_mm, la_x, la_t, la_d, la_e, la_s, qk_ready = (sem(n) for n in ("la_mm", "la_x", "la_t", "la_d", "la_e", "la_s", "qk_ready"))
        f_x, f_t, f_c = sem("f_x"), sem("f_t"), sem("f_c")
        f_mm, f_out = sem("f_mm"), sem("f_out")
        kt_mm, kt_out, k_sent = sem("kt_mm"), sem("kt_out"), [sem(f"k_sent{i}") for i in range(2)]
        ket_mm, ket_out = sem("ket_mm"), sem("ket_out")
        zeroed, st_in, pst_in = sem("zeroed"), sem("st_in"), sem("pst_in")
        a_mm, a_out, o_mm, o_out, s_mm, s_out, s_sc = (sem(n) for n in ("a_mm", "a_out", "o_mm", "o_out", "s_mm", "s_out", "s_sc"))
        ss_sc, vm_ready = sem("ss_sc"), sem("vm_ready")
        silu, stored = sem("silu"), sem("stored")
        px_ready, pst_mm, pst_out, p_d, p_mm, p_out = (sem(n) for n in ("px_ready", "pst_mm", "pst_out", "p_d", "p_mm", "p_out"))
        pt_mm, pt_out = sem("pt_mm"), sem("pt_out")

        def tiles(x):
            return (x[:, :, 0:SEQ].rearrange("p c (n t) -> p c n t", t=P),
                    x[:, :, SEQ:TOK].rearrange("p c (n t) -> p c n t", t=DEC_L))

        FOX_NORMS = [(ZFQ, m.fqg8[:]), (ZFQ + 1, m.fqg8[:]), (ZFK, m.fkg[:]), (ZFK + 1, m.fkg[:])]
        GLA_NORMS = [(ZQ, m.gla_g[:, 0:1]), (ZQ + 1, m.gla_g[:, 1:2])]
        norm_steps = [(z, g, n) for z, g in FOX_NORMS + GLA_NORMS for n in range(NCH)]
        N_FOX = len(FOX_NORMS) * NCH
        cols = lambda n: slice(n * CH, (n + 1) * CH)

        def norm_square(e, i):
            z, g, n = norm_steps[i]
            if i >= 2:
                e.wait_ge(n_ms, i - 1)
            e.activation(sq[:, i % 2, :], m.Z[:, z, cols(n)], ACT.Square).then_inc(n_sq, 1)

        def norm_root(e, i):
            e.wait_ge(n_ms, i + 1)
            if i >= 2:
                e.wait_ge(n_norm, i - 1)
            e.activation(std[:, i % 2, :], ps[:, i % 2, 0:CH], ACT.Sqrt, bias=m.eps[:, :]).then_inc(n_std, 1)

        def norm_mean(e, i):
            e.wait_ge(n_sq, i + 1)
            if i >= 2:
                e.wait_ge(n_std, i - 1)
            e.matmul(ps[:, i % 2, 0:CH], m.headmean[:], sq[:, i % 2, :], start=True, stop=True).then_inc(n_ms, 1)

        def norm_scale(e, i):
            z, g, n = norm_steps[i]
            e.wait_ge(n_std, i + 1)
            e.reciprocal(rec[:, i % 2, :], std[:, i % 2, :])
            e.drain()
            e.scalar_tensor_tensor(out=m.Z[:, z, cols(n)], in0=m.Z[:, z, cols(n)], scalar=g,
                                   in1=rec[:, i % 2, :], op0=ALU.mult, op1=ALU.mult).then_inc(n_norm, 1)

        with nc.Block() as block:

            @block.sync
            def _(e):
                e.wait_ge(zeroed, 1)
                for h in range(H):
                    o = HD * (h % 2)
                    e.dma_start(SS[o:o + HD, h // 2, :, o:o + HD],
                                m.state_gla[0, :, h].rearrange("b d e -> d b e")).then_inc(st_in, 16)
                e.dma_start(pst[:], m.state_pool[0].rearrange("b t c -> (b t) c")).then_inc(pst_in, 16)
                e.dma_start(m.conv_sample[0, :, 0:TAPS - 1 - DEC_L, :], m.state_conv[0, :, DEC_L:TAPS - 1, :]).then_inc(stored, 16)
                e.dma_start(m.pool_sample[0, :, 0:PMAX - 1 - DEC_L, :], m.state_pool[0, :, DEC_L:PMAX - 1, :]).then_inc(stored, 16)
                n = 2
                e.wait_ge(f_out, 1)
                e.dma_start(m.logf_prompt[0, 0].rearrange("(t p) h -> p t h", p=P), m.lft[:, 0:NT - 1, 0:H]).then_inc(stored, 16)
                e.dma_start(m.logf_sample[0].rearrange("b l h -> (b l) h"), m.lft[0:NS, NT - 1, 0:H]).then_inc(stored, 16)
                n += 2
                for t in range(NT):
                    r = rows_of(t)
                    e.wait_ge(kt_out, t + 1)
                    to = m.k_prompt[0, 0, t * P:(t + 1) * P] if t < NT - 1 else m.k_sample[0].rearrange("b l h d -> (b l) h d")
                    e.dma_start(to.rearrange("p h d -> p (h d)"), kout[0:r, t % 2, :]).then_inc(k_sent[t % 2], 16)
                e.wait_ge(s_out, NT - 1)
                for h in range(H):
                    o = HD * (h % 2)
                    e.dma_start(m.gla_prompt[0, 0, h], S[o:o + HD, h // 2, o:o + HD]).then_inc(stored, 16)
                e.wait_ge(s_out, NT)
                for h in range(H):
                    o = HD * (h % 2)
                    e.dma_start(m.gla_sample[0, :, h].rearrange("b d e -> d b e"), SS[o:o + HD, h // 2, :, o:o + HD]).then_inc(stored, 16)
                e.wait_ge(pt_out, 1)
                e.dma_start(m.pool_prompt[0, 0], tailT[NS - PMAX + 1:NS, :]).then_inc(stored, 16)
                for b in range(DEC_B):
                    e.dma_start(m.pool_sample[0, b, PMAX - 1 - DEC_L:PMAX - 1, :],
                                tailT[NS + DEC_L * b:NS + DEC_L * b + DEC_L, :]).then_inc(stored, 16)
                n += 2 * H + 1 + DEC_B
                e.wait_ge(stored, 16 * n)
                for i in range(2):
                    e.wait_ge(k_sent[i], 16 * ((NT + 1 - i) // 2))

            @block.gpsimd
            def _(e):
                e.memset(SS[:], 0.0)
                e.memset(at[:], 0.0)
                e.memset(S[:], 0.0)
                e.drain().then_inc(zeroed, 1)
                e.memset(px[:, :, 0:PMAX], 0.0)
                e.memset(pxs[:, :, :, 0:1], 0.0)
                e.tensor_copy(px[:, :, PMAX:], m.Z[:, ZPU:ZPU + 2, 0:SEQ])
                e.tensor_copy(pxs[:, :, :, PMAX:], m.Z[:, ZPU:ZPU + 2, SEQ:TOK].rearrange("p c (b l) -> p c b l", l=DEC_L))
                e.wait_ge(pst_out, 1)
                e.drain()
                N, NB = PMAX + SEQ, PMAX + DEC_L
                for lo, c0, w, src, dst, ssrc, sdst in ((0, 0, 1, px, pa, pxs, pas), (64, 0, 2, pa, pb, pas, pbs),
                                                        (0, 1, 2, pa, pb, pas, pbs), (0, 1, 4, pb, pa, pbs, pas),
                                                        (64, 1, 8, pa, pb, pas, pbs)):
                    c1 = 2 if w == 1 else c0 + 1
                    j = 2 * w - 1
                    e.tensor_tensor(dst[lo:P, c0:c1, j:N], src[lo:P, c0:c1, j:N], src[lo:P, c0:c1, j - w:N - w], ALU.add)
                    e.drain()
                    e.tensor_tensor(sdst[lo:P, c0:c1, :, j:NB], ssrc[lo:P, c0:c1, :, j:NB],
                                    ssrc[lo:P, c0:c1, :, j - w:NB - w], ALU.add)
                    e.drain()
                e.drain().then_inc(p_d, 1)

            @block.scalar
            def _(e):
                for i in range(N_FOX + 1):
                    if i < N_FOX:
                        norm_square(e, i)
                    if i:
                        norm_root(e, i - 1)
                e.wait_ge(la_x, 6)
                log_sigmoid_act(e, la[:], tmp[:]).then_inc(la_t, 1)
                e.wait_ge(f_x, 1)
                log_sigmoid_act(e, fx[FROW:FROW + H, :], ft[FROW:FROW + H, :]).then_inc(f_t, 1)
                e.wait_ge(la_s, 1)
                e.activation(e_mid[:], mid[:], ACT.Exp, scale=1.0 / TAU)
                e.activation(e_last[:], last[:], ACT.Exp, scale=1.0 / TAU)
                e.activation(e_dlm[:], dlm[:], ACT.Exp, scale=1.0 / TAU).then_inc(la_e, 1)
                e.wait_ge(la_d, 1)
                e.activation(la[:], tmp[:], ACT.Exp, scale=1.0 / TAU).then_inc(la_e, 1)
                e.drain()
                e.activation(tmp[:], tmp[:], ACT.Exp, scale=-1.0 / TAU).then_inc(la_e, 1)
                for t in range(NT):
                    e.wait_ge(ket_mm, t + 1)
                    e.copy(keT[0:rows_of(t), t, :], ps[0:rows_of(t), 4 + t % 2, 0:W]).then_inc(ket_out, 1)
                for t in range(NT):
                    r = rows_of(t)
                    e.wait_ge(o_mm, t + 1)
                    e.copy(QE[:, :, t * P:t * P + r], ps[:, 4 + t % 2, 0:2 * P].rearrange("p (c t) -> p c t", c=2)[:, :, 0:r]).then_inc(o_out, 1)
                e.drain()
                for i in range(N_FOX, len(norm_steps) + 1):
                    if i < len(norm_steps):
                        norm_square(e, i)
                    if i > N_FOX:
                        norm_root(e, i - 1)
                e.activation(m.Z[:, ZG:ZG + 2, :], m.Z[:, ZG:ZG + 2, :], ACT.Silu).then_inc(silu, 1)
                for t in range(NT):
                    e.wait_ge(kt_mm, t + 1)
                    if t >= 2:
                        e.wait_ge(k_sent[t % 2], 16 * (t // 2))
                    e.copy(kout[0:rows_of(t), t % 2, :], ps[0:rows_of(t), t % 2, 0:W]).then_inc(kt_out, 1)

            @block.vector
            def _(e):
                for n in range(2 * NCH):
                    c = n // NCH
                    e.wait_ge(la_mm, n + 1)
                    e.tensor_scalar(la[:, c, cols(n % NCH)], ps[:, 2 + n % 2, 0:CH], m.gla_b[:, c:c + 1], None, ALU.add).then_inc(la_x, 1)
                e.tensor_scalar(fx[FROW:FROW + H, :], m.ZS[FROW:FROW + H, :], m.fb[FROW:FROW + H, :], None, ALU.add).then_inc(f_x, 1)
                for i in range(N_FOX):
                    norm_scale(e, i)
                e.wait_ge(pst_mm, 1)
                for c in range(2):
                    i = e.tensor_copy(pxs[:, c, :, 1:PMAX], ps[:, 7, c * P:c * P + DEC_B * (PMAX - 1)].rearrange("p (b t) -> p b t", b=DEC_B))
                i.then_inc(pst_out, 1)
                e.wait_ge(la_t, 1)
                e.scalar_tensor_tensor(out=la[:], in0=la[:], scalar=0.0, in1=tmp[:], op0=ALU.min, op1=ALU.subtract)
                e.drain()
                for c in range(2):
                    e.tensor_tensor_scan(bsum[:, c, :], m.reset[:], la[:, c, :], 0.0, ALU.mult, ALU.add)
                e.drain()
                bp, bs = tiles(bsum)
                tp, ts_ = tiles(tmp)
                for src, n0, n1, im, il in ((bp, 0, NT - 1, P // 2 - 1, P - 1), (bs, NT - 1, NC, 1, DEC_L - 1)):
                    e.tensor_copy(mid[:, :, n0:n1], src[:, :, :, im])
                    e.tensor_copy(last[:, :, n0:n1], src[:, :, :, il])
                e.drain()
                e.tensor_tensor(dlm[:], last[:], mid[:], ALU.subtract).then_inc(la_s, 1)
                for c in range(2):
                    e.tensor_tensor(tp[:, c], bp[:, c], mid[:, c, 0:NT - 1].unsqueeze(2).broadcast_to([P, NT - 1, P]), ALU.subtract)
                    i = e.tensor_tensor(ts_[:, c], bs[:, c], mid[:, c, NT - 1:NC].unsqueeze(2).broadcast_to([P, DEC_B, DEC_L]), ALU.subtract)
                i.then_inc(la_d, 1)
                F4 = slice(FROW, FROW + H)
                e.wait_ge(f_t, 1)
                e.scalar_tensor_tensor(out=fx[F4, :], in0=fx[F4, :], scalar=0.0, in1=ft[F4, :], op0=ALU.min, op1=ALU.subtract)
                e.drain()
                e.tensor_tensor_scan(m.CF[F4, 0:SEQ], m.ones[F4, 0:1].broadcast_to([H, SEQ]), fx[F4, 0:SEQ], 0.0, ALU.mult, ALU.add).then_inc(f_c, 1)
                e.wait_ge(la_e, 3)
                e.scalar_tensor_tensor(out=QE, in0=QE, scalar=HD ** -0.5, in1=la[:], op0=ALU.mult, op1=ALU.mult)
                e.tensor_tensor(KE, KE, tmp[:], ALU.mult).then_inc(qk_ready, 1)
                e.wait_ge(zeroed, 1)
                e.wait_ge(f_mm, 1)
                e.tensor_copy(m.lft[:, 0:NT - 1, :], ps[:, 6, 0:8 * NT].rearrange("p (t c) -> p t c", c=8)[:, 0:NT - 1, :])
                e.tensor_copy(m.lft[0:NS, NT - 1, 0:H], ps[0:NS, 6, 8 * (NT - 1):8 * (NT - 1) + H]).then_inc(f_out, 1)

                def mask_scores(t):
                    r, b = rows_of(t), t % 2
                    mask = (m.causal if t < NT - 1 else m.sampmask)[0:r, 0:r].bitcast(I32)
                    e.wait_ge(a_mm, t + 1)
                    if t >= 2:
                        e.wait_ge(o_mm, t - 1)
                    if t == NT - 1:
                        e.memset(at[0:r, b], 0.0)
                        e.drain()
                    for hb in range(2):
                        i = e.copy_predicated(at[0:r, b, hb, :, 0:r], mask.unsqueeze(1).broadcast_to([r, 2, r]),
                                              ps[0:r, 2 * b + hb, 0:2 * P].rearrange("p (h t) -> p h t", h=2)[:, :, 0:r])
                    i.then_inc(a_out, 1)

                mask_scores(0)
                for t in range(NT - 1):
                    if t >= 1:
                        e.wait_ge(o_mm, t)
                    for c in range(2):
                        i = e.tensor_scalar(Ssc[:, c, :], S[:, c, :], e_mid[:, c, t:t + 1], None, ALU.mult)
                    i.then_inc(s_sc, 1)
                    mask_scores(t + 1)
                    e.wait_ge(s_mm, t + 1)
                    for c in range(2):
                        for o in (0, HD):
                            e.tensor_scalar(Stmp[o:o + HD, c, 0, :], ps[o:o + HD, 6, c * P + o:c * P + o + HD],
                                            e_dlm[o:o + HD, c, t:t + 1], None, ALU.mult)
                    e.drain()
                    for c in range(2):
                        for o in (0, HD):
                            i = e.scalar_tensor_tensor(out=S[o:o + HD, c, o:o + HD], in0=S[o:o + HD, c, o:o + HD],
                                                       scalar=e_last[o:o + HD, c, t:t + 1], in1=Stmp[o:o + HD, c, 0, :],
                                                       op0=ALU.mult, op1=ALU.add)
                    i.then_inc(s_out, 1)
                    e.drain()
                e.wait_ge(st_in, 16 * H)
                for c in range(2):
                    i = e.tensor_tensor(SSsc[:, c], SS[:, c], e_mid[:, c, NT - 1:NC].unsqueeze(2).broadcast_to([P, DEC_B, P]), ALU.mult)
                i.then_inc(ss_sc, 1)
                for b in range(DEC_B):
                    i = e.tensor_scalar(vmask[:, b, :], m.V[0:NS, NT - 1, 0:W], m.sampmask[:, DEC_L * b + DEC_L - 1:DEC_L * b + DEC_L], None, ALU.mult)
                i.then_inc(vm_ready, 1)
                for g in range(4):
                    c, b0 = g // 2, g % 2 * 4
                    e.wait_ge(s_mm, NT - 1 + g + 1)
                    for o in (0, HD):
                        view = SS[o:o + HD, c, b0:b0 + 4, o:o + HD]
                        pv = ps[o:o + HD, 6 + g % 2, :].rearrange("p (b e) -> p b e", b=4)[:, :, o:o + HD]
                        bc = lambda x: x[o:o + HD, c, NT - 1 + b0:NT - 1 + b0 + 4].unsqueeze(2).broadcast_to([HD, 4, HD])
                        e.tensor_tensor(Stmp[o:o + HD, 0], pv, bc(e_dlm), ALU.mult)
                        e.tensor_tensor(view, view, bc(e_last), ALU.mult)
                        e.drain()
                        i = e.tensor_tensor(view, view, Stmp[o:o + HD, 0], ALU.add)
                        e.drain()
                    e.engine_nop().then_inc(s_out if g == 3 else vm_ready, 1)
                for i in range(N_FOX, len(norm_steps)):
                    norm_scale(e, i)
                e.wait_ge(silu, 1)
                e.drain()
                e.tensor_tensor(m.mixT[:, 0:2, :], QE, m.Z[:, ZG:ZG + 2, :], ALU.mult)
                for g, w in enumerate(WINDOWS):
                    o, c = HD * (g % 2), g // 2
                    e.tensor_scalar(rcount[o:o + HD, c, :], m.count[o:o + HD, :], float(w), None, ALU.min)
                e.drain()
                e.reciprocal(rcount[:], rcount[:])
                e.drain()
                e.wait_ge(p_d, 1)
                for g, w in enumerate(WINDOWS):
                    o, c = HD * (g % 2), g // 2
                    R = slice(o, o + HD)
                    src, ssrc = ((pa, pas), (pb, pbs))[g % 2]
                    e.scalar_tensor_tensor(out=pa[R, c, 2 * PMAX:], in0=src[R, c, 2 * PMAX:], scalar=1.0 / w,
                                           in1=px[R, c, 2 * PMAX:], op0=ALU.mult, op1=ALU.subtract)
                    e.tensor_tensor(src[R, c, PMAX:2 * PMAX], src[R, c, PMAX:2 * PMAX], rcount[R, c, :], ALU.mult)
                    e.scalar_tensor_tensor(out=pxs[R, c, :, PMAX:], in0=ssrc[R, c, :, PMAX:], scalar=1.0 / w,
                                           in1=pxs[R, c, :, PMAX:], op0=ALU.mult, op1=ALU.subtract)
                    e.drain()
                    i = e.tensor_tensor(pa[R, c, PMAX:2 * PMAX], src[R, c, PMAX:2 * PMAX], px[R, c, PMAX:2 * PMAX], ALU.subtract)
                i.then_inc(p_out, 1)
                for n in range(6):
                    c, k = n // 3, n % 3
                    w0, w1 = ((0, 512), (512, SEQ), (SEQ, TOK))[k]
                    e.wait_ge(p_mm, n + 1)
                    e.tensor_scalar(m.mixT[:, 6 + c, w0:w1], ps[:, n % 4, 0:w1 - w0], m.pscale[:, c:c + 1], None, ALU.mult).then_inc(p_out, 1)
                e.wait_ge(pt_mm, 1)
                e.tensor_copy(tailT[:], ps[0:2 * NS, 4, 0:W]).then_inc(pt_out, 1)

            @block.tensor
            def _(e):
                for n in range(2 * NCH):
                    if n >= 2:
                        e.wait_ge(la_x, n - 1)
                    e.matmul(ps[:, 2 + n % 2, 0:CH], m.wa2[:, n // NCH * P:n // NCH * P + P], m.ZS[0:RANK, cols(n % NCH)],
                             start=True, stop=True).then_inc(la_mm, 1)
                for i in range(N_FOX):
                    norm_mean(e, i)
                e.wait_ge(pst_in, 16)
                for c in range(2):
                    i = e.transpose(ps[:, 7, c * P:c * P + DEC_B * (PMAX - 1)], pst[:, c * P:c * P + P],
                                    m.ident[0:DEC_B * (PMAX - 1), 0:DEC_B * (PMAX - 1)])
                i.then_inc(pst_mm, 1)
                e.wait_ge(f_c, 1)
                F4 = slice(FROW, FROW + H)
                for t in range(NT):
                    r = rows_of(t)
                    i = e.transpose(ps[0:r, 6, 8 * t:8 * t + H], fx[F4, t * P:t * P + r], m.ident[F4, F4])
                    if t < NT - 1:
                        i = e.transpose(ps[0:r, 6, 8 * t + H:8 * t + 2 * H], m.CF[F4, t * P:t * P + r], m.ident[F4, F4])
                i.then_inc(f_mm, 1)
                e.wait_ge(qk_ready, 1)
                for t in range(NT):
                    r = rows_of(t)
                    if t >= 2:
                        e.wait_ge(ket_out, t - 1)
                    for c in range(2):
                        i = e.transpose(ps[0:r, 4 + t % 2, c * P:c * P + P], KE[:, c, t * P:t * P + r], m.ident[:])
                    i.then_inc(ket_mm, 1)
                e.wait_ge(ket_out, NT)
                e.wait_ge(la_x, 6)
                e.wait_ge(n_std, N_FOX)
                e.wait_ge(f_out, 1)

                def scores(t):
                    r = rows_of(t)
                    if t >= 2:
                        e.wait_ge(a_out, t - 1)
                    for h in range(H):
                        o, c = HD * (h % 2), h // 2
                        i = e.matmul(ps[0:r, 2 * (t % 2) + h % 2, c * P:c * P + r], KE[o:o + HD, c, t * P:t * P + r],
                                     QE[o:o + HD, c, t * P:t * P + r], start=True, stop=True)
                    i.then_inc(a_mm, 1)

                scores(0)
                for t in range(NT):
                    r, b, last_t = rows_of(t), t % 2, t == NT - 1
                    if not last_t:
                        scores(t + 1)
                        if t >= 1:
                            e.wait_ge(s_out, t)
                        for c in range(2):
                            i = e.matmul(ps[:, 6, c * P:c * P + P], keT[:, t, c * P:c * P + P], m.V[:, t, c * P:c * P + P],
                                         start=(c == 0), stop=(c == 1), skip_group_check=True)
                        i.then_inc(s_mm, 1)
                        e.wait_ge(s_sc, t + 1)
                    else:
                        e.wait_ge(ss_sc, 1)
                    if t >= 2:
                        e.wait_ge(o_out, t - 1)
                    for c in range(2):
                        if not last_t:
                            e.matmul(ps[:, 4 + b, c * P:c * P + P], Ssc[:, c, :], QE[:, c, t * P:t * P + P],
                                     start=(c == 0), stop=False, skip_group_check=True)
                        else:
                            for s in range(DEC_B):
                                o = c * P + DEC_L * s
                                e.matmul(ps[:, 4 + b, o:o + DEC_L], SSsc[:, c, s, :],
                                         QE[:, c, SEQ + DEC_L * s:SEQ + DEC_L * s + DEC_L],
                                         start=(c == 0 and s == 0), stop=False, skip_group_check=True)
                    e.wait_ge(a_out, t + 1)
                    for h in range(H):
                        o, c = HD * (h % 2), h // 2
                        i = e.matmul(ps[o:o + HD, 4 + b, c * P:c * P + r], m.V[0:r, t, h * HD:h * HD + HD],
                                     at[0:r, b, h % 2, c, 0:r], start=False, stop=True, skip_group_check=True)
                    i.then_inc(o_mm, 1)
                e.wait_ge(vm_ready, 1)
                e.wait_ge(pst_out, 1)
                e.wait_ge(s_out, NT - 1)
                for g in range(4):
                    c, b0 = g // 2, g % 2 * 4
                    if g >= 2:
                        e.wait_ge(vm_ready, g)
                    e.matmul(ps[:, 6 + g % 2, :].rearrange("p (b e) -> p b e", b=4), keT[0:NS, NT - 1, c * P:c * P + P],
                             vmask[:, b0:b0 + 4, c * P:c * P + P], start=True, stop=True).then_inc(s_mm, 1)
                e.wait_ge(a_out, NT)
                for i in range(N_FOX, len(norm_steps)):
                    norm_mean(e, i)
                e.wait_ge(n_std, len(norm_steps))
                for t in range(NT):
                    r = rows_of(t)
                    if t >= 2:
                        e.wait_ge(kt_out, t - 1)
                    for c in range(2):
                        i = e.transpose(ps[0:r, t % 2, c * P:c * P + P], m.Z[:, ZFK + c, t * P:t * P + r], m.ident[:])
                    i.then_inc(kt_mm, 1)
                e.wait_ge(o_out, NT)
                for c in range(2):
                    i = e.transpose(ps[0:2 * NS, 4, c * P:c * P + P], m.Z[:, ZPU + c, SEQ - NS:TOK], m.ident[:])
                i.then_inc(pt_mm, 1)
                e.wait_ge(kt_out, NT)
                e.wait_ge(p_out, 1)
                for n in range(6):
                    c, k = n // 3, n % 3
                    src, w = ((pa[:, c, PMAX:PMAX + 512], 512), (pa[:, c, PMAX + 512:], 512), (pxs[:, c, :, PMAX:], NS))[k]
                    to = ps[:, n % 4, 0:w]
                    if k == 2:
                        to = to.rearrange("p (b l) -> p b l", l=DEC_L)
                    if n >= 4:
                        e.wait_ge(p_out, 1 + n - 3)
                    e.matmul(to, m.poolw[:, c, :], src, start=True, stop=True).then_inc(p_mm, 1)


def fox_conv(nc, m):
    ctx = ExitStack()
    sb = lambda name, shape: ctx.enter_context(nc.sbuf_tensor(name, shape, F32))
    sem = lambda name: ctx.enter_context(nc.semaphore(name))
    ps = m.ps
    R = DEC_L * H
    QG = 4
    NQ = NPG // QG
    NKEY = PAST + NS
    SP0 = HD
    NB1 = TAPS - 1
    F4 = slice(FROW, FROW + H)
    with ctx:
        ck = m.Z[:, ZQ:ZQ + 4, 0:SEQ]
        sc = m.Z[:, ZG:ZG + 2, 0:SEQ]
        pT = m.Z[:, ZPU:ZPU + 2, 0:SEQ].rearrange("p b (k q) -> p b k q", q=P)
        kpg = sb("kpg", [P, 2, QG, W])
        vpg = sb("vpg", [P, NPG, W])
        kT = sb("kT", [P, 2, 2, QG * PAGE])
        low = sb("low", [P, 2, NKEY])
        cb = low[0:FROW + H]
        ss = low[SP0:SP0 + R]
        sT = sb("sT", [P, NPG + 1, R])
        u = sb("u", [P, 2, NB1 + SEQ])
        us, unew = sb("us", [P, 2, DEC_B, NB1 + DEC_L]), sb("unew", [P, 2, NS])
        cst = sb("cst", [DEC_B // 2 * NB1, 2, W])
        ctail = cst[0:NS]
        lfp, cpg = kT[:, 0, 0, :], kT[:, 1, 0, :].rearrange("p (h t) -> p h t", h=H)
        tapT = sb("tapT", [P, 2, TAPS])
        carry = sb("page_carry", [P, H])
        cnew = sb("cnew", [FROW + H, DEC_B, DEC_L])
        clast = sb("clast", [FROW + H, DEC_B])
        csel = sb("csel", [FROW + H, DEC_B, DEC_L, H])
        qbd = sb("qbd", [P, 2, DEC_B, DEC_L, H])
        nmax, rsum, rinv = sb("nmax", [P, 4]), sb("rsum", [P, 4]), sb("rinv", [P, 4])
        pad = sb("fmax", [P, 4])
        wtmp = m.Z[:, ZCA:ZCA + 2, 0:DEC_L * DEC_B * TAPS].rearrange("p c (l b k) -> p c l b k", l=DEC_L, b=DEC_B)
        y = m.mixT[:, 4:6, :]
        ysq = m.Z[:, ZCA:ZCA + 2, :]
        lstd, lrec = m.Z[:, ZCB, :], m.Z[:, ZCB + 1, :]

        lf_in, cst_in, page_mm, page_c, c_sent, cl_in = (sem(n) for n in ("lf_in", "cst_in", "page_mm", "page_c", "c_sent", "cl_in"))
        sc_tot = sem("sc_tot")
        ck_mm, ck_out, set_mm, set_out = (sem(n) for n in ("ck_mm", "ck_out", "set_mm", "set_out"))
        zeros, csel_ready, qbd_ready, sig, u_ready = (sem(n) for n in ("zeros", "csel_ready", "qbd_ready", "sig", "u_ready"))
        ct_mm, ct_out, stored2 = sem("ct_mm"), sem("ct_out"), sem("stored2")
        p_sc, p_so, p_exp, p_inv, p_scaled, p_tr, p_to, p_pv, p_oo = (sem("fox_" + n) for n in ("sc", "so", "exp", "inv", "scaled", "tr", "to", "pv", "oo"))
        k_in, v_in, cb_in = [sem(f"k_in{i}") for i in range(2)], sem("v_in"), [sem(f"cb_in{i}") for i in range(2)]
        k_tr, k_o0, k_o1, one_mm, one_out = (sem(n) for n in ("k_tr", "k_o0", "k_o1", "one_mm", "one_out"))
        cb_used = sem("cb_used")
        s_max, s_exp, s_p, s_pv = (sem("samp_" + n) for n in ("max", "exp", "p", "pv"))
        y_done, l_mean, l_sub, l_sq, l_var, l_std, l_scaled, l_out = (sem("ln_" + n) for n in ("y", "mean", "sub", "sq", "var", "std", "scaled", "out"))

        steps = [(i, h) for i in range(NT - 1) for h in range(H)]
        N = len(steps)
        assert N == DEC_B * NQ
        cd = m.cd

        order7 = []
        for n in range(N + 5):
            if 1 <= n <= N:
                order7.append(("q", n - 1))
                if (n - 1) % NQ == NQ - 1:
                    order7.append(("new", (n - 1) // NQ))
            if n % NQ == 2 and 1 <= n // NQ <= DEC_B:
                order7.append(("tr", n // NQ - 1))
            if n % NQ == 3 and 1 <= n // NQ <= DEC_B:
                order7.append(("pv", n // NQ - 1))
        turn7 = {k: i + 1 for i, k in enumerate(order7)}
        LAST = N + 5

        with nc.Block() as block:

            @block.sync
            def _(e):
                e.wait_ge(zeros, 1)
                for g in range(2):
                    e.dma_start(cst[:, g, :], m.state_conv[0, g * (DEC_B // 2):(g + 1) * (DEC_B // 2)].rearrange("b t c -> (b t) c")).then_inc(cst_in, 16)

                def load_k(b, j, par, first):
                    for g in range(QG):
                        page = e.value_load(m.pages[0:1, ds(b * NPG + (QG * j + g), 1)], min_val=0, max_val=POOLPG - 1)
                        if g == 0 and not first:
                            e.wait_ge(k_tr, NQ * b + (j - 1))
                        e.dma_start(kpg[:, par, g, :].unsqueeze(1),
                                    m.cache_k[0, ds(page, 1)].rearrange("a t h d -> t a (h d)")).then_inc(k_in[par], 16)

                def load_v(b, first):
                    for g in range(NPG):
                        page = e.value_load(m.pages[0:1, ds(b * NPG + g, 1)], min_val=0, max_val=POOLPG - 1)
                        if g == 0 and not first:
                            e.wait_ge(s_pv, b)
                        e.dma_start(vpg[:, g, :].unsqueeze(1),
                                    m.cache_v[0, ds(page, 1)].rearrange("a t h d -> t a (h d)")).then_inc(v_in, 16)

                for j in range(NQ):
                    load_k(0, j, j % 2, j < 2)
                load_v(0, True)
                e.wait_ge(ct_out, 1)
                e.dma_start(m.conv_prompt[0, 0], ctail[NS - NB1:NS, 0, :]).then_inc(stored2, 16)
                for b in range(DEC_B):
                    e.dma_start(m.conv_sample[0, b, NB1 - DEC_L:NB1, :], ctail[DEC_L * b:DEC_L * b + DEC_L, 1, :]).then_inc(stored2, 16)
                with e.Fori(1, DEC_B) as b:
                    for j in range(NQ):
                        load_k(b, j, j % 2, False)
                    load_v(b, False)
                e.wait_ge(stored2, 16 * (1 + DEC_B))

            @block.gpsimd
            def _(e):
                e.memset(cb[:], 1.0)
                e.memset(csel[:], 0.0)
                e.memset(u[:, :, 0:NB1], 0.0)
                e.memset(qbd[:], 0.0)
                e.drain().then_inc(zeros, 1)
                e.indirect_dma_start(out=lfp, out_offset=None,
                                     in_=m.cache_logf[0].rearrange("n t h -> n (t h)"),
                                     in_offset=bass.IndirectOffsetOnAxis(ap=m.pages_col[:, 0:1], axis=0)).then_inc(lf_in, 16)
                for h in range(H):
                    o, c = HD * (h % 2), h // 2
                    e.tensor_copy(qbd[o:o + HD, c, :, :, h], m.Z[o:o + HD, ZFQ + c, SEQ:TOK].rearrange("p (b l) -> p b l", l=DEC_L))
                    e.drain()
                e.drain().then_inc(qbd_ready, 1)
                for n, (i, h) in enumerate(steps):
                    e.wait_ge(p_inv, n + 1)
                    nk = (i + 1) * P
                    e.tensor_scalar(sc[:, n % 2, 0:nk], sc[:, n % 2, 0:nk], rinv[:, n % 2:n % 2 + 1], None, ALU.mult).then_inc(p_scaled, 1)

            @block.scalar
            def _(e):
                e.activation(m.Z[:, ZCB:ZCB + 2, :], m.Z[:, ZCB:ZCB + 2, :], ACT.Sigmoid).then_inc(sig, 1)
                e.wait_ge(page_c, 1)
                for b in range(DEC_B):
                    e.dma_start(cd[b].rearrange("h (g t) -> g h t", t=PAGE), cpg[NPG * b:NPG * b + NPG, :, :]).then_inc(c_sent, 16)
                e.wait_ge(c_sent, 16 * DEC_B)
                e.dma_start(clast[F4, :].unsqueeze(2), cd[:, :, PAST - 1:PAST].rearrange("b h t -> h b t"),
                            allow_slow_non_contiguous=True).then_inc(cl_in, 16)

                def load_cb(b):
                    if b >= 2:
                        e.wait_ge(cb_used, b - 1)
                    e.dma_start(cb[0:H, b % 2, 0:PAST], cd[b]).then_inc(cb_in[b % 2], 16)

                load_cb(0)
                load_cb(1)
                for n in range(2 * H):
                    e.wait_ge(ck_mm, n + 1)
                    e.copy(ck[:, n // 2, n % 2 * 512:n % 2 * 512 + 512], ps[:, n % 4, :]).then_inc(ck_out, 1)
                for n in range(LAST):
                    if n < N:
                        i, h = steps[n]
                        nk = (i + 1) * P
                        e.wait_ge(k_tr, n + 1)
                        if n == 0:
                            e.wait_ge(c_sent, 16 * DEC_B)
                        if n >= 2:
                            e.wait_ge(one_mm, turn7[("q", n - 2)])
                        e.copy(kT[:, n % 2, 0, :], ps[:, 5, :]).then_inc(k_o0, 1)
                    if 1 <= n <= N:
                        b, j = (n - 1) // NQ, (n - 1) % NQ
                        e.wait_ge(one_mm, turn7[("q", n - 1)])
                        if j == 0 and b >= 2:
                            e.wait_ge(one_mm, turn7[("tr", b - 2)])
                        e.copy(ss[:, b % 2, 512 * j:512 * j + 512], ps[SP0:SP0 + R, 7, :]).then_inc(one_out, 1)
                    if n < N:
                        e.wait_ge(p_so, n + 1)
                        e.activation(sc[:, n % 2, 0:nk], sc[:, n % 2, 0:nk], ACT.Exp, bias=nmax[:, n % 2:n % 2 + 1],
                                     accum_out=rsum[:, n % 2:n % 2 + 1]).then_inc(p_exp, 1)
                    if 1 <= n <= N:
                        i, h = steps[n - 1]
                        for g in range(i // 4 + 1):
                            k = sum(a // 4 + 1 for a, _ in steps[:n - 1]) + g
                            w = min(4, i + 1 - 4 * g)
                            e.wait_ge(p_tr, k + 1)
                            if g == 0 and n >= 3:
                                e.wait_ge(p_pv, n - 2)
                            e.copy(pT[:, (n - 1) % 2, 4 * g:4 * g + w, :], ps[:, 2 + k % 2, 0:w * P].rearrange("p (k q) -> p k q", q=P)).then_inc(p_to, 1)
                    if n % NQ == 1 and 1 <= n // NQ <= DEC_B:
                        b = n // NQ - 1
                        e.wait_ge(s_max, b + 1)
                        e.activation(ss[:, b % 2, :], ss[:, b % 2, :], ACT.Exp, bias=nmax[SP0:SP0 + R, 2:3],
                                     accum_out=rsum[SP0:SP0 + R, 2:3]).then_inc(s_exp, 1)
                        if b + 2 < DEC_B:
                            load_cb(b + 2)
                    if n % NQ == 2 and 1 <= n // NQ <= DEC_B:
                        b = n // NQ - 1
                        e.wait_ge(one_mm, turn7[("tr", b)])
                        if b >= 1:
                            e.wait_ge(s_pv, b)
                        e.copy(sT[:, 0:NPG, :], ps[:, 7, 0:NPG * R].rearrange("p (g r) -> p g r", r=R))
                        e.copy(sT[0:NS, NPG, :], ps[0:NS, 7, NPG * R:(NPG + 1) * R]).then_inc(one_out, 1)
                for n in range(NCH):
                    cc = slice(n * CH, (n + 1) * CH)
                    e.wait_ge(l_sub, n + 1)
                    e.activation(ysq[:, :, cc], y[:, :, cc], ACT.Square).then_inc(l_sq, 1)
                    e.wait_ge(l_var, n + 1)
                    e.activation(lstd[:, cc], ps[:, 4 + n, 0:CH], ACT.Sqrt, bias=m.eps[:, :]).then_inc(l_std, 1)
                for n in range(2):
                    e.wait_ge(l_scaled, NCH)
                    i = e.activation(y[:, n, :], y[:, n, :], ACT.Silu, bias=m.ln_b[:, n:n + 1])

            @block.vector
            def _(e):
                e.wait_ge(lf_in, 16)
                for h in range(H):
                    i = e.tensor_tensor_scan(cpg[:, h, :], m.ones[:, 0:1].broadcast_to([P, PAGE]),
                                             lfp.rearrange("p (t h) -> p h t", h=H)[:, h, :], 0.0, ALU.mult, ALU.add)
                e.drain()
                e.tensor_copy(carry[:], cpg[:, :, PAGE - 1]).then_inc(sc_tot, 1)
                e.wait_ge(page_mm, 1)
                e.tensor_copy(carry[:], ps[:, 5, 0:H])
                e.drain()
                for h in range(H):
                    i = e.tensor_scalar(cpg[:, h, :], cpg[:, h, :], carry[:, h:h + 1], None, ALU.add)
                i.then_inc(page_c, 1)
                e.wait_ge(set_mm, 1)
                e.tensor_copy(tapT[:], ps[:, 6, 0:2 * TAPS].rearrange("p (c k) -> p c k", c=2))
                for g in range(2):
                    for c in range(2):
                        e.tensor_copy(us[:, c, g * 4:g * 4 + 4, 0:NB1],
                                      ps[:, 7, (2 * g + c) * 4 * NB1:(2 * g + c + 1) * 4 * NB1].rearrange("p (b t) -> p b t", t=NB1))
                e.wait_ge(sig, 1)
                e.wait_ge(zeros, 1)
                e.tensor_tensor(u[:, :, NB1:], m.Z[:, ZCA:ZCA + 2, 0:SEQ], m.Z[:, ZCB:ZCB + 2, 0:SEQ], ALU.mult)
                for c in range(2):
                    e.tensor_tensor(unew[:, c, :], m.Z[:, ZCA + c, SEQ:TOK], m.Z[:, ZCB + c, SEQ:TOK], ALU.mult)
                e.drain()
                for c in range(2):
                    i = e.tensor_copy(us[:, c, :, NB1:], unew[:, c, :].rearrange("p (b l) -> p b l", l=DEC_L))
                i.then_inc(u_ready, 1)
                e.wait_ge(cl_in, 16)
                e.tensor_tensor_scan(cnew[F4].rearrange("p b l -> p (b l)"), m.reset[F4, SEQ:TOK], m.ZS[F4, SEQ:TOK], 0.0, ALU.mult, ALU.add)
                e.drain()
                e.tensor_tensor(cnew[F4], cnew[F4], clast[F4, :].unsqueeze(2).broadcast_to([H, DEC_B, DEC_L]), ALU.add)
                e.drain()
                sel = m.headsel[:].rearrange("p (l h) -> p l h", h=H)
                e.tensor_copy(cb[0:H, 0, PAST:], cnew[F4].rearrange("p b l -> p (b l)"))
                e.tensor_copy(cb[0:H, 1, PAST:], cnew[F4].rearrange("p b l -> p (b l)"))
                for b in range(DEC_B):
                    e.tensor_copy(csel[0:H, b], sel[0:H])
                    i = e.tensor_tensor(csel[F4, b], cnew[F4, b, :].unsqueeze(2).broadcast_to([H, DEC_L, H]), sel[F4], ALU.mult)
                e.drain().then_inc(csel_ready, 1)
                e.wait_ge(ct_mm, 1)
                e.tensor_copy(ctail[:, 0, :], ps[0:NS, 6, 0:W])
                e.tensor_copy(ctail[:, 1, :], ps[0:NS, 6, W:2 * W]).then_inc(ct_out, 1)

                def tap(k):
                    for c in range(2):
                        if k == 0:
                            e.tensor_scalar(y[:, c, 0:SEQ], u[:, c, 0:SEQ], tapT[:, c, 0:1], m.cb[:, c:c + 1], ALU.mult, ALU.add)
                        else:
                            e.scalar_tensor_tensor(out=y[:, c, 0:SEQ], in0=u[:, c, k:k + SEQ], scalar=tapT[:, c, k:k + 1],
                                                   in1=y[:, c, 0:SEQ], op0=ALU.mult, op1=ALU.add)
                    e.drain()

                e.wait_ge(ck_out, 2 * H)
                for n in range(LAST):
                    if n < N:
                        i, h = steps[n]
                        nk = (i + 1) * P
                        e.wait_ge(p_sc, n + 1)
                        if n >= 2:
                            e.wait_ge(p_tr, sum(a // 4 + 1 for a, _ in steps[:n - 1]))
                        for g in range(i // 4 + 1):
                            w = min(512, nk - 512 * g)
                            e.scalar_tensor_tensor(out=sc[:, n % 2, 512 * g:512 * g + w], in0=ps[:, g, 0:w], scalar=m.lft[:, i, H + h:H + h + 1],
                                                   in1=ck[:, h, 512 * g:512 * g + w], op0=ALU.add, op1=ALU.subtract)
                        e.drain()
                        e.tensor_tensor(sc[:, n % 2, nk - P:nk], sc[:, n % 2, nk - P:nk], m.qmask[:], ALU.add)
                        e.drain()
                        e.tensor_reduce(pad[:, n % 2:n % 2 + 1], sc[:, n % 2, 0:nk], AX.X, ALU.max)
                        e.drain()
                        e.tensor_scalar(nmax[:, n % 2:n % 2 + 1], pad[:, n % 2:n % 2 + 1], -1.0, None, ALU.mult).then_inc(p_so, 1)
                        e.wait_ge(k_tr, n + 1)
                        if n >= 2:
                            e.wait_ge(one_mm, turn7[("q", n - 2)])
                        if n == 0:
                            e.wait_ge(c_sent, 16 * DEC_B)
                        e.tensor_copy(kT[:, n % 2, 1, :], ps[:, 6, :]).then_inc(k_o1, 1)
                    if n < TAPS:
                        tap(n)
                    if n < N:
                        e.wait_ge(p_exp, n + 1)
                        e.reciprocal(rinv[:, n % 2:n % 2 + 1], rsum[:, n % 2:n % 2 + 1]).then_inc(p_inv, 1)
                    if 1 <= n <= N:
                        if (n - 1) % NQ == NQ - 1:
                            b = (n - 1) // NQ
                            e.wait_ge(one_mm, turn7[("new", b)])
                            e.tensor_tensor(ss[:, b % 2, PAST:], ps[SP0:SP0 + R, 7, 0:NS], m.newmask[SP0:SP0 + R, b, :], ALU.add).then_inc(one_out, 1)
                            e.drain()
                            e.tensor_reduce(pad[SP0:SP0 + R, 2:3], ss[:, b % 2, :], AX.X, ALU.max)
                            e.drain()
                            e.tensor_scalar(nmax[SP0:SP0 + R, 2:3], pad[SP0:SP0 + R, 2:3], -1.0, None, ALU.mult).then_inc(s_max, 1)
                        i, h = steps[n - 1]
                        o, c = HD * (h % 2), h // 2
                        e.wait_ge(p_pv, n)
                        e.tensor_copy(m.mixT[o:o + HD, 2 + c, i * P:i * P + P], ps[o:o + HD, 4, 0:P]).then_inc(p_oo, 1)
                    if n % NQ == 1 and 1 <= n // NQ <= DEC_B:
                        b = n // NQ - 1
                        e.wait_ge(s_exp, b + 1)
                        e.reciprocal(rinv[SP0:SP0 + R, 2:3], rsum[SP0:SP0 + R, 2:3])
                        e.drain()
                        e.tensor_scalar(ss[:, b % 2, :], ss[:, b % 2, :], rinv[SP0:SP0 + R, 2:3], None, ALU.mult).then_inc(s_p, 1)
                    if n % NQ == 3 and 1 <= n // NQ <= DEC_B:
                        b = n // NQ - 1
                        e.wait_ge(one_mm, turn7[("pv", b)])
                        for h in range(H):
                            o, c = HD * (h % 2), h // 2
                            i = e.tensor_copy(m.mixT[o:o + HD, 2 + c, SEQ + DEC_L * b:SEQ + DEC_L * b + DEC_L],
                                              ps[o:o + HD, 7, 8 * c:8 * c + 8].rearrange("p (q h) -> p h q", h=2)[:, h % 2, :])
                        i.then_inc(one_out, 1)
                for c in range(2):
                    for l in range(DEC_L):
                        e.tensor_tensor(wtmp[:, c, l], us[:, c, :, l:l + TAPS], tapT[:, c, :].unsqueeze(1).broadcast_to([P, DEC_B, TAPS]), ALU.mult)
                    e.drain()
                    for l in range(DEC_L):
                        e.tensor_reduce(y[:, c, SEQ:TOK].rearrange("p (b l) -> p l b", l=DEC_L)[:, l], wtmp[:, c, l], AX.X, ALU.add)
                e.drain()
                for c in range(2):
                    i = e.tensor_scalar(y[:, c, SEQ:TOK], y[:, c, SEQ:TOK], m.cb[:, c:c + 1], None, ALU.add)
                i.then_inc(y_done, 1)
                for n in range(NCH):
                    cc = slice(n * CH, (n + 1) * CH)
                    e.wait_ge(l_mean, n + 1)
                    for c in range(2):
                        i = e.tensor_tensor(y[:, c, cc], y[:, c, cc], ps[:, n, 0:CH], ALU.subtract)
                    i.then_inc(l_sub, 1)
                for n in range(NCH):
                    cc = slice(n * CH, (n + 1) * CH)
                    e.wait_ge(l_std, n + 1)
                    e.reciprocal(lrec[:, cc], lstd[:, cc])
                    e.drain()
                    for c in range(2):
                        i = e.scalar_tensor_tensor(out=y[:, c, cc], in0=y[:, c, cc], scalar=m.ln_g[:, c:c + 1], in1=lrec[:, cc],
                                                   op0=ALU.mult, op1=ALU.mult)
                    i.then_inc(l_scaled, 1)

            @block.tensor
            def _(e):
                for c in range(2):
                    e.transpose(ps[:, 6, c * TAPS:(c + 1) * TAPS], m.tapw[:, c * P:c * P + P], m.ident[0:TAPS, 0:TAPS])
                e.wait_ge(cst_in, 32)
                for g in range(2):
                    for c in range(2):
                        i = e.transpose(ps[:, 7, (2 * g + c) * 4 * NB1:(2 * g + c + 1) * 4 * NB1], cst[:, g, c * P:c * P + P],
                                        m.ident[0:4 * NB1, 0:4 * NB1])
                i.then_inc(set_mm, 1)
                e.wait_ge(sc_tot, 1)
                e.matmul(ps[:, 5, 0:H], m.carry[:], carry[:], start=True, stop=True).then_inc(page_mm, 1)
                for n in range(2 * H):
                    h = n // 2
                    if n >= 4:
                        e.wait_ge(ck_out, n - 3)
                    e.matmul(ps[:, n % 4, :], m.ident[F4, FROW + h:FROW + h + 1].broadcast_to([H, P]),
                             m.CF[F4, n % 2 * 512:n % 2 * 512 + 512], start=True, stop=True).then_inc(ck_mm, 1)
                e.wait_ge(u_ready, 1)
                for c in range(2):
                    e.transpose(ps[0:NS, 6, c * P:c * P + P], u[:, c, NB1 + SEQ - NS:], m.ident[:])
                    i = e.transpose(ps[0:NS, 6, W + c * P:W + c * P + P], unew[:, c, :], m.ident[:])
                i.then_inc(ct_mm, 1)
                e.wait_ge(ct_out, 1)
                e.wait_ge(csel_ready, 1)
                e.wait_ge(qbd_ready, 1)
                e.wait_ge(ck_out, 2 * H)

                def claim7(key):
                    if turn7[key] > 1:
                        e.wait_ge(one_out, turn7[key] - 1)

                for n in range(LAST):
                    if n < N:
                        i, h = steps[n]
                        o, c = HD * (h % 2), h // 2
                        nk = (i + 1) * P
                        if n >= 1:
                            e.wait_ge(p_so, n)
                        for g in range(i // 4 + 1):
                            w = min(512, nk - 512 * g)
                            mm = e.matmul(ps[:, g, 0:w], m.Z[o:o + HD, ZFQ + c, i * P:i * P + P],
                                          m.Z[o:o + HD, ZFK + c, 512 * g:512 * g + w], start=True, stop=True)
                        mm.then_inc(p_sc, 1)
                        e.wait_ge(k_in[n % 2], 16 * QG * (n // 2 + 1))
                        if n >= 1:
                            e.wait_ge(k_o0, n)
                            e.wait_ge(k_o1, n)
                        for c in range(2):
                            for g in range(QG):
                                mm = e.transpose(ps[:, 5 + c, g * PAGE:(g + 1) * PAGE], kpg[:, n % 2, g, c * P:c * P + P], m.ident[:])
                        mm.then_inc(k_tr, 1)
                    if 1 <= n <= N:
                        b, j = (n - 1) // NQ, (n - 1) % NQ
                        claim7(("q", n - 1))
                        e.wait_ge(k_o0, n)
                        e.wait_ge(k_o1, n)
                        if j == 0:
                            e.wait_ge(cb_in[b % 2], 16 * (b // 2 + 1))
                        out = ps[SP0:SP0 + R, 7, :]
                        for c in range(2):
                            e.matmul(out, qbd[:, c, b], kT[:, (n - 1) % 2, c, :], start=(c == 0), stop=False)
                        e.matmul(out, csel[:, b], cb[:, b % 2, 512 * j:512 * j + 512], start=False, stop=True).then_inc(one_mm, 1)
                        if j == NQ - 1:
                            claim7(("new", b))
                            out = ps[SP0:SP0 + R, 7, 0:NS]
                            for c in range(2):
                                e.matmul(out, qbd[:, c, b], m.Z[:, ZFK + c, SEQ:TOK], start=(c == 0), stop=False)
                            mm = e.matmul(out, csel[:, b], cb[:, b % 2, PAST:], start=False, stop=True)
                            mm.then_inc(one_mm, 1)
                            e.drain().then_inc(cb_used, 1)
                        i, h = steps[n - 1]
                        o, c = HD * (h % 2), h // 2
                        e.wait_ge(p_scaled, n)
                        for g in range(i // 4 + 1):
                            k = sum(a // 4 + 1 for a, _ in steps[:n - 1]) + g
                            if k >= 2:
                                e.wait_ge(p_to, k - 1)
                            for a in range(4 * g, min(4 * g + 4, i + 1)):
                                mm = e.transpose(ps[:, 2 + k % 2, (a - 4 * g) * P:(a - 4 * g + 1) * P], sc[:, (n - 1) % 2, a * P:a * P + P], m.ident[:])
                            mm.then_inc(p_tr, 1)
                        e.wait_ge(p_to, sum(a // 4 + 1 for a, _ in steps[:n]))
                        if n >= 2:
                            e.wait_ge(p_oo, n - 1)
                        for a in range(i + 1):
                            mm = e.matmul(ps[o:o + HD, 4, 0:P], m.V[:, a, W + h * HD:W + (h + 1) * HD], pT[:, (n - 1) % 2, a, :],
                                          start=(a == 0), stop=(a == i))
                        mm.then_inc(p_pv, 1)
                    if n % NQ == 2 and 1 <= n // NQ <= DEC_B:
                        b = n // NQ - 1
                        claim7(("tr", b))
                        e.wait_ge(s_p, b + 1)
                        idn = m.ident[SP0:SP0 + R, SP0:SP0 + R]
                        for g in range(NPG):
                            e.transpose(ps[:, 7, g * R:(g + 1) * R], ss[:, b % 2, g * PAGE:(g + 1) * PAGE], idn)
                        e.transpose(ps[0:NS, 7, NPG * R:(NPG + 1) * R], ss[:, b % 2, PAST:], idn).then_inc(one_mm, 1)
                    if n % NQ == 3 and 1 <= n // NQ <= DEC_B:
                        b = n // NQ - 1
                        claim7(("pv", b))
                        e.wait_ge(v_in, 16 * NPG * (b + 1))
                        for c in range(2):
                            for g in range(NPG + 1):
                                lhs = vpg[:, g, c * P:c * P + P] if g < NPG else m.V[0:NS, NT - 1, W + c * P:W + c * P + P]
                                r = P if g < NPG else NS
                                mm = e.matmul(ps[:, 7, 8 * c:8 * c + 8].rearrange("p (q h) -> p q h", h=2), lhs,
                                              sT[0:r, g, :].rearrange("p (q h) -> p q h", h=H)[:, :, 2 * c:2 * c + 2],
                                              start=(g == 0), stop=(g == NPG))
                        mm.then_inc(one_mm, 1)
                        e.drain().then_inc(s_pv, 1)
                e.wait_ge(y_done, 1)
                for n in range(NCH):
                    for c in range(2):
                        mm = e.matmul(ps[:, n, 0:CH], m.chmean[:], y[:, c, n * CH:(n + 1) * CH], start=(c == 0), stop=(c == 1))
                    mm.then_inc(l_mean, 1)
                for n in range(NCH):
                    e.wait_ge(l_sq, n + 1)
                    for c in range(2):
                        mm = e.matmul(ps[:, 4 + n, 0:CH], m.chmean[:], ysq[:, c, n * CH:(n + 1) * CH], start=(c == 0), stop=(c == 1))
                    mm.then_inc(l_var, 1)


def out_projection(nc, m):
    ctx = ExitStack()
    sb = lambda name, shape: ctx.enter_context(nc.sbuf_tensor(name, shape, F32))
    sem = lambda name: ctx.enter_context(nc.semaphore(name))
    ps = m.ps
    with ctx:
        wo = sb("wo", [P, KC, D])
        x1 = sb("x1", [P, 2, D])
        h2 = sb("h2", [P, 2, D])
        h2T = sb("h2T", [P, 2, KC, P])
        junk = sb("junk2", [P, D])
        ssq, std, rstd = sb("ssq2", [P, 2]), sb("std2", [P, 2]), sb("rstd2", [P, 2])
        wo_in, x1_in, h2_sent = sem("wo_in"), [sem(f"x1_in{i}") for i in range(2)], [sem(f"h2_sent{i}") for i in range(2)]
        o_mm, x2_done, std_done, h2_done, h2_tr, h2T_out, lg_mm, lg_out = (
            sem("c_" + n) for n in ("o_mm", "x2", "std", "h2", "h2_tr", "h2T_out", "lg_mm", "lg_out"))

        with nc.Block() as block:

            @block.sync
            def _(e):
                for n in range(2):
                    e.dma_start(wo[:, :, n * 512:(n + 1) * 512],
                                m.w_out[0].rearrange("(k p) n -> p k n", p=P)[:, :, n * 512:(n + 1) * 512]).then_inc(wo_in, 16)
                for t in range(NT):
                    r = rows_of(t)
                    if t >= 2:
                        e.wait_ge(x2_done, t - 1)
                    src = m.x_prompt[0, t * P:(t + 1) * P, :] if t < NT - 1 else m.x_sample.rearrange("b l d -> (b l) d")
                    e.dma_start(x1[0:r, t % 2, :], src).then_inc(x1_in[t % 2], 16)

            @block.gpsimd
            def _(e):
                e.memset(m.gidx[:], 0)
                e.drain()
                e.dma_start(m.slot_tok.rearrange("(p t) a -> p (t a)", t=SLOT_TILES), m.gidx[:]).then_inc(m.s_table, 16)
                for t in range(NT):
                    e.wait_ge(h2_done, t + 1)
                    e.dma_start(m.h2d[t * P:t * P + rows_of(t), :], h2[0:rows_of(t), t % 2, :]).then_inc(h2_sent[t % 2], 16)
                e.wait_ge(m.s_table, 16)
                e.wait_ge(m.s_zero_rows, 16 * (SLOT_TILES - 2 * LEAST_PAIRS))
                for i in range(2):
                    e.wait_ge(h2_sent[i], 16 * ((NT + 1 - i) // 2))

            @block.scalar
            def _(e):
                for t in range(NT):
                    r, b = rows_of(t), t % 2
                    e.wait_ge(x2_done, t + 1)
                    e.activation(junk[0:r], m.x2[0:r, t, :], ACT.Square, scale=D ** -0.5, accum_out=ssq[0:r, b:b + 1])
                    e.drain()
                    e.activation(std[0:r, b:b + 1], ssq[0:r, b:b + 1], ACT.Sqrt, bias=m.eps[0:r, :]).then_inc(std_done, 1)

            @block.vector
            def _(e):
                e.memset(m.logits[:], 0.0)

                def tail(t):
                    r, b = rows_of(t), t % 2
                    e.wait_ge(h2_tr, t + 1)
                    if t >= 2:
                        e.wait_ge(lg_mm, t - 1)
                    for c in range(2):
                        i = e.tensor_tensor(h2T[:, b, 4 * c:4 * c + 4, 0:r], ps[:, 4 + c, :].rearrange("p (k t) -> p k t", k=4)[:, :, 0:r],
                                            m.g2[:, 4 * c:4 * c + 4].unsqueeze(2).broadcast_to([P, 4, r]), ALU.mult)
                    i.then_inc(h2T_out, 1)

                def logits(t):
                    r = rows_of(t)
                    e.wait_ge(lg_mm, t + 1)
                    e.tensor_tensor(m.logits[0:r, t, :], ps[0:r, 6 + t % 2, 0:NG + NE], m.rb[0:r, :], ALU.add).then_inc(lg_out, 1)

                for t in range(NT):
                    r, b = rows_of(t), t % 2
                    e.wait_ge(o_mm, t + 1)
                    e.wait_ge(x1_in[b], 16 * (t // 2 + 1))
                    e.tensor_tensor(m.x2[0:r, t, :], ps[0:r, 2 * b:2 * b + 2, :].rearrange("p c n -> p (c n)"), x1[0:r, b, :], ALU.add).then_inc(x2_done, 1)
                    e.wait_ge(std_done, t + 1)
                    e.reciprocal(rstd[0:r, b:b + 1], std[0:r, b:b + 1])
                    e.drain()
                    if t >= 2:
                        e.wait_ge(h2_tr, t - 1)
                        e.wait_ge(h2_sent[b], 16 * (t // 2))
                    e.tensor_scalar(h2[0:r, b, :], m.x2[0:r, t, :], rstd[0:r, b:b + 1], None, ALU.mult).then_inc(h2_done, 1)
                    tail(t)
                    if t:
                        logits(t - 1)
                logits(NT - 1)

            @block.tensor
            def _(e):
                def product(t):
                    r, b = rows_of(t), t % 2
                    if t >= 2:
                        e.wait_ge(x2_done, t - 1)
                    for n in range(2):
                        for k in range(KC):
                            i = e.matmul(ps[0:r, 2 * b + n, :], m.mixT[:, k, t * P:t * P + r], wo[:, k, n * 512:(n + 1) * 512],
                                         start=(k == 0), stop=(k == KC - 1))
                    i.then_inc(o_mm, 1)

                e.wait_ge(wo_in, 32)
                product(0)
                for t in range(NT):
                    if t + 1 < NT:
                        product(t + 1)
                    r, b = rows_of(t), t % 2
                    e.wait_ge(h2_done, t + 1)
                    if t:
                        e.wait_ge(h2T_out, t)
                    for k in range(KC):
                        i = e.transpose(ps[:, 4 + k // 4, k % 4 * P:k % 4 * P + r], h2[0:r, b, k:D:KC], m.ident[0:r, 0:r])
                    i.then_inc(h2_tr, 1)
                    e.wait_ge(h2T_out, t + 1)
                    if t >= 2:
                        e.wait_ge(lg_out, t - 1)
                    for k in range(KC):
                        i = e.matmul(ps[0:r, 6 + b, 0:NG + NE], h2T[:, b, k, 0:r], m.wr[:, k, :], start=(k == 0), stop=(k == KC - 1))
                    i.then_inc(lg_mm, 1)


def route(nc, m):
    ctx = ExitStack()
    sb = lambda name, shape, dt=F32: ctx.enter_context(nc.sbuf_tensor(name, shape, dt))
    sem = lambda name: ctx.enter_context(nc.semaphore(name))
    ps = m.ps
    B3, B4 = [P, NT, NE], [P, NT, NG, NE // NG]
    with ctx:
        G, E = m.logits[:, :, 0:NG], m.logits[:, :, NG:NG + NE]
        gmax, gsum, gw = sb("gmax", [P, NT]), sb("gsum", [P, NT]), sb("gw", [P, NT])
        gx, gsel = sb("gx", [P, NT, NG]), sb("gsel", [P, NT, NG])
        em, wi, prio = sb("em", B3), sb("wi", B3), sb("prio", B3)
        oh = [sb("oh1", B3), sb("oh2", B3)]
        both, valid = sb("both", B3), sb("valid", [P, NT])
        top = [sb("top1", [P, NT]), sb("top2", [P, NT])]
        first = sb("first", [P, NT])
        ex, den = sb("ex", [P, NT]), sb("den", [P, NT])
        slot = sb("slot", B3)
        run = sb("run", [P, NT + 1, NE])
        ntile, incl, base = sb("ntile", [P, NE]), sb("incl", [P, NE]), sb("base", [P, NE])
        sf = sb("sf", [P, 2, NT])
        pos, pos2 = sb("pos", [P, 2, NT], I32), sb("pos2", [P, 2, NT], I32)
        te = sb("te", [1, SLOT_TILES, NE])
        tsum = sb("tsum", [1, SLOT_TILES])
        gdiff, exps, oh_done, cnt_mm, pos_done, sent, tab_in = (
            sem("r_" + n) for n in ("gdiff", "exps", "oh", "cnt_mm", "pos", "sent", "tab_in"))

        with nc.Block() as block:

            @block.scalar
            def _(e):
                e.wait_ge(gdiff, 1)
                e.activation(gx[:], gx[:], ACT.Exp).then_inc(exps, 1)
                e.wait_ge(gdiff, 2)
                e.activation(ex[:], ex[:], ACT.Exp).then_inc(exps, 1)

            @block.vector
            def _(e):
                bc = lambda x, n: x[:].unsqueeze(2).broadcast_to([P, NT, n])

                def pick(src, mx, out, n, pr):
                    e.tensor_tensor(wi[:, :, 0:n], src, bc(mx, n), ALU.is_equal)
                    e.drain()
                    e.tensor_tensor(wi[:, :, 0:n], wi[:, :, 0:n], pr, ALU.mult)
                    e.drain()
                    e.tensor_reduce(first[:], wi[:, :, 0:n], AX.X, ALU.max)
                    e.drain()
                    e.tensor_tensor(out, wi[:, :, 0:n], bc(first, n), ALU.is_equal)
                    e.drain()

                e.tensor_scalar(prio[:], m.exp_id[:], -1.0, float(NE), ALU.mult, ALU.add)
                e.tensor_scalar(valid[:], m.tok_id[:], float(TOK), None, ALU.is_lt)
                e.tensor_reduce(gmax[:], G, AX.X, ALU.max)
                e.drain()
                e.tensor_tensor(gx[:], G, bc(gmax, NG), ALU.subtract).then_inc(gdiff, 1)
                pick(G, gmax, gsel[:], NG, prio[:, :, 0:NG])
                e.tensor_scalar(gsel[:], gsel[:], -1.0, -NEG, ALU.add, ALU.mult)
                e.drain()
                e.tensor_tensor(em[:].rearrange("p t (g k) -> p t g k", g=NG), E.rearrange("p t (g k) -> p t g k", g=NG),
                                gsel[:].unsqueeze(3).broadcast_to(B4), ALU.add)
                e.drain()
                e.tensor_reduce(top[0][:], em[:], AX.X, ALU.max)
                e.drain()
                pick(em[:], top[0], oh[0][:], NE, prio[:])
                e.scalar_tensor_tensor(out=em[:], in0=oh[0][:], scalar=NEG, in1=em[:], op0=ALU.mult, op1=ALU.add)
                e.drain()
                e.tensor_reduce(top[1][:], em[:], AX.X, ALU.max)
                e.drain()
                e.tensor_tensor(ex[:], top[1][:], top[0][:], ALU.subtract).then_inc(gdiff, 1)
                pick(em[:], top[1], oh[1][:], NE, prio[:])
                e.tensor_tensor(both[:], oh[0][:], oh[1][:], ALU.add)
                e.drain()
                e.tensor_tensor(both[:], both[:], bc(valid, NE), ALU.mult).then_inc(oh_done, 1)
                e.wait_ge(exps, 2)
                e.tensor_reduce(gsum[:], gx[:], AX.X, ALU.add)
                e.tensor_scalar(den[:], ex[:], 1.0, None, ALU.add)
                e.drain()
                e.tensor_tensor(den[:], den[:], gsum[:], ALU.mult)
                e.drain()
                e.reciprocal(m.gate[:, 0, :], den[:])
                e.drain()
                e.tensor_tensor(m.gate[:, 1, :], m.gate[:, 0, :], ex[:], ALU.mult)
                e.wait_ge(cnt_mm, 1)
                e.memset(run[:, 0, :], 0.0)
                e.memset(ntile[:], 0.0)
                e.drain()
                for t in range(NT):
                    e.tensor_tensor(run[:, t + 1, :], run[:, t, :], ps[:, 1, t * NE:(t + 1) * NE], ALU.add)
                    e.drain()
                for j in range(NT):
                    e.scalar_tensor_tensor(out=ntile[:], in0=run[:, NT, :], scalar=float(P * j), in1=ntile[:], op0=ALU.is_gt, op1=ALU.add)
                    e.drain()
                e.tensor_tensor_scan(incl[:], m.ones[:, 0:NE], ntile[:], 0.0, ALU.mult, ALU.add)
                e.drain()
                e.tensor_tensor(base[:], incl[:], ntile[:], ALU.subtract)
                e.tensor_tensor(slot[:], ps[:, 0, 0:NT * NE].rearrange("p (t n) -> p t n", n=NE), run[:, 0:NT, :], ALU.add)
                e.drain()
                e.scalar_tensor_tensor(out=slot[:], in0=base[:].unsqueeze(1).broadcast_to(B3), scalar=float(P), in1=slot[:],
                                       op0=ALU.mult, op1=ALU.add)
                e.drain()
                for c in range(2):
                    e.tensor_tensor(em[:], oh[c][:], slot[:], ALU.mult)
                    e.drain()
                    e.tensor_reduce(sf[:, c, :], em[:], AX.X, ALU.add)
                    e.drain()
                e.tensor_copy(m.slots[:], sf[:])
                e.drain()
                e.tensor_scalar(pos[:], m.slots[:], P - 1, 5, ALU.bitwise_and, ALU.logical_shift_left)
                e.tensor_scalar(pos2[:], m.slots[:], 7, None, ALU.logical_shift_right)
                e.drain()
                e.tensor_tensor(pos[:], pos[:], pos2[:], ALU.add).then_inc(pos_done, 1)
                e.tensor_tensor(te[:], m.tile_id[0:1].unsqueeze(2).broadcast_to([1, SLOT_TILES, NE]),
                                incl[0:1].unsqueeze(1).broadcast_to([1, SLOT_TILES, NE]), ALU.is_ge)
                e.drain()
                e.tensor_reduce(tsum[:], te[:], AX.X, ALU.add)
                e.drain()
                e.tensor_scalar(m.tile_exp[:], tsum[:], float(NE - 1), None, ALU.min)
                e.tensor_scalar(m.more_pairs[:], incl[0:1, NE - 1:NE], 1.0 - 2 * LEAST_PAIRS, 0.0, ALU.add, ALU.max)
                e.drain()
                e.tensor_scalar(m.more_pairs[:], m.more_pairs[:], 1, None, ALU.logical_shift_right)

            @block.tensor
            def _(e):
                e.wait_ge(oh_done, 1)
                rhs = both[:].rearrange("p t n -> p (t n)")
                e.matmul(ps[:, 0, 0:NT * NE], m.strict[:], rhs, start=True, stop=True)
                e.matmul(ps[:, 1, 0:NT * NE], m.ones[:], rhs, start=True, stop=True).then_inc(cnt_mm, 1)

            @block.gpsimd
            def _(e):
                e.wait_ge(pos_done, 1)
                for t in range(NT):
                    r = rows_of(t)
                    for c in range(2):
                        e.indirect_dma_start(out=m.slot_tok, out_offset=bass.IndirectOffsetOnAxis(ap=pos[0:r, c, t:t + 1], axis=0),
                                             in_=m.tok_id[0:r, t:t + 1], in_offset=None).then_inc(sent, 16)
                e.wait_ge(sent, 16 * 2 * NT)
                e.dma_start(m.gidx[:], m.slot_tok.rearrange("(p t) a -> p (t a)", t=SLOT_TILES)).then_inc(tab_in, 16)
                e.wait_ge(tab_in, 16)


def experts(nc, m):
    ctx = ExitStack()
    sb = lambda name, shape, dt=F32: ctx.enter_context(nc.sbuf_tensor(name, shape, dt))
    sem = lambda name: ctx.enter_context(nc.semaphore(name))
    ps = m.ps
    KE = DE // P
    S = SLOT_TILES
    with ctx:
        wg, wu = sb("wg", [P, 2, KC, DE]), sb("wu", [P, 2, KC, DE])
        wd = m.mixT[:].rearrange("p k t -> p (k t)")[:, 0:2 * KE * D].rearrange("p (b k n) -> p b k n", b=2, k=KE)
        hg, hgT = sb("hg", [P, 2, D]), sb("hgT", [P, 2, KC, P])
        gcol = [sb(f"gcol{i}", [P, 1], I32) for i in range(2)]
        sg, he, heT = sb("sg", [P, 2, DE]), sb("he", [P, 2, DE]), sb("heT", [P, 2, KE, P])
        yo = sb("yo", [P, 2, D])
        landed = sb("landed", [1, 2])
        pair = lambda n: [sem(f"{n}{i}") for i in range(2)]
        gu_in, dn_in, hg_in, y_sent = pair("gu_in"), pair("dn_in"), pair("hg_in"), pair("y_sent")
        t_mm, t_out, gu_mm, silu, he_done, he_mm, he_out, d_mm, y_a, y_v = (
            sem("e_" + n) for n in ("t_mm", "t_out", "gu_mm", "silu", "he", "he_mm", "he_out", "d_mm", "y_a", "y_v"))


        def pairs(e):
            return e.value_load(m.more_pairs[0:1, 0:1], min_val=0, max_val=S // 2 - LEAST_PAIRS) + LEAST_PAIRS

        with nc.Block() as block:

            @block.sync
            def _(e):
                def load(s, b, first=False):
                    x = e.value_load(m.tile_exp[0:1, ds(s, 1)], min_val=0, max_val=NE - 1)
                    for n, (to, of) in enumerate(((wg, m.exp_w_gate), (wu, m.exp_w_up))):
                        if n == 0 and not first:
                            e.wait_ge(gu_mm, s - 1)
                        e.dma_start(to[:, b].unsqueeze(1), of[0, ds(x, 1)].rearrange("a (p k) n -> p a k n", k=KC)).then_inc(gu_in[b], 16)
                    if not first:
                        e.wait_ge(d_mm, s - 1)
                    e.dma_start(wd[:, b].unsqueeze(1), m.exp_w_down[0, ds(x, 1)].rearrange("a (p k) n -> p a k n", k=KE)).then_inc(dn_in[b], 16)

                load(0, 0, True)
                load(1, 1, True)
                with e.Fori(1, pairs(e)) as j:
                    load(2 * j, 0)
                    load(2 * j + 1, 1)

            @block.gpsimd
            def _(e):
                def gather(s, b, first=False):
                    if not first:
                        e.wait_ge(t_mm, s - 1)
                    e.tensor_copy(gcol[b][:], m.gidx[:, ds(s, 1)])
                    e.drain()
                    e.indirect_dma_start(out=hg[:, b, :], out_offset=None, in_=m.h2d,
                                         in_offset=bass.IndirectOffsetOnAxis(ap=gcol[b][:, 0:1], axis=0)).then_inc(hg_in[b], 16)

                gather(0, 0, True)
                gather(1, 1, True)
                with e.Fori(1, pairs(e)) as j:
                    gather(2 * j, 0)
                    gather(2 * j + 1, 1)

            @block.scalar
            def _(e):
                def act_silu(s, b):
                    e.wait_ge(gu_mm, s + 1)
                    e.activation(sg[:, b, :], ps[:, 2 * b, :], ACT.Silu).then_inc(silu, 1)

                def step(s, b, j, last=False):
                    e.wait_ge(he_mm, s + 1)
                    e.copy(heT[:, b], ps[:, 2 * b, :].rearrange("p (k t) -> p k t", k=KE)).then_inc(he_out, 1)
                    e.wait_ge(d_mm, s + 1)
                    if not (isinstance(j, int) and j == 0):
                        e.wait_ge(y_sent[b], 16 * j)
                    e.copy(yo[:, b, 0:512], ps[:, 6, :]).then_inc(y_a, 1)
                    e.wait_ge(y_a, s + 1)
                    e.wait_ge(y_v, s + 1)
                    e.dma_start(m.yd[ds(s * P, P), :], yo[:, b, :]).then_inc(y_sent[b], 16)
                    if not last:
                        act_silu(s + 2, b)

                act_silu(0, 0)
                act_silu(1, 1)
                step(0, 0, 0)
                step(1, 1, 0)
                n = pairs(e)
                with e.Fori(1, n - 1) as j:
                    step(2 * j, 0, j)
                    step(2 * j + 1, 1, j)
                step(2 * n - 2, 0, n - 1, True)
                step(2 * n - 1, 1, n - 1, True)
                for i in range(2):
                    e.wait_ge(y_sent[i], 16 * n)
                    e.copy(landed[0:1, i:i + 1], m.eps[0:1, :])

            @block.vector
            def _(e):
                def turn_out(s, b, first=False):
                    e.wait_ge(t_mm, s + 1)
                    if not first:
                        e.wait_ge(gu_mm, s - 1)
                    for c in range(2):
                        i = e.tensor_tensor(hgT[:, b, 4 * c:4 * c + 4, :], ps[:, 4 + c, :].rearrange("p (k t) -> p k t", k=4),
                                            m.g2[:, 4 * c:4 * c + 4].unsqueeze(2).broadcast_to([P, 4, P]), ALU.mult)
                    i.then_inc(t_out, 1)

                def make_he(s, b):
                    e.wait_ge(silu, s + 1)
                    e.tensor_tensor(he[:, b, :], sg[:, b, :], ps[:, 2 * b + 1, :], ALU.mult).then_inc(he_done, 1)

                def step(s, b, j, last=False):
                    if not last:
                        turn_out(s + 2, b)
                    e.wait_ge(d_mm, s + 1)
                    if not (isinstance(j, int) and j == 0):
                        e.wait_ge(y_sent[b], 16 * j)
                    e.tensor_copy(yo[:, b, 512:], ps[:, 7, :]).then_inc(y_v, 1)
                    if not last:
                        make_he(s + 2, b)

                for s in range(2):
                    turn_out(s, s, True)
                    make_he(s, s)
                step(0, 0, 0)
                step(1, 1, 0)
                n = pairs(e)
                with e.Fori(1, n - 1) as j:
                    step(2 * j, 0, j)
                    step(2 * j + 1, 1, j)
                step(2 * n - 2, 0, n - 1, True)
                step(2 * n - 1, 1, n - 1, True)

            @block.tensor
            def _(e):
                def turn(s, b, j):
                    e.wait_ge(hg_in[b], 16 * j + 16)
                    if not (isinstance(s, int) and s == 0):
                        e.wait_ge(t_out, s)
                    for k in range(KC):
                        i = e.transpose(ps[:, 4 + k // 4, k % 4 * P:k % 4 * P + P], hg[:, b, k:D:KC], m.ident[:])
                    i.then_inc(t_mm, 1)

                def gate_up(s, b, j):
                    e.wait_ge(t_out, s + 1)
                    e.wait_ge(gu_in[b], 32 * j + 32)
                    for n, w in enumerate((wg, wu)):
                        for k in range(KC):
                            i = e.matmul(ps[:, 2 * b + n, :], hgT[:, b, k, :], w[:, b, k, :], start=(k == 0), stop=(k == KC - 1))
                    i.then_inc(gu_mm, 1)

                def step(s, b, j, last=False):
                    e.wait_ge(he_done, s + 1)
                    for k in range(KE):
                        i = e.transpose(ps[:, 2 * b, k * P:k * P + P], he[:, b, k:DE:KE], m.ident[:])
                    i.then_inc(he_mm, 1)
                    if not last:
                        turn(s + 2, b, j + 1)
                    e.wait_ge(he_out, s + 1)
                    e.wait_ge(dn_in[b], 16 * j + 16)
                    if not (isinstance(s, int) and s == 0):
                        e.wait_ge(y_a, s)
                        e.wait_ge(y_v, s)
                    for n in range(2):
                        for k in range(KE):
                            i = e.matmul(ps[:, 6 + n, :], heT[:, b, k, :], wd[:, b, k, n * 512:(n + 1) * 512],
                                         start=(k == 0), stop=(k == KE - 1))
                    i.then_inc(d_mm, 1)
                    if not last:
                        gate_up(s + 2, b, j + 1)

                for s in range(2):
                    turn(s, s, 0)
                    gate_up(s, s, 0)
                step(0, 0, 0)
                step(1, 1, 0)
                n = pairs(e)
                with e.Fori(1, n - 1) as j:
                    step(2 * j, 0, j)
                    step(2 * j + 1, 1, j)
                step(2 * n - 2, 0, n - 1, True)
                step(2 * n - 1, 1, n - 1, True)


def combine(nc, m):
    ctx = ExitStack()
    sem = lambda name: ctx.enter_context(nc.semaphore(name))
    with ctx:
        yr = ctx.enter_context(nc.sbuf_tensor("yr", [P, 4, D], F32))
        rows_in, done, sent = [sem(f"rows_in{i}") for i in range(4)], sem("y_done2"), sem("y_out")

        with nc.Block() as block:

            @block.gpsimd
            def _(e):
                for t in range(NT):
                    r = rows_of(t)
                    for c in range(2):
                        b = 2 * (t % 2) + c
                        if t >= 2:
                            e.wait_ge(done, t - 1)
                        e.indirect_dma_start(out=yr[0:r, b, :], out_offset=None, in_=m.yd,
                                             in_offset=bass.IndirectOffsetOnAxis(ap=m.slots[0:r, c, t:t + 1], axis=0)).then_inc(rows_in[b], 16)

            @block.vector
            def _(e):
                for t in range(NT):
                    r = rows_of(t)
                    for c in range(2):
                        b = 2 * (t % 2) + c
                        e.wait_ge(rows_in[b], 16 * (t // 2 + 1))
                        i = e.scalar_tensor_tensor(out=m.x2[0:r, t, :], in0=yr[0:r, b, :], scalar=m.gate[0:r, c, t:t + 1],
                                                   in1=m.x2[0:r, t, :], op0=ALU.mult, op1=ALU.add)
                        if c == 0:
                            e.drain()
                    i.then_inc(done, 1)

            @block.sync
            def _(e):
                for t in range(NT):
                    e.wait_ge(done, t + 1)
                    to = m.y_prompt[0, t * P:(t + 1) * P, :] if t < NT - 1 else m.y_sample.rearrange("b l d -> (b l) d")
                    e.dma_start(to, m.x2[0:rows_of(t), t, :]).then_inc(sent, 16)
                e.wait_ge(sent, 16 * NT)


OUTS = [("y_prompt", (1, SEQ, D)), ("y_sample", (DEC_B, DEC_L, D)),
        ("k_prompt", (1, 1, SEQ, H, HD)), ("v_prompt", (1, 1, SEQ, H, HD)), ("logf_prompt", (1, 1, SEQ, H)),
        ("k_sample", (1, DEC_B, DEC_L, H, HD)), ("v_sample", (1, DEC_B, DEC_L, H, HD)), ("logf_sample", (1, DEC_B, DEC_L, H)),
        ("gla_prompt", (1, 1, H, HD, HD)), ("gla_sample", (1, DEC_B, H, HD, HD)),
        ("conv_prompt", (1, 1, TAPS - 1, W)), ("conv_sample", (1, DEC_B, TAPS - 1, W)),
        ("pool_prompt", (1, 1, PMAX - 1, W)), ("pool_sample", (1, DEC_B, PMAX - 1, W))]


def program(nc, m):
    ctx = ExitStack()
    sb = lambda name, shape, dt=F32: ctx.enter_context(nc.sbuf_tensor(name, shape, dt))
    with ctx:
        m.ps = ctx.enter_context(nc.psum_tensor("ps", [P, 8, 512], F32))
        m.s_param, m.s_zero_rows = (ctx.enter_context(nc.semaphore(n)) for n in ("s_param", "s_zero_rows"))
        m.ident, m.ones, m.headmean, m.chmean = sb("ident", [P, P]), sb("ones", [P, P]), sb("headmean", [P, P]), sb("chmean", [P, P])
        m.causal, m.strict, m.qmask = sb("causal", [P, P]), sb("strict", [P, P]), sb("qmask", [P, P])
        m.sampmask, m.newmask = sb("sampmask", [NS, NS]), sb("newmask", [HD + DEC_L * H, DEC_B, NS])
        m.eps = sb("eps", [P, 1])
        m.carry, m.headsel = sb("carry", [P, P]), sb("headsel", [FROW + H, DEC_L * H])
        m.reset, m.poolw = sb("reset", [P, TOK]), sb("poolw", [P, 2, P])
        m.tok_id = sb("tok_id", [P, NT], I32)
        m.exp_id_i, m.exp_id = sb("exp_id_i", [P, NT, NE], I32), sb("exp_id", [P, NT, NE])
        m.tile_id_i, m.tile_id = sb("tile_id_i", [P, SLOT_TILES], I32), sb("tile_id", [P, SLOT_TILES])
        m.count_i, m.count = sb("count_i", [P, PMAX], I32), sb("count", [P, PMAX])
        m.g1, m.g2 = sb("g1", [P, KC]), sb("g2", [P, KC])
        m.gla_g, m.gla_b, m.cb, m.ln_g, m.ln_b, m.pscale = (sb(n, [P, 2]) for n in ("gla_g", "gla_b", "cb", "ln_g", "ln_b", "pscale"))
        m.fqg, m.fkg, m.fb = sb("fqg", [P, 1]), sb("fkg", [P, 1]), sb("fb", [FROW + H, 1])
        m.wa2, m.tapw = sb("wa2", [RANK, W]), sb("tapw", [TAPS, W])
        m.wr, m.rb = sb("wr", [P, KC, NG + NE]), sb("rb", [P, NG + NE])
        m.pages, m.pages_col = sb("pages", [1, P], I32), sb("pages_col", [P, 1], I32)
        m.fqg8 = sb("fqg8", [P, 1])
        m.CF, m.lft = sb("CF", [FROW + H, TOK]), sb("lft", [P, NT, 2 * H])
        constants(nc, m)
        m.mixT = sb("mixT", [P, KC, TOK])
        with (nc.sbuf_tensor("Z", [P, 16, TOK], F32) as m.Z, nc.sbuf_tensor("ZS", [FROW + H, TOK], F32) as m.ZS,
              nc.sbuf_tensor("V", [P, NT, 2 * W], F32) as m.V):
            projections(nc, m)
            gla_pool_norms(nc, m)
            fox_conv(nc, m)
        m.s_table = ctx.enter_context(nc.semaphore("s_table"))
        m.x2 = sb("x2", [P, NT, D])
        m.logits = sb("logits", [P, NT, NG + NE])
        m.gate, m.slots = sb("gate", [P, 2, NT]), sb("slots", [P, 2, NT], I32)
        m.gidx, m.tile_exp = sb("gidx", [P, SLOT_TILES], I32), sb("tile_exp", [1, SLOT_TILES], I32)
        m.more_pairs = sb("more_pairs", [1, 1], I32)
        out_projection(nc, m)
        route(nc, m)
        experts(nc, m)
        combine(nc, m)


def build(nc, arrays):
    m = Memory()
    m.x_prompt, m.x_sample, m.cache_k, m.cache_v = arrays["x_prompt"], arrays["x_sample"], arrays["cache_k"], arrays["cache_v"]
    m.cache_logf, m.page_table, m.state_gla, m.state_conv = arrays["cache_logf"], arrays["page_table"], arrays["state_gla"], arrays["state_conv"]
    m.state_pool, m.norm1_g, m.w_in, m.gla_w_a2 = arrays["state_pool"], arrays["norm1_g"], arrays["w_in"], arrays["gla_w_a2"]
    m.gla_b_a, m.gla_norm_g, m.fox_b_f, m.fox_q_norm_g = arrays["gla_b_a"], arrays["gla_norm_g"], arrays["fox_b_f"], arrays["fox_q_norm_g"]
    m.fox_k_norm_g, m.conv_w, m.conv_b, m.conv_ln_g = arrays["fox_k_norm_g"], arrays["conv_w"], arrays["conv_b"], arrays["conv_ln_g"]
    m.conv_ln_b, m.pool_w, m.pool_scale, m.w_out = arrays["conv_ln_b"], arrays["pool_w"], arrays["pool_scale"], arrays["w_out"]
    m.norm2_g, m.router_wg, m.router_bg, m.router_we = arrays["norm2_g"], arrays["router_wg"], arrays["router_bg"], arrays["router_we"]
    m.router_be, m.exp_w_gate, m.exp_w_up, m.exp_w_down = arrays["router_be"], arrays["exp_w_gate"], arrays["exp_w_up"], arrays["exp_w_down"]
    m.y_prompt, m.y_sample, m.k_prompt, m.v_prompt = arrays["y_prompt"], arrays["y_sample"], arrays["k_prompt"], arrays["v_prompt"]
    m.logf_prompt, m.k_sample, m.v_sample, m.logf_sample = arrays["logf_prompt"], arrays["k_sample"], arrays["v_sample"], arrays["logf_sample"]
    m.gla_prompt, m.gla_sample, m.conv_prompt, m.conv_sample = arrays["gla_prompt"], arrays["gla_sample"], arrays["conv_prompt"], arrays["conv_sample"]
    m.pool_prompt, m.pool_sample = arrays["pool_prompt"], arrays["pool_sample"]
    m.cd = nc.dram_tensor("page_sums", (DEC_B, H, PAST), F32, kind="Internal").ap()
    m.h2d = nc.dram_tensor("normed_rows", (TOK, D), F32, kind="Internal").ap()
    m.slot_tok = nc.dram_tensor("slot_tokens", (SLOT_TILES * P, 1), I32, kind="Internal").ap()
    m.yd = nc.dram_tensor("slot_rows", (SLOT_TILES * P, D), F32, kind="Internal").ap()
    program(nc, m)


def kernel(**inputs):
    import numpy as np
    import concourse.bacc as bacc
    from concourse.bass_utils import run_bass_kernel_spmd

    nc = bacc.Bacc("TRN2", target_bir_lowering=False, num_devices=1)
    arrays, handles = {}, {}
    for name, a in inputs.items():
        arrays["in_" + name] = np.ascontiguousarray(a)
        handles[name] = nc.dram_tensor("in_" + name, arrays["in_" + name].shape, mybir.dt.from_np(arrays["in_" + name].dtype),
                                       kind="ExternalInput").ap()
    for name, shape in OUTS:
        handles[name] = nc.dram_tensor("out_" + name, shape, F32, kind="ExternalOutput").ap()
    build(nc, handles)
    r = run_bass_kernel_spmd(nc, [arrays], core_ids=[0])
    return tuple(r.results[0]["out_" + name] for name, _ in OUTS)
```

```python
from contextlib import ExitStack

import concourse.bass as bass
from concourse import mybir
from concourse.bass import ds

F32 = mybir.dt.float32
I32 = mybir.dt.int32
ALU = mybir.AluOpType
ACT = mybir.ActivationFunctionType
AX = mybir.AxisListType

P = 128
D = 1024
KC = D // P
SEQ = 1024
DEC_B, DEC_L = 8, 4
NS = DEC_B * DEC_L
TOK = SEQ + NS
NT = SEQ // P + 1
W = 256
H, HD = 4, 64
RANK = 16
TAU = 16.0
TAPS = 31
PMAX = 16
WINDOWS = (2, 4, 8, 16)
PAGE = 128
NPG = 16
POOLPG = 160
PAST = NPG * PAGE
EPS = 1e-6
NEG = -1e30
NE, NG = 16, 4
DE = 512
SLOT_TILES = (2 * TOK) // P + NE
LEAST_PAIRS = (-(-2 * TOK // P) + 1) // 2
CH = 352
NCH = TOK // CH

GQ, GK, GV, GG, GA, FQ, FK, FV, FF, CA, CB, PU = 0, 256, 512, 768, 1024, 1040, 1296, 1552, 1808, 1812, 2068, 2324
N_IN = PU + W
Z_GROUPS = (GQ, GK, GG, FQ, FK, CA, CB, PU)
Z_ORDER = (5, 6, 3, 4, 0, 1, 2, 7)
ZQ, ZK, ZG, ZFQ, ZFK, ZCA, ZCB, ZPU = range(0, 16, 2)
FROW = 32


class Memory:
    pass


def rows_of(t):
    return P if t < NT - 1 else NS


def constants(nc, m):
    with nc.Block() as block:

        @block.gpsimd
        def _(e):
            for t, v in ((m.ident, 0.0), (m.ones, 1.0), (m.headmean, 0.0), (m.chmean, 1.0 / W),
                         (m.causal, 1.0), (m.strict, 1.0), (m.qmask, 0.0), (m.sampmask, 1.0),
                         (m.carry, 1.0), (m.pagesel, 1.0), (m.reset, 1.0),
                         (m.poolw, 0.0), (m.eps, EPS)):
                e.memset(t[:], v)
            e.drain()
            for i in range(2):
                e.memset(m.headmean[64 * i:64 * i + 64, 64 * i:64 * i + 64], 1.0 / HD)
                e.drain()
            e.memset(m.reset[:, 0:SEQ].rearrange("p (c t) -> p c t", t=P)[:, :, 0:1], 0.0)
            e.memset(m.reset[:, SEQ:TOK].rearrange("p (c t) -> p c t", t=DEC_L)[:, :, 0:1], 0.0)
            e.drain()
            e.affine_select(out=m.ident[:], in_=m.ident[:], compare_op=ALU.not_equal, fill=1.0, base=0,
                            pattern=[[-1, P]], channel_multiplier=1)
            e.drain()
            e.affine_select(out=m.causal[:], in_=m.causal[:], compare_op=ALU.is_ge, fill=0.0, base=0,
                            pattern=[[1, P]], channel_multiplier=-1)
            e.drain()
            e.affine_select(out=m.strict[:], in_=m.strict[:], compare_op=ALU.is_gt, fill=0.0, base=0,
                            pattern=[[1, P]], channel_multiplier=-1)
            e.drain()
            e.affine_select(out=m.qmask[:], in_=m.qmask[:], compare_op=ALU.is_ge, fill=NEG, base=0,
                            pattern=[[-1, P]], channel_multiplier=1)
            e.drain()
            e.affine_select(out=m.sampmask[:], in_=m.sampmask[:], compare_op=ALU.is_ge, fill=0.0, base=0,
                            pattern=[[1, NS]], channel_multiplier=-1)
            e.drain()
            e.affine_select(out=m.carry[:], in_=m.carry[:], compare_op=ALU.is_gt, fill=0.0, base=0,
                            pattern=[[1, P]], channel_multiplier=-1)
            e.drain()
            e.affine_select(out=m.pagesel[:], in_=m.pagesel[:], compare_op=ALU.is_ge, fill=0.0, base=0,
                            pattern=[[-NPG, DEC_B], [0, DEC_L]], channel_multiplier=1)
            e.drain()
            e.iota(m.tok_id[:], pattern=[[P, NT]], base=0, channel_multiplier=1)
            e.iota(m.exp_id_i[:], pattern=[[0, NT], [1, NE]], base=0, channel_multiplier=0)
            e.iota(m.tile_id_i[:], pattern=[[1, SLOT_TILES]], base=0, channel_multiplier=0)
            e.iota(m.count_i[:], pattern=[[1, PMAX]], base=1, channel_multiplier=0)
            e.drain()
            e.affine_select(out=m.pagesel[:], in_=m.pagesel[:], compare_op=ALU.is_ge, fill=0.0, base=NPG - 1,
                            pattern=[[NPG, DEC_B], [0, DEC_L]], channel_multiplier=-1)
            e.drain()
            e.affine_select(out=m.sampmask[:], in_=m.sampmask[:], compare_op=ALU.is_ge, fill=0.0, base=0,
                            pattern=[[-DEC_L, DEC_B], [0, DEC_L]], channel_multiplier=1)
            e.drain()
            e.affine_select(out=m.carry[:], in_=m.carry[:], compare_op=ALU.is_ge, fill=0.0, base=0,
                            pattern=[[-NPG, DEC_B], [0, NPG]], channel_multiplier=1)
            e.drain()
            e.tensor_copy(m.exp_id[:], m.exp_id_i[:])
            e.tensor_copy(m.tile_id[:], m.tile_id_i[:])
            e.tensor_copy(m.count[:], m.count_i[:])

        @block.sync
        def _(e):
            loads = [
                (m.g1[:], m.norm1_g[0].rearrange("(p k) -> p k", k=KC)),
                (m.g2[:], m.norm2_g[0].rearrange("(p k) -> p k", k=KC)),
                (m.gla_g[:], m.gla_norm_g[0].rearrange("(c p) -> p c", p=P)),
                (m.gla_b[:], m.gla_b_a[0].rearrange("(c p) -> p c", p=P)),
                (m.cb[:], m.conv_b[0].rearrange("(c p) -> p c", p=P)),
                (m.ln_g[:], m.conv_ln_g[0].rearrange("(c p) -> p c", p=P)),
                (m.ln_b[:], m.conv_ln_b[0].rearrange("(c p) -> p c", p=P)),
                (m.pscale[:], m.pool_scale[0].rearrange("(c p) -> p c", p=P)),
                (m.wa2[:], m.gla_w_a2[0]),
                (m.tapw[:], m.conv_w[0]),
                (m.fb[FROW:FROW + H, :], m.fox_b_f[0].rearrange("(h a) -> h a", a=1)),
                (m.wr[:, :, 0:NG], m.router_wg[0].rearrange("(p k) n -> p k n", k=KC)),
                (m.wr[:, :, NG:NG + NE], m.router_we[0].rearrange("(p k) n -> p k n", k=KC)),
                (m.rb[:, 0:NG], m.router_bg[0].partition_broadcast(P)),
                (m.rb[:, NG:NG + NE], m.router_be[0].partition_broadcast(P)),
                (m.pages[:], m.page_table.rearrange("b g -> (b g)").rearrange("(a n) -> a n", a=1)),
                (m.pages_col[:], m.page_table.rearrange("b g -> (b g)").rearrange("(n a) -> n a", a=1)),
            ]
            for i in range(2):
                loads.append((m.fqg[64 * i:64 * i + 64, :], m.fox_q_norm_g[0].rearrange("(p a) -> p a", a=1)))
                loads.append((m.fkg[64 * i:64 * i + 64, :], m.fox_k_norm_g[0].rearrange("(p a) -> p a", a=1)))
            for to, of in loads:
                e.dma_start(to, of, allow_slow_non_contiguous=True).then_inc(m.s_param, 16)
            m.n_params = len(loads)
            e.wait_ge(m.s_param, 16 * m.n_params)

    with nc.Block() as block:

        @block.sync
        def _(e):
            for g in range(4):
                o = HD * (g % 2)
                e.dma_start(m.poolw[o:o + HD, g // 2, o:o + HD], m.pool_w[0, g]).then_inc(m.s_param, 16)
            e.wait_ge(m.s_param, 16 * (m.n_params + 4))

        @block.vector
        def _(e):
            e.tensor_scalar(m.fqg8[:], m.fqg[:], HD ** -0.5, None, ALU.mult)


def projections(nc, m):
    ctx = ExitStack()
    sb = lambda name, shape: ctx.enter_context(nc.sbuf_tensor(name, shape, F32))
    sem = lambda name: ctx.enter_context(nc.semaphore(name))
    NB1 = TAPS - 1
    ps = m.ps
    with ctx:
        hT = m.mixT
        xt = sb("xt", [P, 2, D])
        hn = sb("hn", [P, 2, D])
        junk = sb("junk", [P, D])
        ssq = sb("ssq", [P, 2])
        std = sb("std", [P, 2])
        rstd = sb("rstd", [P, 2])
        wv = sb("wv", [P, KC, 2 * W])
        wz = sb("wz", [P, 2, KC, W])
        wsm = sb("wsm", [P, KC, FROW + H])
        us = sb("us", [P, 2, DEC_B, NB1 + DEC_L])
        cst = sb("cst", [DEC_B // 2 * NB1, 2, W])
        tapT = sb("tapT", [P, 2, TAPS])
        hstd = sb("head_std", [P, 2, CH])
        ctail = cst[0:NS]
        hsq = junk[:, 0:2 * CH].rearrange("p (b n) -> p b n", b=2)
        wtmp = m.Z[:, ZPU, 0:DEC_L * DEC_B * TAPS].rearrange("p (l b k) -> p l b k", l=DEC_L, b=DEC_B)
        lstd = m.Z[:, ZPU, :]
        zrow = m.Z[:, ZPU + 1, 0:D]
        u, y = m.Z[:, ZCA:ZCA + 2, :], m.Z[:, ZCB:ZCB + 2, :]
        ysq = u
        ps_t, ps_v, ps_z = m.ps[:, 0:2, :], m.ps[:, 2:4, :], m.ps[:, 4:8, :]

        x_in = [sem(f"x_in{i}") for i in range(2)]
        std_ready, normed, turned, ht_ready = sem("std_ready"), sem("normed"), sem("turned"), sem("ht_ready")
        wv_in, wsm_in, cst_in = sem("wv_in"), sem("wsm_in"), sem("cst_in")
        rows_mm, rows_out = sem("rows_mm"), sem("rows_out")
        v_done, v_out, v_stored = sem("v_done"), sem("v_out"), sem("v_stored")
        wz_in = [sem(f"wz_in{i}") for i in range(2)]
        z_done, z_out = sem("z_done"), sem("z_out")
        sig, u_ready, y_done = sem("sig"), sem("u_ready"), sem("y_done")
        l_mean, l_sub, l_sq, l_var, l_std, l_scaled = (sem("ln_" + n) for n in ("mean", "sub", "sq", "var", "std", "scaled"))
        n_sq, n_ms, n_std, n_norm = sem("n_sq"), sem("n_ms"), sem("n_std"), sem("n_norm")

        w_rows = m.w_in[0].rearrange("(p k) n -> p k n", k=KC)
        NZ = len(Z_ORDER)
        PER = 2 * NCH
        ALL = NZ * PER + NCH
        cols = lambda n: slice(n * CH, (n + 1) * CH)
        filled = lambda tile: (Z_ORDER.index(tile // 2) + 1) * PER

        SIG_AT, TAIL_AT, MEAN_AT, VAR_AT, NORM_AT = 2 * PER, 2 * PER + 4, 32, 34, 37
        fox_norms = [(z, g, n) for z, g in ((ZFQ, m.fqg8[:]), (ZFQ + 1, m.fqg8[:]), (ZFK, m.fkg[:]), (ZFK + 1, m.fkg[:]))
                     for n in range(NCH)]
        NN = len(fox_norms)
        assert NORM_AT >= filled(ZFK) and NORM_AT + NN <= ALL and VAR_AT + 1 < (NZ - 1) * PER
        tapped = [(k, c) for k in reversed(range(TAPS)) for c in range(2)]

        with nc.Block() as block:

            @block.sync
            def _(e):
                for t in range(NT):
                    r = rows_of(t)
                    if t >= 2:
                        e.wait_ge(normed, t - 1)
                    src = m.x_prompt[0, t * P:(t + 1) * P, :] if t < NT - 1 else m.x_sample.rearrange("b l d -> (b l) d")
                    e.dma_start(xt[0:r, t % 2, :], src).then_inc(x_in[t % 2], 16)
                    if t == 1:
                        e.dma_start(wv[:, :, 0:W], w_rows[:, :, GV:GV + W]).then_inc(wv_in, 16)
                        e.dma_start(wv[:, :, W:2 * W], w_rows[:, :, FV:FV + W]).then_inc(wv_in, 16)
                for g, z in enumerate(Z_ORDER):
                    c = Z_GROUPS[z]
                    if g >= 2:
                        e.wait_ge(z_done, PER * (g - 1))
                    e.dma_start(wz[:, g % 2, :, :], w_rows[:, :, c:c + W]).then_inc(wz_in[g % 2], 16)
                for t in range(NT):
                    r = rows_of(t)
                    e.wait_ge(v_out, t + 1)
                    to = m.v_prompt[0, 0, t * P:(t + 1) * P] if t < NT - 1 else m.v_sample[0].rearrange("b l h d -> (b l) h d")
                    e.dma_start(to.rearrange("p h d -> p (h d)"), m.V[0:r, t, W:2 * W]).then_inc(v_stored, 16)
                e.wait_ge(rows_out, 2)
                e.dma_start(m.conv_prompt[0, 0], ctail[NS - NB1:NS, 0, :]).then_inc(v_stored, 16)
                for b in range(DEC_B):
                    e.dma_start(m.conv_sample[0, b, NB1 - DEC_L:NB1, :], ctail[DEC_L * b:DEC_L * b + DEC_L, 1, :]).then_inc(v_stored, 16)
                e.wait_ge(v_stored, 16 * (NT + 1 + DEC_B))

            @block.gpsimd
            def _(e):
                for g in range(2):
                    e.dma_start(cst[:, g, :], m.state_conv[0, g * (DEC_B // 2):(g + 1) * (DEC_B // 2)].rearrange("b t c -> (b t) c")).then_inc(cst_in, 16)
                e.memset(wsm[:], 0.0)
                e.memset(zrow, 0.0)
                e.drain()
                e.dma_start(wsm[:, :, 0:RANK], w_rows[:, :, GA:GA + RANK]).then_inc(wsm_in, 16)
                e.dma_start(wsm[:, :, FROW:FROW + H], w_rows[:, :, FF:FF + H]).then_inc(wsm_in, 16)
                for t in range(2 * LEAST_PAIRS, SLOT_TILES):
                    e.dma_start(m.yd[t * P:(t + 1) * P, :], zrow).then_inc(m.s_zero_rows, 16)

            @block.scalar
            def _(e):
                def square(t):
                    r = rows_of(t)
                    e.wait_ge(x_in[t % 2], 16 * (t // 2 + 1))
                    e.activation(junk[0:r], xt[0:r, t % 2, :], ACT.Square, scale=D ** -0.5,
                                 accum_out=ssq[0:r, t % 2:t % 2 + 1])
                    e.drain()
                    e.activation(std[0:r, t % 2:t % 2 + 1], ssq[0:r, t % 2:t % 2 + 1], ACT.Sqrt,
                                 bias=m.eps[0:r, :]).then_inc(std_ready, 1)

                square(0)
                for t in range(NT):
                    if t + 1 < NT:
                        square(t + 1)
                    r = rows_of(t)
                    e.wait_ge(v_done, t + 1)
                    e.copy(m.V[0:r, t, :], ps_v[0:r, t % 2, :]).then_inc(v_out, 1)
                e.drain()
                for n in range(ALL):
                    e.wait_ge(z_done, n + 1)
                    if n < NZ * PER:
                        z = 2 * Z_ORDER[n // PER] + n % PER // NCH
                        if n == (NZ - 1) * PER:
                            e.wait_ge(l_scaled, NCH)
                            e.wait_ge(m.s_zero_rows, 16 * (SLOT_TILES - 2 * LEAST_PAIRS))
                        e.copy(m.Z[:, z, cols(n % NCH)], ps_z[:, n % 4, 0:CH]).then_inc(z_out, 1)
                    else:
                        e.copy(m.ZS[:, cols(n % NCH)], ps_z[0:FROW + H, n % 4, 0:CH]).then_inc(z_out, 1)
                    if n + 1 == SIG_AT:
                        e.drain()
                        e.activation(y, y, ACT.Sigmoid).then_inc(sig, 1)
                    if n == MEAN_AT:
                        for i in range(NCH):
                            e.wait_ge(l_sub, i + 1)
                            e.activation(ysq[:, :, cols(i)], y[:, :, cols(i)], ACT.Square).then_inc(l_sq, 1)
                    if n == VAR_AT:
                        for i in range(NCH):
                            e.wait_ge(l_var, i + 1)
                            e.activation(lstd[:, cols(i)], ps[:, i, 0:CH], ACT.Sqrt, bias=m.eps[:, :]).then_inc(l_std, 1)
                    if NORM_AT <= n + 1 < NORM_AT + NN:
                        i = n + 1 - NORM_AT
                        z, g, k = fox_norms[i]
                        if i >= 2:
                            e.wait_ge(n_ms, i - 1)
                        e.activation(hsq[:, i % 2, :], m.Z[:, z, cols(k)], ACT.Square).then_inc(n_sq, 1)
                    if NORM_AT <= n < NORM_AT + NN:
                        i = n - NORM_AT
                        e.wait_ge(n_ms, i + 1)
                        if i >= 2:
                            e.wait_ge(n_norm, i - 1)
                        e.activation(hstd[:, i % 2, :], ps[:, i % 2, 0:CH], ACT.Sqrt, bias=m.eps[:, :]).then_inc(n_std, 1)

            @block.vector
            def _(e):
                def norm(t):
                    r, b = rows_of(t), t % 2
                    e.wait_ge(std_ready, t + 1)
                    e.reciprocal(rstd[0:r, b:b + 1], std[0:r, b:b + 1])
                    e.drain()
                    if t >= 2:
                        e.wait_ge(turned, t - 1)
                    e.tensor_scalar(hn[0:r, b, :], xt[0:r, b, :], rstd[0:r, b:b + 1], None, ALU.mult).then_inc(normed, 1)

                norm(0)
                for t in range(NT):
                    if t + 1 < NT:
                        norm(t + 1)
                    r = rows_of(t)
                    e.wait_ge(turned, t + 1)
                    for c in range(2):
                        g = m.g1[:, 4 * c:4 * c + 4].unsqueeze(2).broadcast_to([P, 4, r])
                        i = e.tensor_tensor(hT[:, 4 * c:4 * c + 4, t * P:t * P + r],
                                            ps_t[:, c, :].rearrange("p (k t) -> p k t", k=4)[:, :, 0:r], g, ALU.mult)
                    i.then_inc(ht_ready, 1)
                    if t == 0:
                        e.wait_ge(rows_mm, 1)
                        e.tensor_copy(tapT[:], ps_z[:, 0, 0:2 * TAPS].rearrange("p (c k) -> p c k", c=2))
                        for g in range(2):
                            for c in range(2):
                                i = e.tensor_copy(us[:, c, g * 4:g * 4 + 4, 0:NB1],
                                                  ps_z[:, 1, (2 * g + c) * 4 * NB1:(2 * g + c + 1) * 4 * NB1].rearrange("p (b t) -> p b t", t=NB1))
                        i.then_inc(rows_out, 1)
                e.wait_ge(sig, 1)
                e.wait_ge(z_out, SIG_AT)
                e.tensor_tensor(u, u, y, ALU.mult)
                e.drain().then_inc(u_ready, 1)
                for c in range(2):
                    e.tensor_copy(us[:, c, :, NB1:], u[:, c, SEQ:TOK].rearrange("p (b l) -> p b l", l=DEC_L))
                for k, c in tapped:
                    lag = NB1 - k
                    if lag == 0:
                        e.tensor_scalar(y[:, c, 0:SEQ], u[:, c, 0:SEQ], tapT[:, c, k:k + 1], m.cb[:, c:c + 1], ALU.mult, ALU.add)
                    else:
                        e.scalar_tensor_tensor(out=y[:, c, lag:SEQ], in0=u[:, c, 0:SEQ - lag], scalar=tapT[:, c, k:k + 1],
                                               in1=y[:, c, lag:SEQ], op0=ALU.mult, op1=ALU.add)
                    if c == 1:
                        e.drain()
                for c in range(2):
                    for l in range(DEC_L):
                        e.tensor_tensor(wtmp[:, l], us[:, c, :, l:l + TAPS], tapT[:, c, :].unsqueeze(1).broadcast_to([P, DEC_B, TAPS]), ALU.mult)
                    e.drain()
                    for l in range(DEC_L):
                        e.tensor_reduce(y[:, c, SEQ:TOK].rearrange("p (b l) -> p l b", l=DEC_L)[:, l], wtmp[:, l], AX.X, ALU.add)
                    e.drain()
                    i = e.tensor_scalar(y[:, c, SEQ:TOK], y[:, c, SEQ:TOK], m.cb[:, c:c + 1], None, ALU.add)
                i.then_inc(y_done, 1)
                e.wait_ge(rows_mm, 2)
                e.tensor_copy(ctail[:, 0, :], ps[0:NS, 3, 0:W])
                e.tensor_copy(ctail[:, 1, :], ps[0:NS, 3, W:2 * W]).then_inc(rows_out, 1)
                for n in range(NCH):
                    e.wait_ge(l_mean, n + 1)
                    for c in range(2):
                        i = e.tensor_tensor(y[:, c, cols(n)], y[:, c, cols(n)], ps[:, n, 0:CH], ALU.subtract)
                    i.then_inc(l_sub, 1)
                for n in range(NCH):
                    e.wait_ge(l_std, n + 1)
                    e.reciprocal(lstd[:, cols(n)], lstd[:, cols(n)])
                    e.drain()
                    for c in range(2):
                        i = e.scalar_tensor_tensor(out=y[:, c, cols(n)], in0=y[:, c, cols(n)], scalar=m.ln_g[:, c:c + 1], in1=lstd[:, cols(n)],
                                                   op0=ALU.mult, op1=ALU.mult)
                    i.then_inc(l_scaled, 1)
                for i, (z, g, k) in enumerate(fox_norms):
                    e.wait_ge(n_std, i + 1)
                    e.reciprocal(hstd[:, i % 2, :], hstd[:, i % 2, :])
                    e.drain()
                    e.scalar_tensor_tensor(out=m.Z[:, z, cols(k)], in0=m.Z[:, z, cols(k)], scalar=g,
                                           in1=hstd[:, i % 2, :], op0=ALU.mult, op1=ALU.mult).then_inc(n_norm, 1)

            @block.tensor
            def _(e):
                def turn(t):
                    r = rows_of(t)
                    e.wait_ge(normed, t + 1)
                    if t >= 1:
                        e.wait_ge(ht_ready, t)
                    for k in range(KC):
                        i = e.transpose(ps_t[:, k // 4, k % 4 * P:k % 4 * P + r], hn[0:r, t % 2, k:D:KC], m.ident[0:r, 0:r])
                    i.then_inc(turned, 1)

                turn(0)
                for c in range(2):
                    e.transpose(ps_z[:, 0, c * TAPS:(c + 1) * TAPS], m.tapw[:, c * P:c * P + P], m.ident[0:TAPS, 0:TAPS])
                e.wait_ge(cst_in, 32)
                for g in range(2):
                    for c in range(2):
                        i = e.transpose(ps_z[:, 1, (2 * g + c) * 4 * NB1:(2 * g + c + 1) * 4 * NB1], cst[:, g, c * P:c * P + P],
                                        m.ident[0:4 * NB1, 0:4 * NB1])
                i.then_inc(rows_mm, 1)
                e.wait_ge(wv_in, 32)
                for t in range(NT):
                    if t + 1 < NT:
                        turn(t + 1)
                    r = rows_of(t)
                    e.wait_ge(ht_ready, t + 1)
                    if t >= 2:
                        e.wait_ge(v_out, t - 1)
                    for k in range(KC):
                        i = e.matmul(ps_v[0:r, t % 2, :], hT[:, k, t * P:t * P + r], wv[:, k, :],
                                     start=(k == 0), stop=(k == KC - 1))
                    i.then_inc(v_done, 1)
                e.wait_ge(rows_out, 1)
                for n in range(ALL):
                    f, c, b = n // NCH, n % NCH, n % 4
                    if n == TAIL_AT:
                        e.wait_ge(u_ready, 1)
                        e.wait_ge(v_out, NT)
                        for i in range(2):
                            e.transpose(ps[0:NS, 3, i * P:i * P + P], u[:, i, SEQ - NS:SEQ], m.ident[:])
                            mm = e.transpose(ps[0:NS, 3, W + i * P:W + i * P + P], u[:, i, SEQ:TOK], m.ident[:])
                        mm.then_inc(rows_mm, 1)
                    if n == MEAN_AT:
                        e.wait_ge(y_done, 1)
                        for i in range(NCH):
                            for j in range(2):
                                mm = e.matmul(ps[:, i, 0:CH], m.chmean[:], y[:, j, cols(i)], start=(j == 0), stop=(j == 1))
                            mm.then_inc(l_mean, 1)
                    if n == VAR_AT:
                        for i in range(NCH):
                            e.wait_ge(l_sq, i + 1)
                            for j in range(2):
                                mm = e.matmul(ps[:, i, 0:CH], m.chmean[:], ysq[:, j, cols(i)], start=(j == 0), stop=(j == 1))
                            mm.then_inc(l_var, 1)
                    if NORM_AT <= n < NORM_AT + NN:
                        i = n - NORM_AT
                        e.wait_ge(n_sq, i + 1)
                        if i >= 2:
                            e.wait_ge(n_std, i - 1)
                        e.matmul(ps[:, i % 2, 0:CH], m.headmean[:], hsq[:, i % 2, :], start=True, stop=True).then_inc(n_ms, 1)
                    if f < 2 * NZ:
                        g = n // PER
                        if n % PER == 0:
                            e.wait_ge(wz_in[g % 2], 16 * (g // 2 + 1))
                        lhs, rows = wz[:, g % 2, :, f % 2 * P:f % 2 * P + P], P
                    else:
                        if c == 0:
                            e.wait_ge(wsm_in, 32)
                        lhs, rows = wsm, FROW + H
                    if n >= 4:
                        e.wait_ge(z_out, n - 3)
                    for k in range(KC):
                        i = e.matmul(ps_z[0:rows, b, 0:CH], lhs[:, k, :], hT[:, k, c * CH:(c + 1) * CH],
                                     start=(k == 0), stop=(k == KC - 1))
                    i.then_inc(z_done, 1)


def log_sigmoid_act(e, x, t):
    e.activation(t, x, ACT.Abs)
    e.drain()
    e.activation(t, t, ACT.Exp, scale=-1.0)
    e.drain()
    return e.activation(t, t, ACT.Ln, bias=1.0)


def gla_pool_norms(nc, m):
    ctx = ExitStack()
    sb = lambda name, shape: ctx.enter_context(nc.sbuf_tensor(name, shape, F32))
    sem = lambda name: ctx.enter_context(nc.semaphore(name))
    NC = NT - 1 + DEC_B
    QE, KE = m.Z[:, ZQ:ZQ + 2, :], m.Z[:, ZK:ZK + 2, :]
    ps = m.ps
    with ctx:
        la, bsum, tmp = sb("la", [P, 2, TOK]), sb("bsum", [P, 2, TOK]), sb("tmp", [P, 2, TOK])
        mid, last, dlm = sb("mid", [P, 2, NC]), sb("last", [P, 2, NC]), sb("dlm", [P, 2, NC])
        e_mid, e_last, e_dlm = sb("e_mid", [P, 2, NC]), sb("e_last", [P, 2, NC]), sb("e_dlm", [P, 2, NC])
        keT = sb("keT", [P, NT, W])
        at = sb("at", [P, 2, 2, 2, P])
        S, Ssc, Stmp = sb("S", [P, 2, P]), sb("Ssc", [P, 2, P]), sb("Stmp", [P, 2, 4, HD])
        SS = sb("SS", [P, 2, DEC_B, P])
        sq, std, rec = sb("gla_sq", [P, 2, CH]), sb("gla_std", [P, 2, CH]), sb("gla_rec", [P, 2, CH])
        tailT = sb("tailT", [2 * NS, W])
        kout = sb("kout", [P, 2, W])
        pxs, pas, pbs = (sb(n, [P, 2, DEC_B, PMAX + DEC_L]) for n in ("pxs", "pas", "pbs"))
        pst = sb("pst", [DEC_B * (PMAX - 1), W])
        rcount = sb("rcount", [P, 2, PMAX])
        fx = m.ZS
        ft = m.CF
        SSsc = bsum[:].rearrange("p c t -> p (c t)")[:, 0:2 * DEC_B * P].rearrange("p (c b e) -> p c b e", c=2, b=DEC_B)
        vmask = tmp[:].rearrange("p c t -> p (c t)")[0:NS, 0:DEC_B * W].rearrange("p (b e) -> p b e", b=DEC_B)
        pa, pb, px = (m.mixT[:, c:c + 2, 0:PMAX + SEQ] for c in (2, 4, 6))

        n_sq, n_ms, n_std, n_norm = sem("n_sq"), sem("n_ms"), sem("n_std"), sem("n_norm")
        la_mm, la_x, la_t, la_d, la_e, la_s, qk_ready = (sem(n) for n in ("la_mm", "la_x", "la_t", "la_d", "la_e", "la_s", "qk_ready"))
        f_x, f_t, f_c = sem("f_x"), sem("f_t"), sem("f_c")
        f_mm, f_out = sem("f_mm"), sem("f_out")
        kt_mm, kt_out, k_sent = sem("kt_mm"), sem("kt_out"), [sem(f"k_sent{i}") for i in range(2)]
        ket_mm, ket_out = sem("ket_mm"), sem("ket_out")
        zeroed, st_in, pst_in = sem("zeroed"), sem("st_in"), sem("pst_in")
        a_mm, a_out, o_mm, o_out, s_mm, s_out, s_sc = (sem(n) for n in ("a_mm", "a_out", "o_mm", "o_out", "s_mm", "s_out", "s_sc"))
        ss_sc, vm_ready = sem("ss_sc"), sem("vm_ready")
        silu, stored = sem("silu"), sem("stored")
        pst_mm, pst_out, p_d, p_mm, p_out = (sem(n) for n in ("pst_mm", "pst_out", "p_d", "p_mm", "p_out"))
        pt_mm, pt_out = sem("pt_mm"), sem("pt_out")

        def tiles(x):
            return (x[:, :, 0:SEQ].rearrange("p c (n t) -> p c n t", t=P),
                    x[:, :, SEQ:TOK].rearrange("p c (n t) -> p c n t", t=DEC_L))

        GLA_NORMS = [(ZQ, m.gla_g[:, 0:1]), (ZQ + 1, m.gla_g[:, 1:2])]
        norm_steps = [(z, g, n) for z, g in GLA_NORMS for n in range(NCH)]
        cols = lambda n: slice(n * CH, (n + 1) * CH)

        def norm_square(e, i):
            z, g, n = norm_steps[i]
            if i >= 2:
                e.wait_ge(n_ms, i - 1)
            e.activation(sq[:, i % 2, :], m.Z[:, z, cols(n)], ACT.Square).then_inc(n_sq, 1)

        def norm_root(e, i):
            e.wait_ge(n_ms, i + 1)
            if i >= 2:
                e.wait_ge(n_norm, i - 1)
            e.activation(std[:, i % 2, :], ps[:, i % 2, 0:CH], ACT.Sqrt, bias=m.eps[:, :]).then_inc(n_std, 1)

        def norm_mean(e, i):
            e.wait_ge(n_sq, i + 1)
            if i >= 2:
                e.wait_ge(n_std, i - 1)
            e.matmul(ps[:, i % 2, 0:CH], m.headmean[:], sq[:, i % 2, :], start=True, stop=True).then_inc(n_ms, 1)

        def norm_scale(e, i):
            z, g, n = norm_steps[i]
            e.wait_ge(n_std, i + 1)
            e.reciprocal(rec[:, i % 2, :], std[:, i % 2, :])
            e.drain()
            e.scalar_tensor_tensor(out=m.Z[:, z, cols(n)], in0=m.Z[:, z, cols(n)], scalar=g,
                                   in1=rec[:, i % 2, :], op0=ALU.mult, op1=ALU.mult).then_inc(n_norm, 1)

        with nc.Block() as block:

            @block.sync
            def _(e):
                e.wait_ge(zeroed, 1)
                for h in range(H):
                    o = HD * (h % 2)
                    e.dma_start(SS[o:o + HD, h // 2, :, o:o + HD],
                                m.state_gla[0, :, h].rearrange("b d e -> d b e")).then_inc(st_in, 16)
                e.dma_start(pst[:], m.state_pool[0].rearrange("b t c -> (b t) c")).then_inc(pst_in, 16)
                e.dma_start(m.conv_sample[0, :, 0:TAPS - 1 - DEC_L, :], m.state_conv[0, :, DEC_L:TAPS - 1, :]).then_inc(stored, 16)
                e.dma_start(m.pool_sample[0, :, 0:PMAX - 1 - DEC_L, :], m.state_pool[0, :, DEC_L:PMAX - 1, :]).then_inc(stored, 16)
                n = 2
                e.wait_ge(f_out, 1)
                e.dma_start(m.logf_prompt[0, 0].rearrange("(t p) h -> p t h", p=P), m.lft[:, 0:NT - 1, 0:H]).then_inc(stored, 16)
                e.dma_start(m.logf_sample[0].rearrange("b l h -> (b l) h"), m.lft[0:NS, NT - 1, 0:H]).then_inc(stored, 16)
                n += 2
                for t in range(NT):
                    r = rows_of(t)
                    e.wait_ge(kt_out, t + 1)
                    to = m.k_prompt[0, 0, t * P:(t + 1) * P] if t < NT - 1 else m.k_sample[0].rearrange("b l h d -> (b l) h d")
                    e.dma_start(to.rearrange("p h d -> p (h d)"), kout[0:r, t % 2, :]).then_inc(k_sent[t % 2], 16)
                e.wait_ge(s_out, NT - 1)
                for h in range(H):
                    o = HD * (h % 2)
                    e.dma_start(m.gla_prompt[0, 0, h], S[o:o + HD, h // 2, o:o + HD]).then_inc(stored, 16)
                e.wait_ge(s_out, NT)
                for h in range(H):
                    o = HD * (h % 2)
                    e.dma_start(m.gla_sample[0, :, h].rearrange("b d e -> d b e"), SS[o:o + HD, h // 2, :, o:o + HD]).then_inc(stored, 16)
                e.wait_ge(pt_out, 1)
                e.dma_start(m.pool_prompt[0, 0], tailT[NS - PMAX + 1:NS, :]).then_inc(stored, 16)
                for b in range(DEC_B):
                    e.dma_start(m.pool_sample[0, b, PMAX - 1 - DEC_L:PMAX - 1, :],
                                tailT[NS + DEC_L * b:NS + DEC_L * b + DEC_L, :]).then_inc(stored, 16)
                n += 2 * H + 1 + DEC_B
                e.wait_ge(stored, 16 * n)
                for i in range(2):
                    e.wait_ge(k_sent[i], 16 * ((NT + 1 - i) // 2))

            @block.gpsimd
            def _(e):
                e.memset(SS[:], 0.0)
                e.memset(at[:], 0.0)
                e.memset(S[:], 0.0)
                e.drain().then_inc(zeroed, 1)
                e.memset(px[:, :, 0:PMAX], 0.0)
                e.memset(pxs[:, :, :, 0:1], 0.0)
                e.tensor_copy(px[:, :, PMAX:], m.Z[:, ZPU:ZPU + 2, 0:SEQ])
                e.tensor_copy(pxs[:, :, :, PMAX:], m.Z[:, ZPU:ZPU + 2, SEQ:TOK].rearrange("p c (b l) -> p c b l", l=DEC_L))
                e.wait_ge(pst_out, 1)
                e.drain()
                N, NB = PMAX + SEQ, PMAX + DEC_L
                for lo, c0, w, src, dst, ssrc, sdst in ((0, 0, 1, px, pa, pxs, pas), (64, 0, 2, pa, pb, pas, pbs),
                                                        (0, 1, 2, pa, pb, pas, pbs), (0, 1, 4, pb, pa, pbs, pas),
                                                        (64, 1, 8, pa, pb, pas, pbs)):
                    c1 = 2 if w == 1 else c0 + 1
                    j = 2 * w - 1
                    e.tensor_tensor(dst[lo:P, c0:c1, j:N], src[lo:P, c0:c1, j:N], src[lo:P, c0:c1, j - w:N - w], ALU.add)
                    e.drain()
                    e.tensor_tensor(sdst[lo:P, c0:c1, :, j:NB], ssrc[lo:P, c0:c1, :, j:NB],
                                    ssrc[lo:P, c0:c1, :, j - w:NB - w], ALU.add)
                    e.drain()
                e.drain().then_inc(p_d, 1)

            @block.scalar
            def _(e):
                e.wait_ge(la_x, 6)
                log_sigmoid_act(e, la[:], tmp[:]).then_inc(la_t, 1)
                e.wait_ge(f_x, 1)
                log_sigmoid_act(e, fx[FROW:FROW + H, :], ft[FROW:FROW + H, :]).then_inc(f_t, 1)
                e.wait_ge(la_s, 1)
                e.activation(e_mid[:], mid[:], ACT.Exp, scale=1.0 / TAU)
                e.activation(e_last[:], last[:], ACT.Exp, scale=1.0 / TAU)
                e.activation(e_dlm[:], dlm[:], ACT.Exp, scale=1.0 / TAU).then_inc(la_e, 1)
                e.wait_ge(la_d, 1)
                e.activation(la[:], tmp[:], ACT.Exp, scale=1.0 / TAU).then_inc(la_e, 1)
                e.drain()
                e.activation(tmp[:], tmp[:], ACT.Exp, scale=-1.0 / TAU).then_inc(la_e, 1)
                for t in range(NT):
                    e.wait_ge(ket_mm, t + 1)
                    e.copy(keT[0:rows_of(t), t, :], ps[0:rows_of(t), 4 + t % 2, 0:W]).then_inc(ket_out, 1)
                for t in range(NT):
                    r = rows_of(t)
                    e.wait_ge(o_mm, t + 1)
                    e.copy(QE[:, :, t * P:t * P + r], ps[:, 4 + t % 2, 0:2 * P].rearrange("p (c t) -> p c t", c=2)[:, :, 0:r]).then_inc(o_out, 1)
                e.drain()
                for i in range(len(norm_steps) + 1):
                    if i < len(norm_steps):
                        norm_square(e, i)
                    if i:
                        norm_root(e, i - 1)
                e.activation(m.Z[:, ZG:ZG + 2, :], m.Z[:, ZG:ZG + 2, :], ACT.Silu).then_inc(silu, 1)
                for t in range(NT):
                    e.wait_ge(kt_mm, t + 1)
                    if t >= 2:
                        e.wait_ge(k_sent[t % 2], 16 * (t // 2))
                    e.copy(kout[0:rows_of(t), t % 2, :], ps[0:rows_of(t), t % 2, 0:W]).then_inc(kt_out, 1)

            @block.vector
            def _(e):
                for n in range(2 * NCH):
                    c = n // NCH
                    e.wait_ge(la_mm, n + 1)
                    e.tensor_scalar(la[:, c, cols(n % NCH)], ps[:, 2 + n % 2, 0:CH], m.gla_b[:, c:c + 1], None, ALU.add).then_inc(la_x, 1)
                e.tensor_scalar(fx[FROW:FROW + H, :], m.ZS[FROW:FROW + H, :], m.fb[FROW:FROW + H, :], None, ALU.add).then_inc(f_x, 1)
                e.wait_ge(pst_mm, 1)
                for c in range(2):
                    i = e.tensor_copy(pxs[:, c, :, 1:PMAX], ps[:, 7, c * P:c * P + DEC_B * (PMAX - 1)].rearrange("p (b t) -> p b t", b=DEC_B))
                i.then_inc(pst_out, 1)
                e.wait_ge(la_t, 1)
                e.scalar_tensor_tensor(out=la[:], in0=la[:], scalar=0.0, in1=tmp[:], op0=ALU.min, op1=ALU.subtract)
                e.drain()
                for c in range(2):
                    e.tensor_tensor_scan(bsum[:, c, :], m.reset[:], la[:, c, :], 0.0, ALU.mult, ALU.add)
                e.drain()
                bp, bs = tiles(bsum)
                tp, ts_ = tiles(tmp)
                for src, n0, n1, im, il in ((bp, 0, NT - 1, P // 2 - 1, P - 1), (bs, NT - 1, NC, 1, DEC_L - 1)):
                    e.tensor_copy(mid[:, :, n0:n1], src[:, :, :, im])
                    e.tensor_copy(last[:, :, n0:n1], src[:, :, :, il])
                e.drain()
                e.tensor_tensor(dlm[:], last[:], mid[:], ALU.subtract).then_inc(la_s, 1)
                for c in range(2):
                    e.tensor_tensor(tp[:, c], bp[:, c], mid[:, c, 0:NT - 1].unsqueeze(2).broadcast_to([P, NT - 1, P]), ALU.subtract)
                    i = e.tensor_tensor(ts_[:, c], bs[:, c], mid[:, c, NT - 1:NC].unsqueeze(2).broadcast_to([P, DEC_B, DEC_L]), ALU.subtract)
                i.then_inc(la_d, 1)
                F4 = slice(FROW, FROW + H)
                e.wait_ge(f_t, 1)
                e.scalar_tensor_tensor(out=fx[F4, :], in0=fx[F4, :], scalar=0.0, in1=ft[F4, :], op0=ALU.min, op1=ALU.subtract)
                e.drain()
                e.tensor_tensor_scan(m.CF[F4, 0:SEQ], m.ones[F4, 0:1].broadcast_to([H, SEQ]), fx[F4, 0:SEQ], 0.0, ALU.mult, ALU.add).then_inc(f_c, 1)
                e.wait_ge(la_e, 3)
                e.scalar_tensor_tensor(out=QE, in0=QE, scalar=HD ** -0.5, in1=la[:], op0=ALU.mult, op1=ALU.mult)
                e.tensor_tensor(KE, KE, tmp[:], ALU.mult).then_inc(qk_ready, 1)
                e.wait_ge(zeroed, 1)
                e.wait_ge(f_mm, 1)
                e.tensor_copy(m.lft[:, 0:NT - 1, :], ps[:, 6, 0:8 * NT].rearrange("p (t c) -> p t c", c=8)[:, 0:NT - 1, :])
                e.tensor_copy(m.lft[0:NS, NT - 1, 0:H], ps[0:NS, 6, 8 * (NT - 1):8 * (NT - 1) + H]).then_inc(f_out, 1)

                def mask_scores(t):
                    r, b = rows_of(t), t % 2
                    mask = (m.causal if t < NT - 1 else m.sampmask)[0:r, 0:r].bitcast(I32)
                    e.wait_ge(a_mm, t + 1)
                    if t >= 2:
                        e.wait_ge(o_mm, t - 1)
                    if t == NT - 1:
                        e.memset(at[0:r, b], 0.0)
                        e.drain()
                    for hb in range(2):
                        i = e.copy_predicated(at[0:r, b, hb, :, 0:r], mask.unsqueeze(1).broadcast_to([r, 2, r]),
                                              ps[0:r, 2 * b + hb, 0:2 * P].rearrange("p (h t) -> p h t", h=2)[:, :, 0:r])
                    i.then_inc(a_out, 1)

                mask_scores(0)
                for t in range(NT - 1):
                    if t >= 1:
                        e.wait_ge(o_mm, t)
                    for c in range(2):
                        i = e.tensor_scalar(Ssc[:, c, :], S[:, c, :], e_mid[:, c, t:t + 1], None, ALU.mult)
                    i.then_inc(s_sc, 1)
                    mask_scores(t + 1)
                    e.wait_ge(s_mm, t + 1)
                    for c in range(2):
                        for o in (0, HD):
                            e.tensor_scalar(Stmp[o:o + HD, c, 0, :], ps[o:o + HD, 6, c * P + o:c * P + o + HD],
                                            e_dlm[o:o + HD, c, t:t + 1], None, ALU.mult)
                    e.drain()
                    for c in range(2):
                        for o in (0, HD):
                            i = e.scalar_tensor_tensor(out=S[o:o + HD, c, o:o + HD], in0=S[o:o + HD, c, o:o + HD],
                                                       scalar=e_last[o:o + HD, c, t:t + 1], in1=Stmp[o:o + HD, c, 0, :],
                                                       op0=ALU.mult, op1=ALU.add)
                    i.then_inc(s_out, 1)
                    e.drain()
                e.wait_ge(st_in, 16 * H)
                for c in range(2):
                    i = e.tensor_tensor(SSsc[:, c], SS[:, c], e_mid[:, c, NT - 1:NC].unsqueeze(2).broadcast_to([P, DEC_B, P]), ALU.mult)
                i.then_inc(ss_sc, 1)
                for b in range(DEC_B):
                    i = e.tensor_scalar(vmask[:, b, :], m.V[0:NS, NT - 1, 0:W], m.sampmask[:, DEC_L * b + DEC_L - 1:DEC_L * b + DEC_L], None, ALU.mult)
                i.then_inc(vm_ready, 1)
                for g in range(4):
                    c, b0 = g // 2, g % 2 * 4
                    e.wait_ge(s_mm, NT - 1 + g + 1)
                    for o in (0, HD):
                        view = SS[o:o + HD, c, b0:b0 + 4, o:o + HD]
                        pv = ps[o:o + HD, 6 + g % 2, :].rearrange("p (b e) -> p b e", b=4)[:, :, o:o + HD]
                        bc = lambda x: x[o:o + HD, c, NT - 1 + b0:NT - 1 + b0 + 4].unsqueeze(2).broadcast_to([HD, 4, HD])
                        e.tensor_tensor(Stmp[o:o + HD, 0], pv, bc(e_dlm), ALU.mult)
                        e.tensor_tensor(view, view, bc(e_last), ALU.mult)
                        e.drain()
                        i = e.tensor_tensor(view, view, Stmp[o:o + HD, 0], ALU.add)
                        e.drain()
                    e.engine_nop().then_inc(s_out if g == 3 else vm_ready, 1)
                for i in range(len(norm_steps)):
                    norm_scale(e, i)
                e.wait_ge(silu, 1)
                e.drain()
                e.tensor_tensor(m.mixT[:, 0:2, :], QE, m.Z[:, ZG:ZG + 2, :], ALU.mult)
                for g, w in enumerate(WINDOWS):
                    o, c = HD * (g % 2), g // 2
                    e.tensor_scalar(rcount[o:o + HD, c, :], m.count[o:o + HD, :], float(w), None, ALU.min)
                e.drain()
                e.reciprocal(rcount[:], rcount[:])
                e.drain()
                e.wait_ge(p_d, 1)
                for g, w in enumerate(WINDOWS):
                    o, c = HD * (g % 2), g // 2
                    R = slice(o, o + HD)
                    src, ssrc = ((pa, pas), (pb, pbs))[g % 2]
                    e.scalar_tensor_tensor(out=pa[R, c, 2 * PMAX:], in0=src[R, c, 2 * PMAX:], scalar=1.0 / w,
                                           in1=px[R, c, 2 * PMAX:], op0=ALU.mult, op1=ALU.subtract)
                    e.tensor_tensor(src[R, c, PMAX:2 * PMAX], src[R, c, PMAX:2 * PMAX], rcount[R, c, :], ALU.mult)
                    e.scalar_tensor_tensor(out=pxs[R, c, :, PMAX:], in0=ssrc[R, c, :, PMAX:], scalar=1.0 / w,
                                           in1=pxs[R, c, :, PMAX:], op0=ALU.mult, op1=ALU.subtract)
                    e.drain()
                    i = e.tensor_tensor(pa[R, c, PMAX:2 * PMAX], src[R, c, PMAX:2 * PMAX], px[R, c, PMAX:2 * PMAX], ALU.subtract)
                i.then_inc(p_out, 1)
                for n in range(6):
                    c, k = n // 3, n % 3
                    w0, w1 = ((0, 512), (512, SEQ), (SEQ, TOK))[k]
                    e.wait_ge(p_mm, n + 1)
                    e.tensor_scalar(m.mixT[:, 6 + c, w0:w1], ps[:, n % 4, 0:w1 - w0], m.pscale[:, c:c + 1], None, ALU.mult).then_inc(p_out, 1)
                e.wait_ge(pt_mm, 1)
                e.tensor_copy(tailT[:], ps[0:2 * NS, 4, 0:W]).then_inc(pt_out, 1)

            @block.tensor
            def _(e):
                for n in range(2 * NCH):
                    if n >= 2:
                        e.wait_ge(la_x, n - 1)
                    e.matmul(ps[:, 2 + n % 2, 0:CH], m.wa2[:, n // NCH * P:n // NCH * P + P], m.ZS[0:RANK, cols(n % NCH)],
                             start=True, stop=True).then_inc(la_mm, 1)
                e.wait_ge(pst_in, 16)
                for c in range(2):
                    i = e.transpose(ps[:, 7, c * P:c * P + DEC_B * (PMAX - 1)], pst[:, c * P:c * P + P],
                                    m.ident[0:DEC_B * (PMAX - 1), 0:DEC_B * (PMAX - 1)])
                i.then_inc(pst_mm, 1)
                e.wait_ge(f_c, 1)
                F4 = slice(FROW, FROW + H)
                for t in range(NT):
                    r = rows_of(t)
                    i = e.transpose(ps[0:r, 6, 8 * t:8 * t + H], fx[F4, t * P:t * P + r], m.ident[F4, F4])
                    if t < NT - 1:
                        i = e.transpose(ps[0:r, 6, 8 * t + H:8 * t + 2 * H], m.CF[F4, t * P:t * P + r], m.ident[F4, F4])
                i.then_inc(f_mm, 1)
                e.wait_ge(qk_ready, 1)
                for t in range(NT):
                    r = rows_of(t)
                    if t >= 2:
                        e.wait_ge(ket_out, t - 1)
                    for c in range(2):
                        i = e.transpose(ps[0:r, 4 + t % 2, c * P:c * P + P], KE[:, c, t * P:t * P + r], m.ident[:])
                    i.then_inc(ket_mm, 1)
                e.wait_ge(ket_out, NT)
                e.wait_ge(la_x, 6)
                e.wait_ge(f_out, 1)

                def scores(t):
                    r = rows_of(t)
                    if t >= 2:
                        e.wait_ge(a_out, t - 1)
                    for h in range(H):
                        o, c = HD * (h % 2), h // 2
                        i = e.matmul(ps[0:r, 2 * (t % 2) + h % 2, c * P:c * P + r], KE[o:o + HD, c, t * P:t * P + r],
                                     QE[o:o + HD, c, t * P:t * P + r], start=True, stop=True)
                    i.then_inc(a_mm, 1)

                scores(0)
                for t in range(NT):
                    r, b, last_t = rows_of(t), t % 2, t == NT - 1
                    if not last_t:
                        scores(t + 1)
                        if t >= 1:
                            e.wait_ge(s_out, t)
                        for c in range(2):
                            i = e.matmul(ps[:, 6, c * P:c * P + P], keT[:, t, c * P:c * P + P], m.V[:, t, c * P:c * P + P],
                                         start=(c == 0), stop=(c == 1), skip_group_check=True)
                        i.then_inc(s_mm, 1)
                        e.wait_ge(s_sc, t + 1)
                    else:
                        e.wait_ge(ss_sc, 1)
                    if t >= 2:
                        e.wait_ge(o_out, t - 1)
                    for c in range(2):
                        if not last_t:
                            e.matmul(ps[:, 4 + b, c * P:c * P + P], Ssc[:, c, :], QE[:, c, t * P:t * P + P],
                                     start=(c == 0), stop=False, skip_group_check=True)
                        else:
                            for s in range(DEC_B):
                                o = c * P + DEC_L * s
                                e.matmul(ps[:, 4 + b, o:o + DEC_L], SSsc[:, c, s, :],
                                         QE[:, c, SEQ + DEC_L * s:SEQ + DEC_L * s + DEC_L],
                                         start=(c == 0 and s == 0), stop=False, skip_group_check=True)
                    e.wait_ge(a_out, t + 1)
                    for h in range(H):
                        o, c = HD * (h % 2), h // 2
                        i = e.matmul(ps[o:o + HD, 4 + b, c * P:c * P + r], m.V[0:r, t, h * HD:h * HD + HD],
                                     at[0:r, b, h % 2, c, 0:r], start=False, stop=True, skip_group_check=True)
                    i.then_inc(o_mm, 1)
                e.wait_ge(vm_ready, 1)
                e.wait_ge(pst_out, 1)
                e.wait_ge(s_out, NT - 1)
                for g in range(4):
                    c, b0 = g // 2, g % 2 * 4
                    if g >= 2:
                        e.wait_ge(vm_ready, g)
                    e.matmul(ps[:, 6 + g % 2, :].rearrange("p (b e) -> p b e", b=4), keT[0:NS, NT - 1, c * P:c * P + P],
                             vmask[:, b0:b0 + 4, c * P:c * P + P], start=True, stop=True).then_inc(s_mm, 1)
                e.wait_ge(a_out, NT)
                for i in range(len(norm_steps)):
                    norm_mean(e, i)
                e.wait_ge(n_std, len(norm_steps))
                for t in range(NT):
                    r = rows_of(t)
                    if t >= 2:
                        e.wait_ge(kt_out, t - 1)
                    for c in range(2):
                        i = e.transpose(ps[0:r, t % 2, c * P:c * P + P], m.Z[:, ZFK + c, t * P:t * P + r], m.ident[:])
                    i.then_inc(kt_mm, 1)
                e.wait_ge(o_out, NT)
                for c in range(2):
                    i = e.transpose(ps[0:2 * NS, 4, c * P:c * P + P], m.Z[:, ZPU + c, SEQ - NS:TOK], m.ident[:])
                i.then_inc(pt_mm, 1)
                e.wait_ge(kt_out, NT)
                e.wait_ge(p_out, 1)
                for n in range(6):
                    c, k = n // 3, n % 3
                    src, w = ((pa[:, c, PMAX:PMAX + 512], 512), (pa[:, c, PMAX + 512:], 512), (pxs[:, c, :, PMAX:], NS))[k]
                    to = ps[:, n % 4, 0:w]
                    if k == 2:
                        to = to.rearrange("p (b l) -> p b l", l=DEC_L)
                    if n >= 4:
                        e.wait_ge(p_out, 1 + n - 3)
                    e.matmul(to, m.poolw[:, c, :], src, start=True, stop=True).then_inc(p_mm, 1)


def fox(nc, m):
    ctx = ExitStack()
    sb = lambda name, shape: ctx.enter_context(nc.sbuf_tensor(name, shape, F32))
    sem = lambda name: ctx.enter_context(nc.semaphore(name))
    ps = m.ps
    R = DEC_L * H
    QG = 4
    NQ = NPG // QG
    F4 = slice(FROW, FROW + H)
    with ctx:
        ck = m.Z[:, ZQ:ZQ + 4, 0:SEQ]
        sc = [m.Z[:, z, 0:SEQ] for z in (ZG, ZG + 1, ZCA, ZCA + 1)]
        pT = m.Z[:, ZPU:ZPU + 2, 0:SEQ].rearrange("p b (k q) -> p b k q", q=P)
        kpg = sb("kpg", [P, 4, QG, W])
        vpg = sb("vpg", [P, NPG, W])
        kT = sb("kT", [P, 2, 2, QG * PAGE])
        lfp, cpg = sb("lfp", [P, PAGE * H]), sb("cpg", [P, H, PAGE])
        tot, carry = sb("page_totals", [P, H]), sb("page_carry", [P, H])
        cnew = sb("cnew", [NS, H])
        cdiag = sb("cdiag", [NS, NS, H])
        cq = sb("cq", [P, DEC_B, DEC_L, H])
        bias = sb("bias", [P, DEC_B, NPG, DEC_L, H])
        snew = sb("snew", [NS, DEC_B, DEC_L, H])
        nneg = sb("nneg", [NS, NS])
        qbd = sb("qbd", [P, 2, DEC_B, DEC_L, H])
        S = sb("S_fox", [P, 2, NPG + 1, R])
        cmax, csum = sb("cmax", [P, R]), sb("csum", [P, R])
        rmax, maxdiag = sb("rmax", [R, 1]), sb("maxdiag", [R, R])
        sinv, orow = sb("sinv", [R, 1]), sb("orow", [R, W])
        nmax, rsum, rinv, pmax = sb("nmax", [P, 4]), sb("rsum", [P, 4]), sb("rinv", [P, 4]), sb("pmax", [P, 4])
        ot = sb("ot", [P, 2, P])
        srow = sb("srow", [R, 2, QG * PAGE])
        b_q, b_s = ps[0:R, 7, :], ps[:, 7, 0:QG * R]
        b_max, b_bc = ps[0:R, 7, 256:384], ps[:, 7, 384:400]
        b_pv, b_sum, b_ot = ps[0:R, 7, 0:W], ps[0:R, 7, W:W + 1], ps[:, 7, 256:256 + 2 * R]

        lf_in, page_sums, sums_mm = (sem(n) for n in ("lf_in", "page_sums", "sums_mm"))
        ck_mm, ck_out, qbd_ready = (sem(n) for n in ("ck_mm", "ck_out", "qbd_ready"))
        p_sc, p_read, p_so, p_exp, p_tr, p_to, p_pv, p_oo = (sem("fox_" + n) for n in ("sc", "read", "so", "exp", "tr", "to", "pv", "oo"))
        k_in, v_in = [sem(f"k_in{i}") for i in range(4)], sem("v_in")
        k_tr, k_o0, k_o1 = sem("k_tr"), sem("k_o0"), sem("k_o1")
        s_q, s_qo, s_qt, s_ev, s_max, s_row, s_shift, s_exp, s_col, s_pv, s_div, s_small, s_out = (
            sem("samp_" + n) for n in ("q", "qo", "qt", "ev", "max", "row", "shift", "exp", "col", "pv", "div", "small", "out"))

        steps = [(i, h) for i in range(NT - 1) for h in range(H)]
        N = len(steps)
        assert N == DEC_B * NQ
        LAST = N + 6
        groups = lambda n: steps[n][0] // 4 + 1

        order23 = []
        for n in range(LAST):
            if 3 <= n < N + 3 and steps[n - 3][1] % 2:
                order23.append(("o", n - 3))
            if 2 <= n < N + 2:
                order23 += [("p", n - 2, g) for g in range(groups(n - 2))]
        turn23 = {k: i + 1 for i, k in enumerate(order23)}
        last_of = lambda n: turn23[("p", n, groups(n) - 1)]

        def sample_at(n, phase):
            b, rest = divmod(n - NQ - 1 - phase, NQ)
            return b if rest == 0 and 0 <= b < DEC_B else None

        with nc.Block() as block:

            @block.sync
            def _(e):
                pages = []

                def load_k(b):
                    for j in range(NQ):
                        for g in range(QG):
                            k = b * NPG + QG * j + g
                            pages.append(e.value_load(m.pages[0:1, k:k + 1], min_val=0, max_val=POOLPG - 1))
                            if g == 0 and b:
                                e.wait_ge(k_tr, NQ * b + j - 3)
                            e.dma_start(kpg[:, j, g, :].unsqueeze(1),
                                        m.cache_k[0, ds(pages[k], 1)].rearrange("a t h d -> t a (h d)")).then_inc(k_in[j], 16)

                def load_v(b):
                    if b:
                        e.wait_ge(s_pv, b)
                    for g in range(NPG):
                        e.dma_start(vpg[:, g, :].unsqueeze(1),
                                    m.cache_v[0, ds(pages[b * NPG + g], 1)].rearrange("a t h d -> t a (h d)")).then_inc(v_in, 16)

                load_k(0)
                for b in range(1, DEC_B):
                    load_k(b)
                    load_v(b - 1)
                load_v(DEC_B - 1)

            @block.gpsimd
            def _(e):
                e.indirect_dma_start(out=lfp[:], out_offset=None,
                                     in_=m.cache_logf[0].rearrange("n t h -> n (t h)"),
                                     in_offset=bass.IndirectOffsetOnAxis(ap=m.pages_col[:, 0:1], axis=0)).then_inc(lf_in, 16)
                e.memset(S[:], NEG)
                e.memset(qbd[:], 0.0)
                e.drain()
                for h in range(H):
                    o, c = HD * (h % 2), h // 2
                    e.tensor_copy(qbd[o:o + HD, c, :, :, h], m.Z[o:o + HD, ZFQ + c, SEQ:TOK].rearrange("p (b l) -> p b l", l=DEC_L))
                    e.drain()
                e.drain().then_inc(qbd_ready, 1)

            @block.scalar
            def _(e):
                for n in range(2 * H):
                    e.wait_ge(ck_mm, n + 1)
                    e.copy(ck[:, n // 2, n % 2 * 512:n % 2 * 512 + 512], ps[:, n % 4, :]).then_inc(ck_out, 1)
                for n in range(2):
                    e.activation(m.mixT[:, 4 + n, :], m.Z[:, ZCB + n, :], ACT.Silu, bias=m.ln_b[:, n:n + 1])
                for n in range(LAST):
                    if n < N:
                        e.wait_ge(k_tr, n + 1)
                        if n >= 2:
                            e.wait_ge(s_q, n - 1)
                        e.copy(kT[:, n % 2, 0, :], ps[:, 5, :]).then_inc(k_o0, 1)
                    if 3 <= n < N + 3 and steps[n - 3][1] % 2:
                        i, h = steps[n - 3]
                        k = turn23[("o", n - 3)]
                        e.wait_ge(p_tr, k)
                        e.copy(m.mixT[:, 2 + h // 2, i * P:i * P + P], ps[:, 2 + k % 2, 0:P]).then_inc(p_to, 1)
                    if 2 <= n < N + 2:
                        i, h = steps[n - 2]
                        for g in range(groups(n - 2)):
                            k = turn23[("p", n - 2, g)]
                            w = min(4, i + 1 - 4 * g)
                            e.wait_ge(p_tr, k)
                            if g == 0 and n >= 4:
                                e.wait_ge(p_pv, n - 3)
                            e.copy(pT[:, n % 2, 4 * g:4 * g + w, :], ps[:, 2 + k % 2, 0:w * P].rearrange("p (k q) -> p k q", q=P)).then_inc(p_to, 1)
                    if 1 <= n <= N:
                        e.wait_ge(s_q, n)
                        e.copy(srow[:, (n - 1) % 2, :], b_q).then_inc(s_qo, 1)
                    if n < N:
                        nk = (steps[n][0] + 1) * P
                        e.wait_ge(p_so, n + 1)
                        e.activation(sc[n % 4][:, 0:nk], sc[n % 4][:, 0:nk], ACT.Exp, bias=nmax[:, n % 4:n % 4 + 1],
                                     accum_out=rsum[:, n % 4:n % 4 + 1]).then_inc(p_exp, 1)
                    b = sample_at(n, 2)
                    if b is not None:
                        e.wait_ge(s_shift, b + 1)
                        e.activation(S[:, b % 2], S[:, b % 2], ACT.Exp).then_inc(s_exp, 1)

            @block.vector
            def _(e):
                e.wait_ge(lf_in, 16)
                for h in range(H):
                    e.tensor_tensor_scan(cpg[:, h, :], m.ones[:, 0:1].broadcast_to([P, PAGE]),
                                         lfp[:].rearrange("p (t h) -> p h t", h=H)[:, h, :], 0.0, ALU.mult, ALU.add)
                e.tensor_scalar(nneg[:], m.sampmask[:], -1.0, -NEG, ALU.add, ALU.mult)
                e.drain()
                e.tensor_copy(tot[:], cpg[:, :, PAGE - 1]).then_inc(page_sums, 1)
                e.wait_ge(sums_mm, 1)
                e.tensor_copy(carry[:], ps[:, 5, 0:H])
                e.tensor_copy(cnew[:], ps[0:NS, 5, H:2 * H])
                e.drain()
                for h in range(H):
                    e.tensor_scalar(cpg[:, h, :], cpg[:, h, :], carry[:, h:h + 1], None, ALU.add)
                e.tensor_tensor(cdiag[:], m.ident[0:NS, 0:NS].unsqueeze(2).broadcast_to([NS, NS, H]),
                                cnew[:].unsqueeze(1).broadcast_to([NS, NS, H]), ALU.mult)
                e.drain().then_inc(page_sums, 1)
                e.wait_ge(sums_mm, 2)
                e.tensor_copy(cq[:].rearrange("p b l h -> p (b l h)"), ps[:, 5, 0:P])
                e.drain()
                for h in range(H):
                    e.tensor_tensor(bias[:, :, :, :, h], cq[:, :, :, h].unsqueeze(2).broadcast_to([P, DEC_B, NPG, DEC_L]),
                                    ps[:, 6, h * P:(h + 1) * P].rearrange("p (b g) -> p b g", g=NPG).unsqueeze(3).broadcast_to([P, DEC_B, NPG, DEC_L]),
                                    ALU.subtract)
                rows = snew[:].rearrange("p b l h -> p (b l) h")
                e.tensor_tensor(rows, ps[0:NS, 5, P:2 * P].rearrange("p (t h) -> p t h", h=H),
                                cq[0:NS].rearrange("p b l h -> p (b l) h"), ALU.add)
                e.drain()
                e.tensor_tensor(rows, rows, cnew[:].unsqueeze(1).broadcast_to([NS, NS, H]), ALU.subtract)
                e.drain()
                e.tensor_tensor(rows, rows, nneg[:].unsqueeze(2).broadcast_to([NS, NS, H]), ALU.add)
                e.drain().then_inc(page_sums, 1)
                e.wait_ge(qbd_ready, 1)
                e.wait_ge(ck_out, 2 * H)
                def sample_steps(n):
                    b = sample_at(n, 4)
                    if b is not None:
                        e.wait_ge(s_small, 3 * b + 3)
                        for h in range(H):
                            o, c = HD * (h % 2), h // 2
                            mm = e.tensor_copy(m.mixT[o:o + HD, 2 + c, SEQ + DEC_L * b:SEQ + DEC_L * b + DEC_L],
                                               b_ot[o:o + HD, R * c:R * c + R].rearrange("p (q h) -> p h q", h=H)[:, h, :])
                        mm.then_inc(s_out, 1)
                    b = sample_at(n, 1)
                    if b is not None:
                        e.wait_ge(s_small, 3 * b + 1)
                        e.tensor_reduce(rmax[:], b_max, AX.X, ALU.max)
                        e.drain()
                        e.tensor_scalar(maxdiag[:], m.ident[0:R, 0:R], rmax[:], None, ALU.mult).then_inc(s_row, 1)
                    b = sample_at(n, 2)
                    if b is not None:
                        e.wait_ge(s_small, 3 * b + 2)
                        e.tensor_tensor(S[:, b % 2], S[:, b % 2], b_bc.unsqueeze(1).broadcast_to([P, NPG + 1, R]), ALU.subtract).then_inc(s_shift, 1)
                    if 2 <= n < N + 2:
                        b, j = (n - 2) // NQ, (n - 2) % NQ
                        e.wait_ge(s_qt, n - 1)
                        if j == 0 and b >= 2:
                            e.wait_ge(s_pv, b - 1)
                        e.tensor_tensor(S[:, b % 2, QG * j:QG * j + QG, :], b_s.rearrange("p (g r) -> p g r", r=R),
                                        bias[:, b, QG * j:QG * j + QG].rearrange("p g l h -> p g (l h)"), ALU.add).then_inc(s_ev, 1)
                    b = sample_at(n, 0)
                    if b is not None:
                        e.tensor_copy(S[0:NS, b % 2, NPG, :], snew[:, b].rearrange("p l h -> p (l h)"))
                        e.drain()
                        e.tensor_reduce(cmax[:], S[:, b % 2].rearrange("p g r -> p r g"), AX.X, ALU.max).then_inc(s_max, 1)

                for n in range(LAST):
                    if sample_at(n, 4) is None:
                        sample_steps(n)
                    if n < N:
                        i, h = steps[n]
                        nk, s = (i + 1) * P, sc[n % 4]
                        e.wait_ge(p_sc, n + 1)
                        if n >= 4:
                            e.wait_ge(p_tr, last_of(n - 4))
                        for g in range(groups(n)):
                            w = min(512, nk - 512 * g)
                            mm = e.scalar_tensor_tensor(out=s[:, 512 * g:512 * g + w], in0=ps[:, g, 0:w], scalar=m.lft[:, i, H + h:H + h + 1],
                                                        in1=ck[:, h, 512 * g:512 * g + w], op0=ALU.add, op1=ALU.subtract)
                        mm.then_inc(p_read, 1)
                        e.drain()
                        e.tensor_tensor(s[:, nk - P:nk], s[:, nk - P:nk], m.qmask[:], ALU.add)
                        e.drain()
                        e.tensor_reduce(pmax[:, n % 4:n % 4 + 1], s[:, 0:nk], AX.X, ALU.max)
                        e.drain()
                        if n >= 4:
                            e.wait_ge(p_exp, n - 3)
                        e.tensor_scalar(nmax[:, n % 4:n % 4 + 1], pmax[:, n % 4:n % 4 + 1], -1.0, None, ALU.mult).then_inc(p_so, 1)
                        e.wait_ge(k_tr, n + 1)
                        if n >= 2:
                            e.wait_ge(s_q, n - 1)
                        e.tensor_copy(kT[:, n % 2, 1, :], ps[:, 6, :]).then_inc(k_o1, 1)
                    if sample_at(n, 4) is not None:
                        sample_steps(n)
                    b = sample_at(n, 3)
                    if b is not None:
                        e.wait_ge(s_exp, b + 1)
                        e.tensor_reduce(csum[:], S[:, b % 2].rearrange("p g r -> p r g"), AX.X, ALU.add).then_inc(s_col, 1)
                    if 2 <= n < N + 2:
                        k = n - 2
                        i, h = steps[k]
                        e.wait_ge(p_exp, k + 1)
                        e.reciprocal(rinv[:, k % 4:k % 4 + 1], rsum[:, k % 4:k % 4 + 1])
                        e.drain()
                        e.wait_ge(p_pv, k + 1)
                        if k >= 4:
                            e.wait_ge(p_tr, turn23[("o", (k - 4) // 2 * 2 + 1)])
                        e.tensor_scalar(ot[:, k // 2 % 2, k % 2 * HD:k % 2 * HD + HD], ps[:, 4, k % 2 * HD:k % 2 * HD + HD],
                                        rinv[:, k % 4:k % 4 + 1], None, ALU.mult).then_inc(p_oo, 1)
                    b = sample_at(n, 3)
                    if b is not None:
                        e.wait_ge(s_pv, b + 1)
                        e.reciprocal(sinv[:], b_sum)
                        e.drain()
                        e.tensor_scalar(orow[:], b_pv, sinv[:], None, ALU.mult).then_inc(s_div, 1)

            @block.tensor
            def _(e):
                for n in range(2 * H):
                    h = n // 2
                    if n >= 4:
                        e.wait_ge(ck_out, n - 3)
                    e.matmul(ps[:, n % 4, :], m.ident[F4, FROW + h:FROW + h + 1].broadcast_to([H, P]),
                             m.CF[F4, n % 2 * 512:n % 2 * 512 + 512], start=True, stop=True).then_inc(ck_mm, 1)
                e.wait_ge(page_sums, 1)
                e.matmul(ps[:, 5, 0:H], m.carry[:], tot[:], start=True, stop=True)
                e.matmul(ps[0:NS, 5, H:2 * H], m.pagesel[:], tot[:], start=True, stop=False, skip_group_check=True)
                e.matmul(ps[0:NS, 5, H:2 * H], m.sampmask[:], m.lft[0:NS, NT - 1, 0:H], start=False, stop=True,
                         skip_group_check=True).then_inc(sums_mm, 1)
                e.wait_ge(page_sums, 2)
                e.wait_ge(qbd_ready, 1)
                for h in range(H):
                    e.transpose(ps[:, 6, h * P:(h + 1) * P], cpg[:, h, :], m.ident[:])
                e.matmul(ps[:, 5, 0:P], m.ones[0:NS, :], cdiag[:].rearrange("p t h -> p (t h)"), start=True, stop=True)
                for c in range(2):
                    mm = e.matmul(ps[0:NS, 5, P:2 * P], m.Z[:, ZFK + c, SEQ:TOK], qbd[:, c].rearrange("p b l h -> p (b l h)"),
                                  start=(c == 0), stop=(c == 1), skip_group_check=True)
                mm.then_inc(sums_mm, 1)
                e.wait_ge(page_sums, 3)
                e.wait_ge(ck_out, 2 * H)

                def sample_steps(n):
                    b = sample_at(n, 4)
                    if b is not None:
                        e.wait_ge(s_div, b + 1)
                        for c in range(2):
                            mm = e.transpose(b_ot[:, R * c:R * c + R], orow[:, c * P:c * P + P], m.ident[0:R, 0:R])
                        mm.then_inc(s_small, 1)
                    b = sample_at(n, 1)
                    if b is not None:
                        e.wait_ge(s_max, b + 1)
                        e.wait_ge(s_qo, min(n - 1, N))
                        e.transpose(b_max, cmax[:], m.ident[:]).then_inc(s_small, 1)
                    b = sample_at(n, 2)
                    if b is not None:
                        e.wait_ge(s_row, b + 1)
                        e.wait_ge(s_qo, min(n - 1, N))
                        e.matmul(b_bc, m.ones[0:R, :], maxdiag[:], start=True, stop=True).then_inc(s_small, 1)
                    if 2 <= n < N + 2:
                        e.wait_ge(s_qo, n - 1)
                        if sample_at(n, 1) is not None:
                            e.wait_ge(s_row, sample_at(n, 1) + 1)
                        if sample_at(n, 2) is not None:
                            e.wait_ge(s_shift, sample_at(n, 2) + 1)
                        if sample_at(n, 4) is not None:
                            e.wait_ge(s_out, sample_at(n, 4) + 1)
                        for g in range(QG):
                            mm = e.transpose(b_s[:, g * R:(g + 1) * R], srow[:, n % 2, g * PAGE:(g + 1) * PAGE], m.ident[0:R, 0:R])
                        mm.then_inc(s_qt, 1)

                for n in range(LAST):
                    if sample_at(n, 4) is None:
                        sample_steps(n)
                    if n < N:
                        i, h = steps[n]
                        o, c = HD * (h % 2), h // 2
                        if n >= 1:
                            e.wait_ge(p_read, n)
                        for g in range(groups(n)):
                            w = min(512, (i + 1) * P - 512 * g)
                            mm = e.matmul(ps[:, g, 0:w], m.Z[o:o + HD, ZFQ + c, i * P:i * P + P],
                                          m.Z[o:o + HD, ZFK + c, 512 * g:512 * g + w], start=True, stop=True)
                        mm.then_inc(p_sc, 1)
                        e.wait_ge(k_in[n % 4], 16 * QG * (n // 4 + 1))
                        if n >= 1:
                            e.wait_ge(k_o0, n)
                            e.wait_ge(k_o1, n)
                        for c in range(2):
                            for g in range(QG):
                                mm = e.transpose(ps[:, 5 + c, g * PAGE:(g + 1) * PAGE], kpg[:, n % 4, g, c * P:c * P + P], m.ident[:])
                        mm.then_inc(k_tr, 1)
                    if sample_at(n, 4) is not None:
                        sample_steps(n)
                    if 3 <= n < N + 3 and steps[n - 3][1] % 2:
                        k = turn23[("o", n - 3)]
                        e.wait_ge(p_oo, n - 2)
                        if k >= 3:
                            e.wait_ge(p_to, k - 2)
                        e.transpose(ps[:, 2 + k % 2, 0:P], ot[:, (n - 3) // 2 % 2, :], m.ident[:]).then_inc(p_tr, 1)
                    if 2 <= n < N + 2:
                        i, h = steps[n - 2]
                        e.wait_ge(p_exp, n - 1)
                        for g in range(groups(n - 2)):
                            k = turn23[("p", n - 2, g)]
                            if k >= 3:
                                e.wait_ge(p_to, k - 2)
                            for a in range(4 * g, min(4 * g + 4, i + 1)):
                                mm = e.transpose(ps[:, 2 + k % 2, (a - 4 * g) * P:(a - 4 * g + 1) * P], sc[(n - 2) % 4][:, a * P:a * P + P], m.ident[:])
                            mm.then_inc(p_tr, 1)
                    if 1 <= n <= N:
                        b = (n - 1) // NQ
                        e.wait_ge(k_o0, n)
                        e.wait_ge(k_o1, n)
                        if n >= 2:
                            e.wait_ge(s_ev, n - 1)
                        for c in range(2):
                            mm = e.matmul(b_q, qbd[:, c, b].rearrange("p l h -> p (l h)"), kT[:, (n - 1) % 2, c, :],
                                          start=(c == 0), stop=(c == 1))
                        mm.then_inc(s_q, 1)
                    if 2 <= n < N + 2:
                        i, h = steps[n - 2]
                        e.wait_ge(p_to, last_of(n - 2))
                        if n >= 3:
                            e.wait_ge(p_oo, n - 2)
                        for a in range(i + 1):
                            mm = e.matmul(ps[:, 4, n % 2 * HD:n % 2 * HD + HD], pT[:, n % 2, a, :], m.V[:, a, W + h * HD:W + (h + 1) * HD],
                                          start=(a == 0), stop=(a == i), skip_group_check=True)
                        mm.then_inc(p_pv, 1)
                    b = sample_at(n, 3)
                    if b is not None:
                        e.wait_ge(s_qo, min(n, N))
                        e.wait_ge(s_ev, min(n - 1, N))
                        e.wait_ge(s_shift, b + 1)
                        e.wait_ge(s_col, b + 1)
                        e.matmul(b_sum, csum[:], m.ones[:, 0:1], start=True, stop=True, skip_group_check=True)
                        e.wait_ge(v_in, 16 * NPG * (b + 1))
                        for g in range(NPG + 1):
                            values = vpg[:, g, :] if g < NPG else m.V[0:NS, NT - 1, W:2 * W]
                            mm = e.matmul(b_pv, S[0:P if g < NPG else NS, b % 2, g, :], values,
                                          start=(g == 0), stop=(g == NPG), skip_group_check=True)
                        mm.then_inc(s_pv, 1)


def out_projection(nc, m):
    ctx = ExitStack()
    sb = lambda name, shape: ctx.enter_context(nc.sbuf_tensor(name, shape, F32))
    sem = lambda name: ctx.enter_context(nc.semaphore(name))
    ps = m.ps
    with ctx:
        wo = sb("wo", [P, KC, D])
        x1 = sb("x1", [P, 2, D])
        h2 = sb("h2", [P, 2, D])
        h2T = sb("h2T", [P, 2, KC, P])
        junk = sb("junk2", [P, D])
        ssq, std, rstd = sb("ssq2", [P, 2]), sb("std2", [P, 2]), sb("rstd2", [P, 2])
        wo_in, x1_in, h2_sent = sem("wo_in"), [sem(f"x1_in{i}") for i in range(2)], [sem(f"h2_sent{i}") for i in range(2)]
        o_mm, x2_done, std_done, h2_done, h2_tr, h2T_out, lg_mm, lg_out = (
            sem("c_" + n) for n in ("o_mm", "x2", "std", "h2", "h2_tr", "h2T_out", "lg_mm", "lg_out"))

        with nc.Block() as block:

            @block.sync
            def _(e):
                for n in range(2):
                    e.dma_start(wo[:, :, n * 512:(n + 1) * 512],
                                m.w_out[0].rearrange("(k p) n -> p k n", p=P)[:, :, n * 512:(n + 1) * 512]).then_inc(wo_in, 16)
                for t in range(NT):
                    r = rows_of(t)
                    if t >= 2:
                        e.wait_ge(x2_done, t - 1)
                    src = m.x_prompt[0, t * P:(t + 1) * P, :] if t < NT - 1 else m.x_sample.rearrange("b l d -> (b l) d")
                    e.dma_start(x1[0:r, t % 2, :], src).then_inc(x1_in[t % 2], 16)

            @block.gpsimd
            def _(e):
                e.memset(m.gidx[:], 0)
                e.drain()
                e.dma_start(m.slot_tok.rearrange("(p t) a -> p (t a)", t=SLOT_TILES), m.gidx[:]).then_inc(m.s_table, 16)
                for t in range(NT):
                    e.wait_ge(h2_done, t + 1)
                    e.dma_start(m.h2d[t * P:t * P + rows_of(t), :], h2[0:rows_of(t), t % 2, :]).then_inc(h2_sent[t % 2], 16)
                e.wait_ge(m.s_table, 16)
                e.wait_ge(m.s_zero_rows, 16 * (SLOT_TILES - 2 * LEAST_PAIRS))
                for i in range(2):
                    e.wait_ge(h2_sent[i], 16 * ((NT + 1 - i) // 2))

            @block.scalar
            def _(e):
                for t in range(NT):
                    r, b = rows_of(t), t % 2
                    e.wait_ge(x2_done, t + 1)
                    e.activation(junk[0:r], m.x2[0:r, t, :], ACT.Square, scale=D ** -0.5, accum_out=ssq[0:r, b:b + 1])
                    e.drain()
                    e.activation(std[0:r, b:b + 1], ssq[0:r, b:b + 1], ACT.Sqrt, bias=m.eps[0:r, :]).then_inc(std_done, 1)

            @block.vector
            def _(e):
                e.memset(m.logits[:], 0.0)

                def tail(t):
                    r, b = rows_of(t), t % 2
                    e.wait_ge(h2_tr, t + 1)
                    if t >= 2:
                        e.wait_ge(lg_mm, t - 1)
                    for c in range(2):
                        i = e.tensor_tensor(h2T[:, b, 4 * c:4 * c + 4, 0:r], ps[:, 4 + c, :].rearrange("p (k t) -> p k t", k=4)[:, :, 0:r],
                                            m.g2[:, 4 * c:4 * c + 4].unsqueeze(2).broadcast_to([P, 4, r]), ALU.mult)
                    i.then_inc(h2T_out, 1)

                def logits(t):
                    r = rows_of(t)
                    e.wait_ge(lg_mm, t + 1)
                    e.tensor_tensor(m.logits[0:r, t, :], ps[0:r, 6 + t % 2, 0:NG + NE], m.rb[0:r, :], ALU.add).then_inc(lg_out, 1)

                for t in range(NT):
                    r, b = rows_of(t), t % 2
                    e.wait_ge(o_mm, t + 1)
                    e.wait_ge(x1_in[b], 16 * (t // 2 + 1))
                    e.tensor_tensor(m.x2[0:r, t, :], ps[0:r, 2 * b:2 * b + 2, :].rearrange("p c n -> p (c n)"), x1[0:r, b, :], ALU.add).then_inc(x2_done, 1)
                    e.wait_ge(std_done, t + 1)
                    e.reciprocal(rstd[0:r, b:b + 1], std[0:r, b:b + 1])
                    e.drain()
                    if t >= 2:
                        e.wait_ge(h2_tr, t - 1)
                        e.wait_ge(h2_sent[b], 16 * (t // 2))
                    e.tensor_scalar(h2[0:r, b, :], m.x2[0:r, t, :], rstd[0:r, b:b + 1], None, ALU.mult).then_inc(h2_done, 1)
                    tail(t)
                    if t:
                        logits(t - 1)
                logits(NT - 1)

            @block.tensor
            def _(e):
                def product(t):
                    r, b = rows_of(t), t % 2
                    if t >= 2:
                        e.wait_ge(x2_done, t - 1)
                    for n in range(2):
                        for k in range(KC):
                            i = e.matmul(ps[0:r, 2 * b + n, :], m.mixT[:, k, t * P:t * P + r], wo[:, k, n * 512:(n + 1) * 512],
                                         start=(k == 0), stop=(k == KC - 1))
                    i.then_inc(o_mm, 1)

                e.wait_ge(wo_in, 32)
                product(0)
                for t in range(NT):
                    if t + 1 < NT:
                        product(t + 1)
                    r, b = rows_of(t), t % 2
                    e.wait_ge(h2_done, t + 1)
                    if t:
                        e.wait_ge(h2T_out, t)
                    for k in range(KC):
                        i = e.transpose(ps[:, 4 + k // 4, k % 4 * P:k % 4 * P + r], h2[0:r, b, k:D:KC], m.ident[0:r, 0:r])
                    i.then_inc(h2_tr, 1)
                    e.wait_ge(h2T_out, t + 1)
                    if t >= 2:
                        e.wait_ge(lg_out, t - 1)
                    for k in range(KC):
                        i = e.matmul(ps[0:r, 6 + b, 0:NG + NE], h2T[:, b, k, 0:r], m.wr[:, k, :], start=(k == 0), stop=(k == KC - 1))
                    i.then_inc(lg_mm, 1)


def route(nc, m):
    ctx = ExitStack()
    sb = lambda name, shape, dt=F32: ctx.enter_context(nc.sbuf_tensor(name, shape, dt))
    sem = lambda name: ctx.enter_context(nc.semaphore(name))
    ps = m.ps
    B3, B4 = [P, NT, NE], [P, NT, NG, NE // NG]
    with ctx:
        G, E = m.logits[:, :, 0:NG], m.logits[:, :, NG:NG + NE]
        gmax, gsum, gw = sb("gmax", [P, NT]), sb("gsum", [P, NT]), sb("gw", [P, NT])
        gx, gsel = sb("gx", [P, NT, NG]), sb("gsel", [P, NT, NG])
        em, wi, prio = sb("em", B3), sb("wi", B3), sb("prio", B3)
        oh = [sb("oh1", B3), sb("oh2", B3)]
        both, valid = sb("both", B3), sb("valid", [P, NT])
        top = [sb("top1", [P, NT]), sb("top2", [P, NT])]
        first = sb("first", [P, NT])
        ex, den = sb("ex", [P, NT]), sb("den", [P, NT])
        slot = sb("slot", B3)
        run = sb("run", [P, NT + 1, NE])
        ntile, incl, base = sb("ntile", [P, NE]), sb("incl", [P, NE]), sb("base", [P, NE])
        sf = sb("sf", [P, 2, NT])
        pos, pos2 = sb("pos", [P, 2, NT], I32), sb("pos2", [P, 2, NT], I32)
        te = sb("te", [1, SLOT_TILES, NE])
        tsum = sb("tsum", [1, SLOT_TILES])
        gdiff, exps, oh_done, cnt_mm, pos_done, sent, tab_in = (
            sem("r_" + n) for n in ("gdiff", "exps", "oh", "cnt_mm", "pos", "sent", "tab_in"))

        with nc.Block() as block:

            @block.scalar
            def _(e):
                e.wait_ge(gdiff, 1)
                e.activation(gx[:], gx[:], ACT.Exp).then_inc(exps, 1)
                e.wait_ge(gdiff, 2)
                e.activation(ex[:], ex[:], ACT.Exp).then_inc(exps, 1)

            @block.vector
            def _(e):
                bc = lambda x, n: x[:].unsqueeze(2).broadcast_to([P, NT, n])

                def pick(src, mx, out, n, pr):
                    e.tensor_tensor(wi[:, :, 0:n], src, bc(mx, n), ALU.is_equal)
                    e.drain()
                    e.tensor_tensor(wi[:, :, 0:n], wi[:, :, 0:n], pr, ALU.mult)
                    e.drain()
                    e.tensor_reduce(first[:], wi[:, :, 0:n], AX.X, ALU.max)
                    e.drain()
                    e.tensor_tensor(out, wi[:, :, 0:n], bc(first, n), ALU.is_equal)
                    e.drain()

                e.tensor_scalar(prio[:], m.exp_id[:], -1.0, float(NE), ALU.mult, ALU.add)
                e.tensor_scalar(valid[:], m.tok_id[:], float(TOK), None, ALU.is_lt)
                e.tensor_reduce(gmax[:], G, AX.X, ALU.max)
                e.drain()
                e.tensor_tensor(gx[:], G, bc(gmax, NG), ALU.subtract).then_inc(gdiff, 1)
                pick(G, gmax, gsel[:], NG, prio[:, :, 0:NG])
                e.tensor_scalar(gsel[:], gsel[:], -1.0, -NEG, ALU.add, ALU.mult)
                e.drain()
                e.tensor_tensor(em[:].rearrange("p t (g k) -> p t g k", g=NG), E.rearrange("p t (g k) -> p t g k", g=NG),
                                gsel[:].unsqueeze(3).broadcast_to(B4), ALU.add)
                e.drain()
                e.tensor_reduce(top[0][:], em[:], AX.X, ALU.max)
                e.drain()
                pick(em[:], top[0], oh[0][:], NE, prio[:])
                e.scalar_tensor_tensor(out=em[:], in0=oh[0][:], scalar=NEG, in1=em[:], op0=ALU.mult, op1=ALU.add)
                e.drain()
                e.tensor_reduce(top[1][:], em[:], AX.X, ALU.max)
                e.drain()
                e.tensor_tensor(ex[:], top[1][:], top[0][:], ALU.subtract).then_inc(gdiff, 1)
                pick(em[:], top[1], oh[1][:], NE, prio[:])
                e.tensor_tensor(both[:], oh[0][:], oh[1][:], ALU.add)
                e.drain()
                e.tensor_tensor(both[:], both[:], bc(valid, NE), ALU.mult).then_inc(oh_done, 1)
                e.wait_ge(exps, 2)
                e.tensor_reduce(gsum[:], gx[:], AX.X, ALU.add)
                e.tensor_scalar(den[:], ex[:], 1.0, None, ALU.add)
                e.drain()
                e.tensor_tensor(den[:], den[:], gsum[:], ALU.mult)
                e.drain()
                e.reciprocal(m.gate[:, 0, :], den[:])
                e.drain()
                e.tensor_tensor(m.gate[:, 1, :], m.gate[:, 0, :], ex[:], ALU.mult)
                e.wait_ge(cnt_mm, 1)
                e.memset(run[:, 0, :], 0.0)
                e.memset(ntile[:], 0.0)
                e.drain()
                for t in range(NT):
                    e.tensor_tensor(run[:, t + 1, :], run[:, t, :], ps[:, 1, t * NE:(t + 1) * NE], ALU.add)
                    e.drain()
                for j in range(NT):
                    e.scalar_tensor_tensor(out=ntile[:], in0=run[:, NT, :], scalar=float(P * j), in1=ntile[:], op0=ALU.is_gt, op1=ALU.add)
                    e.drain()
                e.tensor_tensor_scan(incl[:], m.ones[:, 0:NE], ntile[:], 0.0, ALU.mult, ALU.add)
                e.drain()
                e.tensor_tensor(base[:], incl[:], ntile[:], ALU.subtract)
                e.tensor_tensor(slot[:], ps[:, 0, 0:NT * NE].rearrange("p (t n) -> p t n", n=NE), run[:, 0:NT, :], ALU.add)
                e.drain()
                e.scalar_tensor_tensor(out=slot[:], in0=base[:].unsqueeze(1).broadcast_to(B3), scalar=float(P), in1=slot[:],
                                       op0=ALU.mult, op1=ALU.add)
                e.drain()
                for c in range(2):
                    e.tensor_tensor(em[:], oh[c][:], slot[:], ALU.mult)
                    e.drain()
                    e.tensor_reduce(sf[:, c, :], em[:], AX.X, ALU.add)
                    e.drain()
                e.tensor_copy(m.slots[:], sf[:])
                e.drain()
                e.tensor_scalar(pos[:], m.slots[:], P - 1, 5, ALU.bitwise_and, ALU.logical_shift_left)
                e.tensor_scalar(pos2[:], m.slots[:], 7, None, ALU.logical_shift_right)
                e.drain()
                e.tensor_tensor(pos[:], pos[:], pos2[:], ALU.add).then_inc(pos_done, 1)
                e.tensor_tensor(te[:], m.tile_id[0:1].unsqueeze(2).broadcast_to([1, SLOT_TILES, NE]),
                                incl[0:1].unsqueeze(1).broadcast_to([1, SLOT_TILES, NE]), ALU.is_ge)
                e.drain()
                e.tensor_reduce(tsum[:], te[:], AX.X, ALU.add)
                e.drain()
                e.tensor_scalar(m.tile_exp[:], tsum[:], float(NE - 1), None, ALU.min)
                e.tensor_scalar(m.more_pairs[:], incl[0:1, NE - 1:NE], 1.0 - 2 * LEAST_PAIRS, 0.0, ALU.add, ALU.max)
                e.drain()
                e.tensor_scalar(m.more_pairs[:], m.more_pairs[:], 1, None, ALU.logical_shift_right)

            @block.tensor
            def _(e):
                e.wait_ge(oh_done, 1)
                rhs = both[:].rearrange("p t n -> p (t n)")
                e.matmul(ps[:, 0, 0:NT * NE], m.strict[:], rhs, start=True, stop=True)
                e.matmul(ps[:, 1, 0:NT * NE], m.ones[:], rhs, start=True, stop=True).then_inc(cnt_mm, 1)

            @block.gpsimd
            def _(e):
                e.wait_ge(pos_done, 1)
                for t in range(NT):
                    r = rows_of(t)
                    for c in range(2):
                        e.indirect_dma_start(out=m.slot_tok, out_offset=bass.IndirectOffsetOnAxis(ap=pos[0:r, c, t:t + 1], axis=0),
                                             in_=m.tok_id[0:r, t:t + 1], in_offset=None).then_inc(sent, 16)
                e.wait_ge(sent, 16 * 2 * NT)
                e.dma_start(m.gidx[:], m.slot_tok.rearrange("(p t) a -> p (t a)", t=SLOT_TILES)).then_inc(tab_in, 16)
                e.wait_ge(tab_in, 16)


def experts(nc, m):
    ctx = ExitStack()
    sb = lambda name, shape, dt=F32: ctx.enter_context(nc.sbuf_tensor(name, shape, dt))
    sem = lambda name: ctx.enter_context(nc.semaphore(name))
    ps = m.ps
    KE = DE // P
    S = SLOT_TILES
    with ctx:
        wg, wu = sb("wg", [P, 2, KC, DE]), sb("wu", [P, 2, KC, DE])
        wd = m.mixT[:].rearrange("p k t -> p (k t)")[:, 0:2 * KE * D].rearrange("p (b k n) -> p b k n", b=2, k=KE)
        hg, hgT = sb("hg", [P, 2, D]), sb("hgT", [P, 2, KC, P])
        gcol = [sb(f"gcol{i}", [P, 1], I32) for i in range(2)]
        sg, he, heT = sb("sg", [P, 2, DE]), sb("he", [P, 2, DE]), sb("heT", [P, 2, KE, P])
        yo = sb("yo", [P, 2, D])
        landed = sb("landed", [1, 2])
        pair = lambda n: [sem(f"{n}{i}") for i in range(2)]
        gu_in, dn_in, hg_in, y_sent = pair("gu_in"), pair("dn_in"), pair("hg_in"), pair("y_sent")
        t_mm, t_out, gu_mm, silu, he_done, he_mm, he_out, d_mm, y_a, y_v = (
            sem("e_" + n) for n in ("t_mm", "t_out", "gu_mm", "silu", "he", "he_mm", "he_out", "d_mm", "y_a", "y_v"))


        def pairs(e):
            return e.value_load(m.more_pairs[0:1, 0:1], min_val=0, max_val=S // 2 - LEAST_PAIRS) + LEAST_PAIRS

        with nc.Block() as block:

            @block.sync
            def _(e):
                def load(s, b, first=False):
                    x = e.value_load(m.tile_exp[0:1, ds(s, 1)], min_val=0, max_val=NE - 1)
                    for n, (to, of) in enumerate(((wg, m.exp_w_gate), (wu, m.exp_w_up))):
                        if n == 0 and not first:
                            e.wait_ge(gu_mm, s - 1)
                        e.dma_start(to[:, b].unsqueeze(1), of[0, ds(x, 1)].rearrange("a (p k) n -> p a k n", k=KC)).then_inc(gu_in[b], 16)
                    if not first:
                        e.wait_ge(d_mm, s - 1)
                    e.dma_start(wd[:, b].unsqueeze(1), m.exp_w_down[0, ds(x, 1)].rearrange("a (p k) n -> p a k n", k=KE)).then_inc(dn_in[b], 16)

                load(0, 0, True)
                load(1, 1, True)
                with e.Fori(1, pairs(e)) as j:
                    load(2 * j, 0)
                    load(2 * j + 1, 1)

            @block.gpsimd
            def _(e):
                def gather(s, b, first=False):
                    if not first:
                        e.wait_ge(t_mm, s - 1)
                    e.tensor_copy(gcol[b][:], m.gidx[:, ds(s, 1)])
                    e.drain()
                    e.indirect_dma_start(out=hg[:, b, :], out_offset=None, in_=m.h2d,
                                         in_offset=bass.IndirectOffsetOnAxis(ap=gcol[b][:, 0:1], axis=0)).then_inc(hg_in[b], 16)

                gather(0, 0, True)
                gather(1, 1, True)
                with e.Fori(1, pairs(e)) as j:
                    gather(2 * j, 0)
                    gather(2 * j + 1, 1)

            @block.scalar
            def _(e):
                def act_silu(s, b):
                    e.wait_ge(gu_mm, s + 1)
                    e.activation(sg[:, b, :], ps[:, 2 * b, :], ACT.Silu).then_inc(silu, 1)

                def step(s, b, j, last=False):
                    e.wait_ge(he_mm, s + 1)
                    e.copy(heT[:, b], ps[:, 2 * b, :].rearrange("p (k t) -> p k t", k=KE)).then_inc(he_out, 1)
                    e.wait_ge(d_mm, s + 1)
                    if not (isinstance(j, int) and j == 0):
                        e.wait_ge(y_sent[b], 16 * j)
                    e.copy(yo[:, b, 0:512], ps[:, 6, :]).then_inc(y_a, 1)
                    e.wait_ge(y_a, s + 1)
                    e.wait_ge(y_v, s + 1)
                    e.dma_start(m.yd[ds(s * P, P), :], yo[:, b, :]).then_inc(y_sent[b], 16)
                    if not last:
                        act_silu(s + 2, b)

                act_silu(0, 0)
                act_silu(1, 1)
                step(0, 0, 0)
                step(1, 1, 0)
                n = pairs(e)
                with e.Fori(1, n - 1) as j:
                    step(2 * j, 0, j)
                    step(2 * j + 1, 1, j)
                step(2 * n - 2, 0, n - 1, True)
                step(2 * n - 1, 1, n - 1, True)
                for i in range(2):
                    e.wait_ge(y_sent[i], 16 * n)
                    e.copy(landed[0:1, i:i + 1], m.eps[0:1, :])

            @block.vector
            def _(e):
                def turn_out(s, b, first=False):
                    e.wait_ge(t_mm, s + 1)
                    if not first:
                        e.wait_ge(gu_mm, s - 1)
                    for c in range(2):
                        i = e.tensor_tensor(hgT[:, b, 4 * c:4 * c + 4, :], ps[:, 4 + c, :].rearrange("p (k t) -> p k t", k=4),
                                            m.g2[:, 4 * c:4 * c + 4].unsqueeze(2).broadcast_to([P, 4, P]), ALU.mult)
                    i.then_inc(t_out, 1)

                def make_he(s, b):
                    e.wait_ge(silu, s + 1)
                    e.tensor_tensor(he[:, b, :], sg[:, b, :], ps[:, 2 * b + 1, :], ALU.mult).then_inc(he_done, 1)

                def step(s, b, j, last=False):
                    if not last:
                        turn_out(s + 2, b)
                    e.wait_ge(d_mm, s + 1)
                    if not (isinstance(j, int) and j == 0):
                        e.wait_ge(y_sent[b], 16 * j)
                    e.tensor_copy(yo[:, b, 512:], ps[:, 7, :]).then_inc(y_v, 1)
                    if not last:
                        make_he(s + 2, b)

                for s in range(2):
                    turn_out(s, s, True)
                    make_he(s, s)
                step(0, 0, 0)
                step(1, 1, 0)
                n = pairs(e)
                with e.Fori(1, n - 1) as j:
                    step(2 * j, 0, j)
                    step(2 * j + 1, 1, j)
                step(2 * n - 2, 0, n - 1, True)
                step(2 * n - 1, 1, n - 1, True)

            @block.tensor
            def _(e):
                def turn(s, b, j):
                    e.wait_ge(hg_in[b], 16 * j + 16)
                    if not (isinstance(s, int) and s == 0):
                        e.wait_ge(t_out, s)
                    for k in range(KC):
                        i = e.transpose(ps[:, 4 + k // 4, k % 4 * P:k % 4 * P + P], hg[:, b, k:D:KC], m.ident[:])
                    i.then_inc(t_mm, 1)

                def gate_up(s, b, j):
                    e.wait_ge(t_out, s + 1)
                    e.wait_ge(gu_in[b], 32 * j + 32)
                    for n, w in enumerate((wg, wu)):
                        for k in range(KC):
                            i = e.matmul(ps[:, 2 * b + n, :], hgT[:, b, k, :], w[:, b, k, :], start=(k == 0), stop=(k == KC - 1))
                    i.then_inc(gu_mm, 1)

                def step(s, b, j, last=False):
                    e.wait_ge(he_done, s + 1)
                    for k in range(KE):
                        i = e.transpose(ps[:, 2 * b, k * P:k * P + P], he[:, b, k:DE:KE], m.ident[:])
                    i.then_inc(he_mm, 1)
                    if not last:
                        turn(s + 2, b, j + 1)
                    e.wait_ge(he_out, s + 1)
                    e.wait_ge(dn_in[b], 16 * j + 16)
                    if not (isinstance(s, int) and s == 0):
                        e.wait_ge(y_a, s)
                        e.wait_ge(y_v, s)
                    for n in range(2):
                        for k in range(KE):
                            i = e.matmul(ps[:, 6 + n, :], heT[:, b, k, :], wd[:, b, k, n * 512:(n + 1) * 512],
                                         start=(k == 0), stop=(k == KE - 1))
                    i.then_inc(d_mm, 1)
                    if not last:
                        gate_up(s + 2, b, j + 1)

                for s in range(2):
                    turn(s, s, 0)
                    gate_up(s, s, 0)
                step(0, 0, 0)
                step(1, 1, 0)
                n = pairs(e)
                with e.Fori(1, n - 1) as j:
                    step(2 * j, 0, j)
                    step(2 * j + 1, 1, j)
                step(2 * n - 2, 0, n - 1, True)
                step(2 * n - 1, 1, n - 1, True)


def combine(nc, m):
    ctx = ExitStack()
    sem = lambda name: ctx.enter_context(nc.semaphore(name))
    with ctx:
        yr = ctx.enter_context(nc.sbuf_tensor("yr", [P, 4, D], F32))
        rows_in, done, sent = [sem(f"rows_in{i}") for i in range(4)], sem("y_done2"), sem("y_out")

        with nc.Block() as block:

            @block.gpsimd
            def _(e):
                for t in range(NT):
                    r = rows_of(t)
                    for c in range(2):
                        b = 2 * (t % 2) + c
                        if t >= 2:
                            e.wait_ge(done, t - 1)
                        e.indirect_dma_start(out=yr[0:r, b, :], out_offset=None, in_=m.yd,
                                             in_offset=bass.IndirectOffsetOnAxis(ap=m.slots[0:r, c, t:t + 1], axis=0)).then_inc(rows_in[b], 16)

            @block.vector
            def _(e):
                for t in range(NT):
                    r = rows_of(t)
                    for c in range(2):
                        b = 2 * (t % 2) + c
                        e.wait_ge(rows_in[b], 16 * (t // 2 + 1))
                        i = e.scalar_tensor_tensor(out=m.x2[0:r, t, :], in0=yr[0:r, b, :], scalar=m.gate[0:r, c, t:t + 1],
                                                   in1=m.x2[0:r, t, :], op0=ALU.mult, op1=ALU.add)
                        if c == 0:
                            e.drain()
                    i.then_inc(done, 1)

            @block.sync
            def _(e):
                for t in range(NT):
                    e.wait_ge(done, t + 1)
                    to = m.y_prompt[0, t * P:(t + 1) * P, :] if t < NT - 1 else m.y_sample.rearrange("b l d -> (b l) d")
                    e.dma_start(to, m.x2[0:rows_of(t), t, :]).then_inc(sent, 16)
                e.wait_ge(sent, 16 * NT)


OUTS = [("y_prompt", (1, SEQ, D)), ("y_sample", (DEC_B, DEC_L, D)),
        ("k_prompt", (1, 1, SEQ, H, HD)), ("v_prompt", (1, 1, SEQ, H, HD)), ("logf_prompt", (1, 1, SEQ, H)),
        ("k_sample", (1, DEC_B, DEC_L, H, HD)), ("v_sample", (1, DEC_B, DEC_L, H, HD)), ("logf_sample", (1, DEC_B, DEC_L, H)),
        ("gla_prompt", (1, 1, H, HD, HD)), ("gla_sample", (1, DEC_B, H, HD, HD)),
        ("conv_prompt", (1, 1, TAPS - 1, W)), ("conv_sample", (1, DEC_B, TAPS - 1, W)),
        ("pool_prompt", (1, 1, PMAX - 1, W)), ("pool_sample", (1, DEC_B, PMAX - 1, W))]


def program(nc, m):
    ctx = ExitStack()
    sb = lambda name, shape, dt=F32: ctx.enter_context(nc.sbuf_tensor(name, shape, dt))
    with ctx:
        m.ps = ctx.enter_context(nc.psum_tensor("ps", [P, 8, 512], F32))
        m.s_param, m.s_zero_rows = (ctx.enter_context(nc.semaphore(n)) for n in ("s_param", "s_zero_rows"))
        m.ident, m.ones, m.headmean, m.chmean = sb("ident", [P, P]), sb("ones", [P, P]), sb("headmean", [P, P]), sb("chmean", [P, P])
        m.causal, m.strict, m.qmask = sb("causal", [P, P]), sb("strict", [P, P]), sb("qmask", [P, P])
        m.sampmask = sb("sampmask", [NS, NS])
        m.eps = sb("eps", [P, 1])
        m.carry, m.pagesel = sb("carry", [P, P]), sb("pagesel", [P, NS])
        m.reset, m.poolw = sb("reset", [P, TOK]), sb("poolw", [P, 2, P])
        m.tok_id = sb("tok_id", [P, NT], I32)
        m.exp_id_i, m.exp_id = sb("exp_id_i", [P, NT, NE], I32), sb("exp_id", [P, NT, NE])
        m.tile_id_i, m.tile_id = sb("tile_id_i", [P, SLOT_TILES], I32), sb("tile_id", [P, SLOT_TILES])
        m.count_i, m.count = sb("count_i", [P, PMAX], I32), sb("count", [P, PMAX])
        m.g1, m.g2 = sb("g1", [P, KC]), sb("g2", [P, KC])
        m.gla_g, m.gla_b, m.cb, m.ln_g, m.ln_b, m.pscale = (sb(n, [P, 2]) for n in ("gla_g", "gla_b", "cb", "ln_g", "ln_b", "pscale"))
        m.fqg, m.fkg, m.fb = sb("fqg", [P, 1]), sb("fkg", [P, 1]), sb("fb", [FROW + H, 1])
        m.wa2, m.tapw = sb("wa2", [RANK, W]), sb("tapw", [TAPS, W])
        m.wr, m.rb = sb("wr", [P, KC, NG + NE]), sb("rb", [P, NG + NE])
        m.pages, m.pages_col = sb("pages", [1, P], I32), sb("pages_col", [P, 1], I32)
        m.fqg8 = sb("fqg8", [P, 1])
        m.CF, m.lft = sb("CF", [FROW + H, TOK]), sb("lft", [P, NT, 2 * H])
        constants(nc, m)
        m.mixT = sb("mixT", [P, KC, TOK])
        with (nc.sbuf_tensor("Z", [P, 16, TOK], F32) as m.Z, nc.sbuf_tensor("ZS", [FROW + H, TOK], F32) as m.ZS,
              nc.sbuf_tensor("V", [P, NT, 2 * W], F32) as m.V):
            projections(nc, m)
            gla_pool_norms(nc, m)
            fox(nc, m)
        m.s_table = ctx.enter_context(nc.semaphore("s_table"))
        m.x2 = sb("x2", [P, NT, D])
        m.logits = sb("logits", [P, NT, NG + NE])
        m.gate, m.slots = sb("gate", [P, 2, NT]), sb("slots", [P, 2, NT], I32)
        m.gidx, m.tile_exp = sb("gidx", [P, SLOT_TILES], I32), sb("tile_exp", [1, SLOT_TILES], I32)
        m.more_pairs = sb("more_pairs", [1, 1], I32)
        out_projection(nc, m)
        route(nc, m)
        experts(nc, m)
        combine(nc, m)


def build(nc, arrays):
    m = Memory()
    m.x_prompt, m.x_sample, m.cache_k, m.cache_v = arrays["x_prompt"], arrays["x_sample"], arrays["cache_k"], arrays["cache_v"]
    m.cache_logf, m.page_table, m.state_gla, m.state_conv = arrays["cache_logf"], arrays["page_table"], arrays["state_gla"], arrays["state_conv"]
    m.state_pool, m.norm1_g, m.w_in, m.gla_w_a2 = arrays["state_pool"], arrays["norm1_g"], arrays["w_in"], arrays["gla_w_a2"]
    m.gla_b_a, m.gla_norm_g, m.fox_b_f, m.fox_q_norm_g = arrays["gla_b_a"], arrays["gla_norm_g"], arrays["fox_b_f"], arrays["fox_q_norm_g"]
    m.fox_k_norm_g, m.conv_w, m.conv_b, m.conv_ln_g = arrays["fox_k_norm_g"], arrays["conv_w"], arrays["conv_b"], arrays["conv_ln_g"]
    m.conv_ln_b, m.pool_w, m.pool_scale, m.w_out = arrays["conv_ln_b"], arrays["pool_w"], arrays["pool_scale"], arrays["w_out"]
    m.norm2_g, m.router_wg, m.router_bg, m.router_we = arrays["norm2_g"], arrays["router_wg"], arrays["router_bg"], arrays["router_we"]
    m.router_be, m.exp_w_gate, m.exp_w_up, m.exp_w_down = arrays["router_be"], arrays["exp_w_gate"], arrays["exp_w_up"], arrays["exp_w_down"]
    m.y_prompt, m.y_sample, m.k_prompt, m.v_prompt = arrays["y_prompt"], arrays["y_sample"], arrays["k_prompt"], arrays["v_prompt"]
    m.logf_prompt, m.k_sample, m.v_sample, m.logf_sample = arrays["logf_prompt"], arrays["k_sample"], arrays["v_sample"], arrays["logf_sample"]
    m.gla_prompt, m.gla_sample, m.conv_prompt, m.conv_sample = arrays["gla_prompt"], arrays["gla_sample"], arrays["conv_prompt"], arrays["conv_sample"]
    m.pool_prompt, m.pool_sample = arrays["pool_prompt"], arrays["pool_sample"]
    m.h2d = nc.dram_tensor("normed_rows", (TOK, D), F32, kind="Internal").ap()
    m.slot_tok = nc.dram_tensor("slot_tokens", (SLOT_TILES * P, 1), I32, kind="Internal").ap()
    m.yd = nc.dram_tensor("slot_rows", (SLOT_TILES * P, D), F32, kind="Internal").ap()
    program(nc, m)


def kernel(**inputs):
    import numpy as np
    import concourse.bacc as bacc
    from concourse.bass_utils import run_bass_kernel_spmd

    nc = bacc.Bacc("TRN2", target_bir_lowering=False, num_devices=1)
    arrays, handles = {}, {}
    for name, a in inputs.items():
        arrays["in_" + name] = np.ascontiguousarray(a)
        handles[name] = nc.dram_tensor("in_" + name, arrays["in_" + name].shape, mybir.dt.from_np(arrays["in_" + name].dtype),
                                       kind="ExternalInput").ap()
    for name, shape in OUTS:
        handles[name] = nc.dram_tensor("out_" + name, shape, F32, kind="ExternalOutput").ap()
    build(nc, handles)
    r = run_bass_kernel_spmd(nc, [arrays], core_ids=[0])
    return tuple(r.results[0]["out_" + name] for name, _ in OUTS)
```

```python
from contextlib import ExitStack

import concourse.bass as bass
from concourse import mybir
from concourse.bass import ds

F32 = mybir.dt.float32
F32R = mybir.dt.float32r
I32 = mybir.dt.int32
ALU = mybir.AluOpType
ACT = mybir.ActivationFunctionType
AX = mybir.AxisListType

P = 128
D = 1024
KC = D // P
SEQ = 1024
DEC_B, DEC_L = 8, 4
NS = DEC_B * DEC_L
TOK = SEQ + NS
NT = SEQ // P + 1
W = 256
H, HD = 4, 64
RANK = 16
TAU = 16.0
TAPS = 31
PMAX = 16
WINDOWS = (2, 4, 8, 16)
PAGE = 128
NPG = 16
POOLPG = 160
PAST = NPG * PAGE
EPS = 1e-6
NEG = -1e30
NE, NG = 16, 4
DE = 512
SLOT_TILES = (2 * TOK) // P + NE
LEAST_PAIRS = (-(-2 * TOK // P) + 1) // 2
CH = 352
NCH = TOK // CH

GQ, GK, GV, GG, GA, FQ, FK, FV, FF, CA, CB, PU = 0, 256, 512, 768, 1024, 1040, 1296, 1552, 1808, 1812, 2068, 2324
N_IN = PU + W
Z_GROUPS = (GQ, GK, GG, FQ, FK, CA, CB, PU)
Z_ORDER = (5, 6, 3, 4, 0, 1, 2, 7)
ZQ, ZK, ZG, ZFQ, ZFK, ZCA, ZCB, ZPU = range(0, 16, 2)
FROW = 32


class Memory:
    pass


def next_address(nc):
    return -(-nc.sbuf_base // 32) * 32


def rows_of(t):
    return P if t < NT - 1 else NS


def constants(nc, m):
    with nc.Block() as block:

        @block.gpsimd
        def _(e):
            for t, v in ((m.ident, 0.0), (m.ones, 1.0), (m.headmean, 0.0), (m.chmean, 1.0 / W),
                         (m.causal, 1.0), (m.strict, 1.0), (m.qmask, 0.0), (m.sampmask, 1.0),
                         (m.carry, 1.0), (m.pagesel, 1.0), (m.reset, 1.0),
                         (m.poolw, 0.0), (m.eps, EPS)):
                e.memset(t[:], v)
            e.drain()
            for i in range(2):
                e.memset(m.headmean[64 * i:64 * i + 64, 64 * i:64 * i + 64], 1.0 / HD)
                e.drain()
            e.memset(m.reset[:, 0:SEQ].rearrange("p (c t) -> p c t", t=P)[:, :, 0:1], 0.0)
            e.memset(m.reset[:, SEQ:TOK].rearrange("p (c t) -> p c t", t=DEC_L)[:, :, 0:1], 0.0)
            e.drain()
            e.affine_select(out=m.ident[:], in_=m.ident[:], compare_op=ALU.not_equal, fill=1.0, base=0,
                            pattern=[[-1, P]], channel_multiplier=1)
            e.drain()
            e.affine_select(out=m.causal[:], in_=m.causal[:], compare_op=ALU.is_ge, fill=0.0, base=0,
                            pattern=[[1, P]], channel_multiplier=-1)
            e.drain()
            e.affine_select(out=m.strict[:], in_=m.strict[:], compare_op=ALU.is_gt, fill=0.0, base=0,
                            pattern=[[1, P]], channel_multiplier=-1)
            e.drain()
            e.affine_select(out=m.qmask[:], in_=m.qmask[:], compare_op=ALU.is_ge, fill=NEG, base=0,
                            pattern=[[-1, P]], channel_multiplier=1)
            e.drain()
            e.affine_select(out=m.sampmask[:], in_=m.sampmask[:], compare_op=ALU.is_ge, fill=0.0, base=0,
                            pattern=[[1, NS]], channel_multiplier=-1)
            e.drain()
            e.affine_select(out=m.carry[:], in_=m.carry[:], compare_op=ALU.is_gt, fill=0.0, base=0,
                            pattern=[[1, P]], channel_multiplier=-1)
            e.drain()
            e.affine_select(out=m.pagesel[:], in_=m.pagesel[:], compare_op=ALU.is_ge, fill=0.0, base=0,
                            pattern=[[-NPG, DEC_B], [0, DEC_L]], channel_multiplier=1)
            e.drain()
            e.iota(m.tok_id[:], pattern=[[P, NT]], base=0, channel_multiplier=1)
            e.iota(m.exp_id_i[:], pattern=[[0, NT], [1, NE]], base=0, channel_multiplier=0)
            e.iota(m.tile_id_i[:], pattern=[[1, SLOT_TILES]], base=0, channel_multiplier=0)
            e.iota(m.count_i[:], pattern=[[1, PMAX]], base=1, channel_multiplier=0)
            e.drain()
            e.affine_select(out=m.pagesel[:], in_=m.pagesel[:], compare_op=ALU.is_ge, fill=0.0, base=NPG - 1,
                            pattern=[[NPG, DEC_B], [0, DEC_L]], channel_multiplier=-1)
            e.drain()
            e.affine_select(out=m.sampmask[:], in_=m.sampmask[:], compare_op=ALU.is_ge, fill=0.0, base=0,
                            pattern=[[-DEC_L, DEC_B], [0, DEC_L]], channel_multiplier=1)
            e.drain()
            e.affine_select(out=m.carry[:], in_=m.carry[:], compare_op=ALU.is_ge, fill=0.0, base=0,
                            pattern=[[-NPG, DEC_B], [0, NPG]], channel_multiplier=1)
            e.drain()
            e.tensor_copy(m.exp_id[:], m.exp_id_i[:])
            e.tensor_copy(m.tile_id[:], m.tile_id_i[:])
            e.tensor_copy(m.count[:], m.count_i[:])

        @block.scalar
        def _(e):
            for t in range(4):
                e.dma_start(m.xt[t], m.x_prompt[0, t * P:(t + 1) * P, :]).then_inc(m.x_in[t], 16)
                if t == 1:
                    w_rows = m.w_in[0].rearrange("(p k) n -> p k n", k=KC)
                    e.dma_start(m.wv[:, :, 0:W], w_rows[:, :, GV:GV + W]).then_inc(m.wv_in, 16)
                    e.dma_start(m.wv[:, :, W:2 * W], w_rows[:, :, FV:FV + W]).then_inc(m.wv_in, 16)

        @block.sync
        def _(e):
            loads = [
                (m.g1[:], m.norm1_g[0].rearrange("(p k) -> p k", k=KC)),
                (m.g2[:], m.norm2_g[0].rearrange("(p k) -> p k", k=KC)),
                (m.gla_g[:], m.gla_norm_g[0].rearrange("(c p) -> p c", p=P)),
                (m.gla_b[:], m.gla_b_a[0].rearrange("(c p) -> p c", p=P)),
                (m.cb[:], m.conv_b[0].rearrange("(c p) -> p c", p=P)),
                (m.ln_g[:], m.conv_ln_g[0].rearrange("(c p) -> p c", p=P)),
                (m.ln_b[:], m.conv_ln_b[0].rearrange("(c p) -> p c", p=P)),
                (m.pscale[:], m.pool_scale[0].rearrange("(c p) -> p c", p=P)),
                (m.wa2[:], m.gla_w_a2[0]),
                (m.tapw[:], m.conv_w[0]),
                (m.fb[FROW:FROW + H, :], m.fox_b_f[0].rearrange("(h a) -> h a", a=1)),
                (m.wr[:, :, 0:NG], m.router_wg[0].rearrange("(p k) n -> p k n", k=KC)),
                (m.wr[:, :, NG:NG + NE], m.router_we[0].rearrange("(p k) n -> p k n", k=KC)),
                (m.rb[:, 0:NG], m.router_bg[0].partition_broadcast(P)),
                (m.rb[:, NG:NG + NE], m.router_be[0].partition_broadcast(P)),
                (m.pages[:], m.page_table.rearrange("b g -> (b g)").rearrange("(a n) -> a n", a=1)),
                (m.pages_col[:], m.page_table.rearrange("b g -> (b g)").rearrange("(n a) -> n a", a=1)),
            ]
            for i in range(2):
                loads.append((m.fqg[64 * i:64 * i + 64, :], m.fox_q_norm_g[0].rearrange("(p a) -> p a", a=1)))
                loads.append((m.fkg[64 * i:64 * i + 64, :], m.fox_k_norm_g[0].rearrange("(p a) -> p a", a=1)))
            for to, of in loads:
                e.dma_start(to, of, allow_slow_non_contiguous=True).then_inc(m.s_param, 16)
            m.n_params = len(loads)
            e.wait_ge(m.s_param, 16 * m.n_params)

    with nc.Block() as block:

        @block.sync
        def _(e):
            for g in range(4):
                o = HD * (g % 2)
                e.dma_start(m.poolw[o:o + HD, g // 2, o:o + HD], m.pool_w[0, g]).then_inc(m.s_param, 16)
            e.wait_ge(m.s_param, 16 * (m.n_params + 4))

        @block.vector
        def _(e):
            e.tensor_scalar(m.fqg8[:], m.fqg[:], HD ** -0.5, None, ALU.mult)


def products(e, out, pairs):
    for k, (a_hi, a_lo, b_hi, b_lo) in enumerate(pairs):
        for n, (a, b) in enumerate(((a_hi, b_hi), (a_hi, b_lo), (a_lo, b_hi))):
            i = e.matmul(out, a, b, start=(k == n == 0), stop=(k == len(pairs) - 1 and n == 2))
    return i


def projections(nc, m):
    ctx = ExitStack()
    sb = lambda name, shape: ctx.enter_context(nc.sbuf_tensor(name, shape, F32))
    sbr = lambda name, shape: ctx.enter_context(nc.sbuf_tensor(name, shape, F32R))
    sem = lambda name: ctx.enter_context(nc.semaphore(name))
    NB1 = TAPS - 1
    ps = m.ps
    with ctx:
        over = lambda name, shape, at: nc.alloc_sbuf_tensor_at(name, shape, F32R, offset=at)
        hT_hi = over("hT_hi", [P, KC, TOK], m.mixT_at)
        hT_at = next_address(nc)
        hT = sb("hT", [P, KC, TOK])
        hT_lo = over("hT_lo", [P, KC, TOK], hT_at)
        ssq = sb("ssq", [P, 4])
        std = sb("std", [P, 4])
        rstd = sb("rstd", [P, 4])
        wz_at = next_address(nc)
        wz = sb("wz", [P, 3, KC, P])
        wz_lo, wz_hi = over("wz_lo", [P, 3, KC, P], wz_at), sbr("wz_hi", [P, 2, KC, P])
        wsm_at = next_address(nc)
        wsm = sb("wsm", [P, KC, FROW + H])
        wsm_lo, wsm_hi = over("wsm_lo", [P, KC, FROW + H], wsm_at), sbr("wsm_hi", [P, KC, FROW + H])
        hsq = sb("head_sq", [P, 2, CH])
        us = sb("us", [P, 2, DEC_B, NB1 + DEC_L])
        cst = sb("cst", [DEC_B // 2 * NB1, 2, W])
        tapT = sb("tapT", [P, 2, TAPS])
        hstd = sb("head_std", [P, 2, CH])
        ctail = cst[0:NS]
        junk, zrow = m.Z[:, ZCA, 0:D], m.Z[:, ZPU + 1, 0:D]
        xt, wv = m.xt, m.wv
        hn = m.Z[:, ZPU:ZPU + 2, 0:D]
        wv_lo = over("wv_lo", [P, KC, 2 * W], m.Z_at + 4 * ZFQ * TOK)
        wv_hi = over("wv_hi", [P, KC, 2 * W], m.Z_at + 4 * ZQ * TOK)
        wtmp = m.Z[:, ZPU, 0:DEC_L * DEC_B * TAPS].rearrange("p (l b k) -> p l b k", l=DEC_L, b=DEC_B)
        lstd = m.Z[:, ZPU, :]
        u, y = m.Z[:, ZCA:ZCA + 2, :], m.Z[:, ZCB:ZCB + 2, :]
        ysq = u
        ps_t, ps_v, ps_z = m.ps[:, 0:2, :], m.ps[:, 2:4, :], m.ps[:, 4:8, :]

        std_ready, normed, turned, ht_ready, ht_read = sem("std_ready"), sem("normed"), sem("turned"), sem("ht_ready"), sem("ht_read")
        x_in, wv_in, small_in = m.x_in, m.wv_in, sem("small_in")
        w_hi, w_lo = sem("w_hi"), sem("w_lo")
        rows_mm, rows_out = sem("rows_mm"), sem("rows_out")
        v_done, v_out, v_stored = sem("v_done"), sem("v_out"), sem("v_stored")
        wz_in = [sem(f"wz_in{i}") for i in range(3)]
        z_done, z_out = sem("z_done"), sem("z_out")
        sig, u_ready, y_done = sem("sig"), sem("u_ready"), sem("y_done")
        l_mean, l_sub, l_scaled, n_norm = sem("ln_mean"), sem("ln_sub"), sem("ln_scaled"), sem("n_norm")
        squares, meansq, roots = sem("squares"), sem("meansq"), sem("roots")

        w_rows = m.w_in[0].rearrange("(p k) n -> p k n", k=KC)
        NZ = len(Z_ORDER)
        PER = 2 * NCH
        ALL = NZ * PER + NCH
        cols = lambda n: slice(n * CH, (n + 1) * CH)
        filled = lambda tile: (Z_ORDER.index(tile // 2) + 1) * PER

        SIG_AT, TAIL_AT, MEAN_AT, VAR_AT, NORM_AT = 2 * PER, 2 * PER + 4, 36, 38, 37
        fox_norms = [(z, g, n) for z, g in ((ZFQ, m.fqg8[:]), (ZFQ + 1, m.fqg8[:]), (ZFK, m.fkg[:]), (ZFK + 1, m.fkg[:]))
                     for n in range(NCH)]
        NN = len(fox_norms)
        assert NORM_AT >= filled(ZFK) and NORM_AT + NN < ALL and VAR_AT + 1 < (NZ - 1) * PER
        tapped = [(k, c) for k in reversed(range(TAPS)) for c in range(2)]

        splits = [(wv_hi[:, :, c], wv_lo[:, :, c], wv[:, :, c]) for c in (slice(0, W), slice(W, 2 * W))]
        splits += [(wsm_hi[:], wsm_lo[:], wsm[:])]
        splits += [(wz_hi[:, f % 2], wz_lo[:, f % 3], wz[:, f % 3]) for f in range(2 * NZ)]

        with nc.Block() as block:

            @block.sync
            def _(e):
                for t in range(4, NT):
                    r = rows_of(t)
                    e.wait_ge(normed, t - 3)
                    src = m.x_prompt[0, t * P:(t + 1) * P, :] if t < NT - 1 else m.x_sample.rearrange("b l d -> (b l) d")
                    e.dma_start(xt[t % 4][0:r, :], src).then_inc(x_in[t % 4], 16)
                for f in range(2 * NZ):
                    c = Z_GROUPS[Z_ORDER[f // 2]] + f % 2 * P
                    if f >= 3:
                        e.wait_ge(z_done, NCH * (f - 2))
                    e.dma_start(wz[:, f % 3, :, :], w_rows[:, :, c:c + P]).then_inc(wz_in[f % 3], 16)
                for t in range(NT):
                    r = rows_of(t)
                    e.wait_ge(v_out, t + 1)
                    to = m.v_prompt[0, 0, t * P:(t + 1) * P] if t < NT - 1 else m.v_sample[0].rearrange("b l h d -> (b l) h d")
                    e.dma_start(to.rearrange("p h d -> p (h d)"), m.V[0:r, t, W:2 * W]).then_inc(v_stored, 16)
                e.wait_ge(rows_out, 2)
                e.dma_start(m.conv_prompt[0, 0], ctail[NS - NB1:NS, 0, :]).then_inc(v_stored, 16)
                for b in range(DEC_B):
                    e.dma_start(m.conv_sample[0, b, NB1 - DEC_L:NB1, :], ctail[DEC_L * b:DEC_L * b + DEC_L, 1, :]).then_inc(v_stored, 16)
                e.wait_ge(v_stored, 16 * (NT + 1 + DEC_B))

            @block.gpsimd
            def _(e):
                for g in range(2):
                    e.dma_start(cst[:, g, :], m.state_conv[0, g * (DEC_B // 2):(g + 1) * (DEC_B // 2)].rearrange("b t c -> (b t) c")).then_inc(small_in, 16)
                e.memset(wsm[:], 0.0)
                e.drain()
                e.dma_start(wsm[:, :, 0:RANK], w_rows[:, :, GA:GA + RANK]).then_inc(small_in, 16)
                e.dma_start(wsm[:, :, FROW:FROW + H], w_rows[:, :, FF:FF + H]).then_inc(small_in, 16)
                for i, (hi, lo, whole) in enumerate(splits):
                    if i == 1:
                        continue
                    if i == 3:
                        e.wait_ge(turned, NT)
                        e.memset(zrow, 0.0)
                        e.drain()
                    if 5 <= i < 5 + SLOT_TILES - 2 * LEAST_PAIRS:
                        t = 2 * LEAST_PAIRS + i - 5
                        e.dma_start(m.yd[t * P:(t + 1) * P, :], zrow).then_inc(m.s_zero_rows, 16)
                    e.wait_ge(w_hi, i + 1)
                    e.tensor_tensor(lo, whole, hi.bitcast(F32), ALU.subtract).then_inc(w_lo, 1)

            @block.scalar
            def _(e):
                def square(t):
                    r, b = rows_of(t), t % 4
                    e.wait_ge(x_in[b], 16 * (t // 4 + 1))
                    if t >= 4:
                        e.wait_ge(normed, t - 3)
                    e.activation(junk[0:r], xt[b][0:r, :], ACT.Square, scale=D ** -0.5, accum_out=ssq[0:r, b:b + 1])
                    e.drain()
                    e.activation(std[0:r, b:b + 1], ssq[0:r, b:b + 1], ACT.Sqrt, bias=m.eps[0:r, :]).then_inc(std_ready, 1)

                def high(i):
                    hi, _, whole = splits[i]
                    e.copy(hi, whole).then_inc(w_hi, 1)

                def high_z(f):
                    e.wait_ge(wz_in[f % 3], 16 * (f // 3 + 1))
                    high(3 + f)

                for t in range(3):
                    square(t)
                e.wait_ge(wv_in, 32)
                high(0)
                high(1)
                for t in range(NT):
                    if t + 3 < NT:
                        square(t + 3)
                    if t == NT - 3:
                        e.wait_ge(small_in, 64)
                        high(2)
                        high_z(0)
                        high_z(1)
                    r = rows_of(t)
                    e.wait_ge(v_done, t + 1)
                    e.copy(m.V[0:r, t, :], ps_v[0:r, t % 2, :]).then_inc(v_out, 1)
                e.drain()
                for n in range(ALL):
                    e.wait_ge(z_done, n + 1)
                    if n < NZ * PER:
                        z = 2 * Z_ORDER[n // PER] + n % PER // NCH
                        if n == (NZ - 1) * PER:
                            e.wait_ge(l_scaled, NCH)
                        if n == (NZ - 1) * PER + NCH:
                            e.wait_ge(m.s_zero_rows, 16 * (SLOT_TILES - 2 * LEAST_PAIRS))
                        e.copy(m.Z[:, z, cols(n % NCH)], ps_z[:, n % 4, 0:CH]).then_inc(z_out, 1)
                    else:
                        e.copy(m.ZS[:, cols(n % NCH)], ps_z[0:FROW + H, n % 4, 0:CH]).then_inc(z_out, 1)
                    if n % NCH == NCH - 1 and n // NCH + 2 < 2 * NZ:
                        high_z(n // NCH + 2)
                    if n + 1 == SIG_AT:
                        e.drain()
                        e.activation(y, y, ACT.Sigmoid).then_inc(sig, 1)
                    if n == MEAN_AT:
                        for i in range(NCH):
                            e.wait_ge(l_sub, i + 1)
                            e.activation(ysq[:, :, cols(i)], y[:, :, cols(i)], ACT.Square).then_inc(squares, 1)
                    if n == VAR_AT:
                        for i in range(NCH):
                            e.wait_ge(meansq, i + 1)
                            e.activation(lstd[:, cols(i)], ps[:, 1 + i, 0:CH], ACT.Sqrt, bias=m.eps[:, :]).then_inc(roots, 1)
                    if NORM_AT <= n + 1 < NORM_AT + NN:
                        i = n + 1 - NORM_AT
                        z, g, k = fox_norms[i]
                        if i >= 2:
                            e.wait_ge(meansq, NCH + i - 1)
                        e.activation(hsq[:, i % 2, :], m.Z[:, z, cols(k)], ACT.Square).then_inc(squares, 1)
                    if NORM_AT + 1 <= n < NORM_AT + 1 + NN:
                        i = n - NORM_AT - 1
                        e.wait_ge(meansq, NCH + i + 1)
                        if i >= 2:
                            e.wait_ge(n_norm, i - 1)
                        e.activation(hstd[:, i % 2, :], ps[:, i % 2, 0:CH], ACT.Sqrt, bias=m.eps[:, :]).then_inc(roots, 1)

            @block.vector
            def _(e):
                def norm(t):
                    r, b = rows_of(t), t % 4
                    e.wait_ge(std_ready, t + 1)
                    e.reciprocal(rstd[0:r, b:b + 1], std[0:r, b:b + 1])
                    e.drain()
                    if t >= 2:
                        e.wait_ge(turned, t - 1)
                    e.tensor_scalar(hn[0:r, t % 2, :], xt[b][0:r, :], rstd[0:r, b:b + 1], None, ALU.mult).then_inc(normed, 1)

                norm(0)
                hi, lo, whole = splits[1]
                e.wait_ge(w_hi, 2)
                e.tensor_tensor(lo, whole, hi.bitcast(F32), ALU.subtract).then_inc(w_lo, 1)
                for t in range(NT):
                    if t + 1 < NT:
                        norm(t + 1)
                    r = rows_of(t)
                    e.wait_ge(turned, t + 1)
                    for c in range(2):
                        g = m.g1[:, 4 * c:4 * c + 4].unsqueeze(2).broadcast_to([P, 4, r])
                        to = (slice(None), slice(4 * c, 4 * c + 4), slice(t * P, t * P + r))
                        turned_x = ps_t[:, c, :].rearrange("p (k t) -> p k t", k=4)[:, :, 0:r]
                        e.tensor_tensor(hT[to], turned_x, g, ALU.mult)
                        e.tensor_tensor(hT_hi[to], turned_x, g, ALU.mult)
                    e.drain().then_inc(ht_read, 1)
                    to = (slice(None), slice(None), slice(t * P, t * P + r))
                    e.tensor_tensor(hT_lo[to], hT[to], hT_hi[to].bitcast(F32), ALU.subtract).then_inc(ht_ready, 1)
                    if t == 0:
                        e.wait_ge(rows_mm, 1)
                        e.tensor_copy(tapT[:], ps_z[:, 0, 0:2 * TAPS].rearrange("p (c k) -> p c k", c=2))
                        for g in range(2):
                            for c in range(2):
                                i = e.tensor_copy(us[:, c, g * 4:g * 4 + 4, 0:NB1],
                                                  ps_z[:, 1, (2 * g + c) * 4 * NB1:(2 * g + c + 1) * 4 * NB1].rearrange("p (b t) -> p b t", t=NB1))
                        i.then_inc(rows_out, 1)
                e.wait_ge(sig, 1)
                e.wait_ge(z_out, SIG_AT)
                e.tensor_tensor(u, u, y, ALU.mult)
                e.drain().then_inc(u_ready, 1)
                for c in range(2):
                    e.tensor_copy(us[:, c, :, NB1:], u[:, c, SEQ:TOK].rearrange("p (b l) -> p b l", l=DEC_L))
                for k, c in tapped:
                    lag = NB1 - k
                    if lag == 0:
                        e.tensor_scalar(y[:, c, 0:SEQ], u[:, c, 0:SEQ], tapT[:, c, k:k + 1], m.cb[:, c:c + 1], ALU.mult, ALU.add)
                    else:
                        e.scalar_tensor_tensor(out=y[:, c, lag:SEQ], in0=u[:, c, 0:SEQ - lag], scalar=tapT[:, c, k:k + 1],
                                               in1=y[:, c, lag:SEQ], op0=ALU.mult, op1=ALU.add)
                    if c == 1:
                        e.drain()
                for c in range(2):
                    for l in range(DEC_L):
                        e.tensor_tensor(wtmp[:, l], us[:, c, :, l:l + TAPS], tapT[:, c, :].unsqueeze(1).broadcast_to([P, DEC_B, TAPS]), ALU.mult)
                    e.drain()
                    for l in range(DEC_L):
                        e.tensor_reduce(y[:, c, SEQ:TOK].rearrange("p (b l) -> p l b", l=DEC_L)[:, l], wtmp[:, l], AX.X, ALU.add)
                    e.drain()
                    i = e.tensor_scalar(y[:, c, SEQ:TOK], y[:, c, SEQ:TOK], m.cb[:, c:c + 1], None, ALU.add)
                i.then_inc(y_done, 1)
                e.wait_ge(rows_mm, 2)
                e.tensor_copy(ctail[:, 0, :], ps[0:NS, 3, 0:W])
                e.tensor_copy(ctail[:, 1, :], ps[0:NS, 3, W:2 * W]).then_inc(rows_out, 1)
                for n in range(NCH):
                    e.wait_ge(l_mean, n + 1)
                    for c in range(2):
                        i = e.tensor_tensor(y[:, c, cols(n)], y[:, c, cols(n)], ps[:, n, 0:CH], ALU.subtract)
                    i.then_inc(l_sub, 1)
                for n in range(NCH):
                    e.wait_ge(roots, n + 1)
                    e.reciprocal(lstd[:, cols(n)], lstd[:, cols(n)])
                    e.drain()
                    for c in range(2):
                        i = e.scalar_tensor_tensor(out=y[:, c, cols(n)], in0=y[:, c, cols(n)], scalar=m.ln_g[:, c:c + 1], in1=lstd[:, cols(n)],
                                                   op0=ALU.mult, op1=ALU.mult)
                    i.then_inc(l_scaled, 1)
                for i, (z, g, k) in enumerate(fox_norms):
                    e.wait_ge(roots, NCH + i + 1)
                    e.reciprocal(hstd[:, i % 2, :], hstd[:, i % 2, :])
                    e.drain()
                    e.scalar_tensor_tensor(out=m.Z[:, z, cols(k)], in0=m.Z[:, z, cols(k)], scalar=g,
                                           in1=hstd[:, i % 2, :], op0=ALU.mult, op1=ALU.mult).then_inc(n_norm, 1)

            @block.tensor
            def _(e):
                def turn(t):
                    r = rows_of(t)
                    e.wait_ge(normed, t + 1)
                    if t >= 1:
                        e.wait_ge(ht_read, t)
                    for k in range(KC):
                        i = e.transpose(ps_t[:, k // 4, k % 4 * P:k % 4 * P + r], hn[0:r, t % 2, k:D:KC], m.ident[0:r, 0:r])
                    i.then_inc(turned, 1)

                turn(0)
                for c in range(2):
                    e.transpose(ps_z[:, 0, c * TAPS:(c + 1) * TAPS], m.tapw[:, c * P:c * P + P], m.ident[0:TAPS, 0:TAPS])
                e.wait_ge(small_in, 64)
                for g in range(2):
                    for c in range(2):
                        i = e.transpose(ps_z[:, 1, (2 * g + c) * 4 * NB1:(2 * g + c + 1) * 4 * NB1], cst[:, g, c * P:c * P + P],
                                        m.ident[0:4 * NB1, 0:4 * NB1])
                i.then_inc(rows_mm, 1)
                e.wait_ge(w_lo, 2)
                for t in range(NT):
                    if t + 1 < NT:
                        turn(t + 1)
                    r = rows_of(t)
                    e.wait_ge(ht_ready, t + 1)
                    if t >= 2:
                        e.wait_ge(v_out, t - 1)
                    tt = slice(t * P, t * P + r)
                    products(e, ps_v[0:r, t % 2, :], [(hT_hi[:, k, tt], hT_lo[:, k, tt], wv_hi[:, k, :], wv_lo[:, k, :])
                                                      for k in range(KC)]).then_inc(v_done, 1)
                e.wait_ge(rows_out, 1)
                for n in range(ALL):
                    f, c, b = n // NCH, n % NCH, n % 4
                    if n == TAIL_AT:
                        e.wait_ge(u_ready, 1)
                        e.wait_ge(v_out, NT)
                        for i in range(2):
                            e.transpose(ps[0:NS, 3, i * P:i * P + P], u[:, i, SEQ - NS:SEQ], m.ident[:])
                            mm = e.transpose(ps[0:NS, 3, W + i * P:W + i * P + P], u[:, i, SEQ:TOK], m.ident[:])
                        mm.then_inc(rows_mm, 1)
                    if n == MEAN_AT:
                        e.wait_ge(y_done, 1)
                        for i in range(NCH):
                            for j in range(2):
                                mm = e.matmul(ps[:, i, 0:CH], m.chmean[:], y[:, j, cols(i)], start=(j == 0), stop=(j == 1))
                            mm.then_inc(l_mean, 1)
                    if n == VAR_AT:
                        e.wait_ge(rows_out, 2)
                        for i in range(NCH):
                            e.wait_ge(squares, i + 1)
                            e.wait_ge(l_sub, min(i + 2, NCH))
                            for j in range(2):
                                mm = e.matmul(ps[:, 1 + i, 0:CH], m.chmean[:], ysq[:, j, cols(i)], start=(j == 0), stop=(j == 1))
                            mm.then_inc(meansq, 1)
                    if NORM_AT + 1 <= n < NORM_AT + 1 + NN:
                        i = n - NORM_AT - 1
                        e.wait_ge(squares, NCH + i + 1)
                        if i == 1:
                            e.wait_ge(roots, NCH)
                        if i >= 2:
                            e.wait_ge(roots, NCH + i - 1)
                        e.matmul(ps[:, i % 2, 0:CH], m.headmean[:], hsq[:, i % 2, :], start=True, stop=True).then_inc(meansq, 1)
                    if f < 2 * NZ:
                        hi, lo, rows = wz_hi[:, f % 2], wz_lo[:, f % 3], P
                        if c == 0:
                            e.wait_ge(w_lo, 3 + f + 1)
                    else:
                        hi, lo, rows = wsm_hi, wsm_lo, FROW + H
                    if n >= 4:
                        e.wait_ge(z_out, n - 3)
                    products(e, ps_z[0:rows, b, 0:CH], [(hi[:, k, :], lo[:, k, :], hT_hi[:, k, cols(c)], hT_lo[:, k, cols(c)])
                                                        for k in range(KC)]).then_inc(z_done, 1)


def log_sigmoid_act(e, x, t):
    e.activation(t, x, ACT.Abs)
    e.drain()
    e.activation(t, t, ACT.Exp, scale=-1.0)
    e.drain()
    return e.activation(t, t, ACT.Ln, bias=1.0)


def gla_pool_norms(nc, m):
    ctx = ExitStack()
    sb = lambda name, shape: ctx.enter_context(nc.sbuf_tensor(name, shape, F32))
    sem = lambda name: ctx.enter_context(nc.semaphore(name))
    NC = NT - 1 + DEC_B
    QE, KE = m.Z[:, ZQ:ZQ + 2, :], m.Z[:, ZK:ZK + 2, :]
    ps = m.ps
    with ctx:
        la, bsum, tmp = sb("la", [P, 2, TOK]), sb("bsum", [P, 2, TOK]), sb("tmp", [P, 2, TOK])
        mid, last, dlm = sb("mid", [P, 2, NC]), sb("last", [P, 2, NC]), sb("dlm", [P, 2, NC])
        e_mid, e_last, e_dlm = sb("e_mid", [P, 2, NC]), sb("e_last", [P, 2, NC]), sb("e_dlm", [P, 2, NC])
        keT = sb("keT", [P, NT, W])
        at = sb("at", [P, 2, 2, 2, P])
        S, Ssc, Stmp = sb("S", [P, 2, P]), sb("Ssc", [P, 2, P]), sb("Stmp", [P, 2, 4, HD])
        SS = sb("SS", [P, 2, DEC_B, P])
        sq, std, rec = sb("gla_sq", [P, 2, CH]), sb("gla_std", [P, 2, CH]), sb("gla_rec", [P, 2, CH])
        tailT = sb("tailT", [2 * NS, W])
        kout = m.mixT[:, 0:2, :].rearrange("p c t -> p (c t)")[:, 0:(NT - 1) * W].rearrange("p (t d) -> p t d", d=W)
        ksamp = sb("ksamp", [NS, W])
        pxs, pas, pbs = (sb(n, [P, 2, DEC_B, PMAX + DEC_L]) for n in ("pxs", "pas", "pbs"))
        pst = sb("pst", [DEC_B * (PMAX - 1), W])
        rcount = sb("rcount", [P, 2, PMAX])
        fx = m.ZS
        ft = m.CF
        SSsc = bsum[:].rearrange("p c t -> p (c t)")[:, 0:2 * DEC_B * P].rearrange("p (c b e) -> p c b e", c=2, b=DEC_B)
        vmask = tmp[:].rearrange("p c t -> p (c t)")[0:NS, 0:DEC_B * W].rearrange("p (b e) -> p b e", b=DEC_B)
        pa, pb, px = (m.mixT[:, c:c + 2, 0:PMAX + SEQ] for c in (2, 4, 6))

        n_sq, n_ms, n_std, n_norm = sem("n_sq"), sem("n_ms"), sem("n_std"), sem("n_norm")
        la_mm, la_x, la_t, la_d, la_e, la_s, qk_ready = (sem(n) for n in ("la_mm", "la_x", "la_t", "la_d", "la_e", "la_s", "qk_ready"))
        f_x, f_t, f_c = sem("f_x"), sem("f_t"), sem("f_c")
        f_mm, f_out = sem("f_mm"), sem("f_out")
        kt_mm, kt_out, k_sent = sem("kt_mm"), sem("kt_out"), sem("k_sent")
        ket_mm, ket_out = sem("ket_mm"), sem("ket_out")
        zeroed, st_in = sem("zeroed"), sem("st_in")
        a_mm, a_out, o_mm, o_out, s_mm, s_out, s_sc = (sem(n) for n in ("a_mm", "a_out", "o_mm", "o_out", "s_mm", "s_out", "s_sc"))
        ss_sc, vm_ready = sem("ss_sc"), sem("vm_ready")
        silu, stored = sem("silu"), sem("stored")
        turn_mm, turn_out, p_d, p_diff, p_mm, p_out = (sem(n) for n in ("turn_mm", "turn_out", "p_d", "p_diff", "p_mm", "p_out"))

        def tiles(x):
            return (x[:, :, 0:SEQ].rearrange("p c (n t) -> p c n t", t=P),
                    x[:, :, SEQ:TOK].rearrange("p c (n t) -> p c n t", t=DEC_L))

        GLA_NORMS = [(ZQ, m.gla_g[:, 0:1]), (ZQ + 1, m.gla_g[:, 1:2])]
        norm_steps = [(z, g, n) for z, g in GLA_NORMS for n in range(NCH)]
        cols = lambda n: slice(n * CH, (n + 1) * CH)

        def norm_square(e, i):
            z, g, n = norm_steps[i]
            if i >= 2:
                e.wait_ge(n_ms, i - 1)
            e.activation(sq[:, i % 2, :], m.Z[:, z, cols(n)], ACT.Square).then_inc(n_sq, 1)

        def norm_root(e, i):
            e.wait_ge(n_ms, i + 1)
            if i >= 2:
                e.wait_ge(n_norm, i - 1)
            e.activation(std[:, i % 2, :], ps[:, i % 2, 0:CH], ACT.Sqrt, bias=m.eps[:, :]).then_inc(n_std, 1)

        def norm_mean(e, i):
            e.wait_ge(n_sq, i + 1)
            if i >= 2:
                e.wait_ge(n_std, i - 1)
            e.matmul(ps[:, i % 2, 0:CH], m.headmean[:], sq[:, i % 2, :], start=True, stop=True).then_inc(n_ms, 1)

        def norm_scale(e, i):
            z, g, n = norm_steps[i]
            e.wait_ge(n_std, i + 1)
            e.reciprocal(rec[:, i % 2, :], std[:, i % 2, :])
            e.drain()
            e.scalar_tensor_tensor(out=m.Z[:, z, cols(n)], in0=m.Z[:, z, cols(n)], scalar=g,
                                   in1=rec[:, i % 2, :], op0=ALU.mult, op1=ALU.mult).then_inc(n_norm, 1)

        with nc.Block() as block:

            @block.sync
            def _(e):
                e.wait_ge(zeroed, 1)
                for h in range(H):
                    o = HD * (h % 2)
                    e.dma_start(SS[o:o + HD, h // 2, :, o:o + HD],
                                m.state_gla[0, :, h].rearrange("b d e -> d b e")).then_inc(st_in, 16)
                e.dma_start(pst[:], m.state_pool[0].rearrange("b t c -> (b t) c")).then_inc(st_in, 16)
                e.dma_start(m.conv_sample[0, :, 0:TAPS - 1 - DEC_L, :], m.state_conv[0, :, DEC_L:TAPS - 1, :]).then_inc(stored, 16)
                e.dma_start(m.pool_sample[0, :, 0:PMAX - 1 - DEC_L, :], m.state_pool[0, :, DEC_L:PMAX - 1, :]).then_inc(stored, 16)
                n = 2
                for t in range(NT):
                    r = rows_of(t)
                    e.wait_ge(kt_out, t + 1)
                    to = m.k_prompt[0, 0, t * P:(t + 1) * P] if t < NT - 1 else m.k_sample[0].rearrange("b l h d -> (b l) h d")
                    e.dma_start(to.rearrange("p h d -> p (h d)"), kout[:, t, :] if t < NT - 1 else ksamp[:]).then_inc(k_sent, 16)
                e.wait_ge(f_out, 1)
                e.dma_start(m.logf_prompt[0, 0].rearrange("(t p) h -> p t h", p=P), m.lft[:, 0:NT - 1, 0:H]).then_inc(stored, 16)
                e.dma_start(m.logf_sample[0].rearrange("b l h -> (b l) h"), m.lft[0:NS, NT - 1, 0:H]).then_inc(stored, 16)
                n += 2
                e.wait_ge(s_out, NT - 1)
                for h in range(H):
                    o = HD * (h % 2)
                    e.dma_start(m.gla_prompt[0, 0, h], S[o:o + HD, h // 2, o:o + HD]).then_inc(stored, 16)
                e.wait_ge(s_out, NT)
                for h in range(H):
                    o = HD * (h % 2)
                    e.dma_start(m.gla_sample[0, :, h].rearrange("b d e -> d b e"), SS[o:o + HD, h // 2, :, o:o + HD]).then_inc(stored, 16)
                e.wait_ge(turn_out, 2)
                e.dma_start(m.pool_prompt[0, 0], tailT[NS - PMAX + 1:NS, :]).then_inc(stored, 16)
                for b in range(DEC_B):
                    e.dma_start(m.pool_sample[0, b, PMAX - 1 - DEC_L:PMAX - 1, :],
                                tailT[NS + DEC_L * b:NS + DEC_L * b + DEC_L, :]).then_inc(stored, 16)
                n += 2 * H + 1 + DEC_B
                e.wait_ge(stored, 16 * n)
                e.wait_ge(k_sent, 16 * NT)

            @block.gpsimd
            def _(e):
                e.memset(SS[:], 0.0)
                e.memset(at[:], 0.0)
                e.memset(S[:], 0.0)
                e.drain().then_inc(zeroed, 1)
                e.memset(px[:, :, 0:PMAX], 0.0)
                e.memset(pxs[:, :, :, 0:1], 0.0)
                e.tensor_copy(px[:, :, PMAX:], m.Z[:, ZPU:ZPU + 2, 0:SEQ])
                e.tensor_copy(pxs[:, :, :, PMAX:], m.Z[:, ZPU:ZPU + 2, SEQ:TOK].rearrange("p c (b l) -> p c b l", l=DEC_L))
                e.wait_ge(turn_out, 1)
                e.drain()
                N, NB = PMAX + SEQ, PMAX + DEC_L
                for lo, c0, w, src, dst, ssrc, sdst in ((0, 0, 1, px, pa, pxs, pas), (64, 0, 2, pa, pb, pas, pbs),
                                                        (0, 1, 2, pa, pb, pas, pbs), (0, 1, 4, pb, pa, pbs, pas),
                                                        (64, 1, 8, pa, pb, pas, pbs)):
                    c1 = 2 if w == 1 else c0 + 1
                    j = 2 * w - 1
                    e.tensor_tensor(dst[lo:P, c0:c1, j:N], src[lo:P, c0:c1, j:N], src[lo:P, c0:c1, j - w:N - w], ALU.add)
                    e.drain()
                    e.tensor_tensor(sdst[lo:P, c0:c1, :, j:NB], ssrc[lo:P, c0:c1, :, j:NB],
                                    ssrc[lo:P, c0:c1, :, j - w:NB - w], ALU.add)
                    e.drain()
                e.drain().then_inc(p_d, 1)

            @block.scalar
            def _(e):
                e.wait_ge(la_x, 6)
                log_sigmoid_act(e, la[:], tmp[:]).then_inc(la_t, 1)
                e.wait_ge(f_x, 1)
                log_sigmoid_act(e, fx[FROW:FROW + H, :], ft[FROW:FROW + H, :]).then_inc(f_t, 1)
                for t in range(NT):
                    e.wait_ge(kt_mm, t + 1)
                    e.copy(kout[:, t, :] if t < NT - 1 else ksamp[:], ps[0:rows_of(t), t % 2, 0:W]).then_inc(kt_out, 1)
                e.wait_ge(la_s, 1)
                e.activation(e_mid[:], mid[:], ACT.Exp, scale=1.0 / TAU)
                e.activation(e_last[:], last[:], ACT.Exp, scale=1.0 / TAU)
                e.activation(e_dlm[:], dlm[:], ACT.Exp, scale=1.0 / TAU).then_inc(la_e, 1)
                e.wait_ge(la_d, 1)
                e.activation(la[:], tmp[:], ACT.Exp, scale=1.0 / TAU).then_inc(la_e, 1)
                e.drain()
                e.activation(tmp[:], tmp[:], ACT.Exp, scale=-1.0 / TAU).then_inc(la_e, 1)
                for n in range(6):
                    c, k = n // 3, n % 3
                    w0, w1 = ((0, 512), (512, SEQ), (SEQ, TOK))[k]
                    e.wait_ge(p_mm, n + 1)
                    e.activation(m.mixT[:, 6 + c, w0:w1], ps[:, n % 4, 0:w1 - w0], ACT.Copy, scale=m.pscale[:, c:c + 1]).then_inc(p_out, 1)
                for t in range(NT):
                    e.wait_ge(ket_mm, t + 1)
                    e.copy(keT[0:rows_of(t), t, :], ps[0:rows_of(t), 4 + t % 2, 0:W]).then_inc(ket_out, 1)
                for t in range(NT):
                    r = rows_of(t)
                    e.wait_ge(o_mm, t + 1)
                    e.copy(QE[:, :, t * P:t * P + r], ps[:, 4 + t % 2, 0:2 * P].rearrange("p (c t) -> p c t", c=2)[:, :, 0:r]).then_inc(o_out, 1)
                e.drain()
                for i in range(len(norm_steps) + 1):
                    if i < len(norm_steps):
                        norm_square(e, i)
                    if i:
                        norm_root(e, i - 1)
                e.activation(m.Z[:, ZG:ZG + 2, :], m.Z[:, ZG:ZG + 2, :], ACT.Silu).then_inc(silu, 1)

            @block.vector
            def _(e):
                for n in range(2 * NCH):
                    c = n // NCH
                    e.wait_ge(la_mm, n + 1)
                    e.tensor_scalar(la[:, c, cols(n % NCH)], ps[:, 2 + n % 2, 0:CH], m.gla_b[:, c:c + 1], None, ALU.add).then_inc(la_x, 1)
                e.tensor_scalar(fx[FROW:FROW + H, :], m.ZS[FROW:FROW + H, :], m.fb[FROW:FROW + H, :], None, ALU.add).then_inc(f_x, 1)
                e.wait_ge(turn_mm, 1)
                for c in range(2):
                    i = e.tensor_copy(pxs[:, c, :, 1:PMAX], ps[:, 7, c * P:c * P + DEC_B * (PMAX - 1)].rearrange("p (b t) -> p b t", b=DEC_B))
                i.then_inc(turn_out, 1)
                e.wait_ge(la_t, 1)
                e.scalar_tensor_tensor(out=la[:], in0=la[:], scalar=0.0, in1=tmp[:], op0=ALU.min, op1=ALU.subtract)
                e.drain()
                for c in range(2):
                    e.tensor_tensor_scan(bsum[:, c, :], m.reset[:], la[:, c, :], 0.0, ALU.mult, ALU.add)
                e.drain()
                bp, bs = tiles(bsum)
                tp, ts_ = tiles(tmp)
                for src, n0, n1, im, il in ((bp, 0, NT - 1, P // 2 - 1, P - 1), (bs, NT - 1, NC, 1, DEC_L - 1)):
                    e.tensor_copy(mid[:, :, n0:n1], src[:, :, :, im])
                    e.tensor_copy(last[:, :, n0:n1], src[:, :, :, il])
                e.drain()
                e.tensor_tensor(dlm[:], last[:], mid[:], ALU.subtract).then_inc(la_s, 1)
                for c in range(2):
                    e.tensor_tensor(tp[:, c], bp[:, c], mid[:, c, 0:NT - 1].unsqueeze(2).broadcast_to([P, NT - 1, P]), ALU.subtract)
                    i = e.tensor_tensor(ts_[:, c], bs[:, c], mid[:, c, NT - 1:NC].unsqueeze(2).broadcast_to([P, DEC_B, DEC_L]), ALU.subtract)
                i.then_inc(la_d, 1)
                F4 = slice(FROW, FROW + H)
                e.wait_ge(f_t, 1)
                e.scalar_tensor_tensor(out=fx[F4, :], in0=fx[F4, :], scalar=0.0, in1=ft[F4, :], op0=ALU.min, op1=ALU.subtract)
                e.drain()
                e.tensor_tensor_scan(m.CF[F4, 0:SEQ], m.ones[F4, 0:1].broadcast_to([H, SEQ]), fx[F4, 0:SEQ], 0.0, ALU.mult, ALU.add).then_inc(f_c, 1)
                e.wait_ge(turn_mm, 2)
                e.tensor_copy(tailT[:], ps[0:2 * NS, 4, 0:W]).then_inc(turn_out, 1)
                for g, w in enumerate(WINDOWS):
                    o, c = HD * (g % 2), g // 2
                    e.tensor_scalar(rcount[o:o + HD, c, :], m.count[o:o + HD, :], float(w), None, ALU.min)
                e.drain()
                e.reciprocal(rcount[:], rcount[:])
                e.drain()
                e.wait_ge(p_d, 1)
                for g, w in enumerate(WINDOWS):
                    o, c = HD * (g % 2), g // 2
                    R = slice(o, o + HD)
                    src, ssrc = ((pa, pas), (pb, pbs))[g % 2]
                    e.scalar_tensor_tensor(out=pa[R, c, 2 * PMAX:], in0=src[R, c, 2 * PMAX:], scalar=1.0 / w,
                                           in1=px[R, c, 2 * PMAX:], op0=ALU.mult, op1=ALU.subtract)
                    e.tensor_tensor(src[R, c, PMAX:2 * PMAX], src[R, c, PMAX:2 * PMAX], rcount[R, c, :], ALU.mult)
                    e.scalar_tensor_tensor(out=pxs[R, c, :, PMAX:], in0=ssrc[R, c, :, PMAX:], scalar=1.0 / w,
                                           in1=pxs[R, c, :, PMAX:], op0=ALU.mult, op1=ALU.subtract)
                    e.drain()
                    i = e.tensor_tensor(pa[R, c, PMAX:2 * PMAX], src[R, c, PMAX:2 * PMAX], px[R, c, PMAX:2 * PMAX], ALU.subtract)
                i.then_inc(p_diff, 1)
                e.wait_ge(la_e, 3)
                e.scalar_tensor_tensor(out=QE, in0=QE, scalar=HD ** -0.5, in1=la[:], op0=ALU.mult, op1=ALU.mult)
                e.tensor_tensor(KE, KE, tmp[:], ALU.mult).then_inc(qk_ready, 1)
                e.wait_ge(zeroed, 1)
                e.wait_ge(f_mm, 1)
                e.tensor_copy(m.lft[:, 0:NT - 1, :], ps[:, 6, 0:8 * NT].rearrange("p (t c) -> p t c", c=8)[:, 0:NT - 1, :])
                e.tensor_copy(m.lft[0:NS, NT - 1, 0:H], ps[0:NS, 6, 8 * (NT - 1):8 * (NT - 1) + H]).then_inc(f_out, 1)

                def mask_scores(t):
                    r, b = rows_of(t), t % 2
                    mask = (m.causal if t < NT - 1 else m.sampmask)[0:r, 0:r].bitcast(I32)
                    e.wait_ge(a_mm, t + 1)
                    if t >= 2:
                        e.wait_ge(o_mm, t - 1)
                    if t == NT - 1:
                        e.memset(at[0:r, b], 0.0)
                        e.drain()
                    for hb in range(2):
                        i = e.copy_predicated(at[0:r, b, hb, :, 0:r], mask.unsqueeze(1).broadcast_to([r, 2, r]),
                                              ps[0:r, 2 * b + hb, 0:2 * P].rearrange("p (h t) -> p h t", h=2)[:, :, 0:r])
                    i.then_inc(a_out, 1)

                mask_scores(0)
                for t in range(NT - 1):
                    if t >= 1:
                        e.wait_ge(o_mm, t)
                    for c in range(2):
                        i = e.tensor_scalar(Ssc[:, c, :], S[:, c, :], e_mid[:, c, t:t + 1], None, ALU.mult)
                    i.then_inc(s_sc, 1)
                    mask_scores(t + 1)
                    e.wait_ge(s_mm, t + 1)
                    for c in range(2):
                        for o in (0, HD):
                            e.tensor_scalar(Stmp[o:o + HD, c, 0, :], ps[o:o + HD, 6, c * P + o:c * P + o + HD],
                                            e_dlm[o:o + HD, c, t:t + 1], None, ALU.mult)
                    e.drain()
                    for c in range(2):
                        for o in (0, HD):
                            i = e.scalar_tensor_tensor(out=S[o:o + HD, c, o:o + HD], in0=S[o:o + HD, c, o:o + HD],
                                                       scalar=e_last[o:o + HD, c, t:t + 1], in1=Stmp[o:o + HD, c, 0, :],
                                                       op0=ALU.mult, op1=ALU.add)
                    i.then_inc(s_out, 1)
                    e.drain()
                e.wait_ge(st_in, 16 * (H + 1))
                for c in range(2):
                    i = e.tensor_tensor(SSsc[:, c], SS[:, c], e_mid[:, c, NT - 1:NC].unsqueeze(2).broadcast_to([P, DEC_B, P]), ALU.mult)
                i.then_inc(ss_sc, 1)
                for b in range(DEC_B):
                    i = e.tensor_scalar(vmask[:, b, :], m.V[0:NS, NT - 1, 0:W], m.sampmask[:, DEC_L * b + DEC_L - 1:DEC_L * b + DEC_L], None, ALU.mult)
                i.then_inc(vm_ready, 1)
                for g in range(4):
                    c, b0 = g // 2, g % 2 * 4
                    e.wait_ge(s_mm, NT - 1 + g + 1)
                    for o in (0, HD):
                        view = SS[o:o + HD, c, b0:b0 + 4, o:o + HD]
                        pv = ps[o:o + HD, 6 + g % 2, :].rearrange("p (b e) -> p b e", b=4)[:, :, o:o + HD]
                        bc = lambda x: x[o:o + HD, c, NT - 1 + b0:NT - 1 + b0 + 4].unsqueeze(2).broadcast_to([HD, 4, HD])
                        e.tensor_tensor(Stmp[o:o + HD, 0], pv, bc(e_dlm), ALU.mult)
                        e.tensor_tensor(view, view, bc(e_last), ALU.mult)
                        e.drain()
                        i = e.tensor_tensor(view, view, Stmp[o:o + HD, 0], ALU.add)
                        e.drain()
                    e.engine_nop().then_inc(s_out if g == 3 else vm_ready, 1)
                for i in range(len(norm_steps)):
                    norm_scale(e, i)
                e.wait_ge(silu, 1)
                e.drain()
                e.wait_ge(k_sent, 16 * NT)
                e.tensor_tensor(m.mixT[:, 0:2, :], QE, m.Z[:, ZG:ZG + 2, :], ALU.mult)

            @block.tensor
            def _(e):
                for n in range(2 * NCH):
                    if n >= 2:
                        e.wait_ge(la_x, n - 1)
                    e.matmul(ps[:, 2 + n % 2, 0:CH], m.wa2[:, n // NCH * P:n // NCH * P + P], m.ZS[0:RANK, cols(n % NCH)],
                             start=True, stop=True).then_inc(la_mm, 1)
                e.wait_ge(st_in, 16 * (H + 1))
                for c in range(2):
                    i = e.transpose(ps[:, 7, c * P:c * P + DEC_B * (PMAX - 1)], pst[:, c * P:c * P + P],
                                    m.ident[0:DEC_B * (PMAX - 1), 0:DEC_B * (PMAX - 1)])
                i.then_inc(turn_mm, 1)
                for t in range(NT):
                    r = rows_of(t)
                    if t >= 2:
                        e.wait_ge(kt_out, t - 1)
                    for c in range(2):
                        i = e.transpose(ps[0:r, t % 2, c * P:c * P + P], m.Z[:, ZFK + c, t * P:t * P + r], m.ident[:])
                    i.then_inc(kt_mm, 1)
                for c in range(2):
                    i = e.transpose(ps[0:2 * NS, 4, c * P:c * P + P], m.Z[:, ZPU + c, SEQ - NS:TOK], m.ident[:])
                i.then_inc(turn_mm, 1)
                e.wait_ge(f_c, 1)
                F4 = slice(FROW, FROW + H)
                for t in range(NT):
                    r = rows_of(t)
                    i = e.transpose(ps[0:r, 6, 8 * t:8 * t + H], fx[F4, t * P:t * P + r], m.ident[F4, F4])
                    if t < NT - 1:
                        i = e.transpose(ps[0:r, 6, 8 * t + H:8 * t + 2 * H], m.CF[F4, t * P:t * P + r], m.ident[F4, F4])
                i.then_inc(f_mm, 1)
                e.wait_ge(kt_out, NT)
                e.wait_ge(la_x, 6)
                e.wait_ge(p_diff, 1)
                for n in range(6):
                    c, k = n // 3, n % 3
                    src, w = ((pa[:, c, PMAX:PMAX + 512], 512), (pa[:, c, PMAX + 512:], 512), (pxs[:, c, :, PMAX:], NS))[k]
                    to = ps[:, n % 4, 0:w]
                    if k == 2:
                        to = to.rearrange("p (b l) -> p b l", l=DEC_L)
                    if n >= 4:
                        e.wait_ge(p_out, n - 3)
                    e.matmul(to, m.poolw[:, c, :], src, start=True, stop=True).then_inc(p_mm, 1)
                e.wait_ge(turn_out, 2)
                e.wait_ge(qk_ready, 1)
                for t in range(NT):
                    r = rows_of(t)
                    if t >= 2:
                        e.wait_ge(ket_out, t - 1)
                    for c in range(2):
                        i = e.transpose(ps[0:r, 4 + t % 2, c * P:c * P + P], KE[:, c, t * P:t * P + r], m.ident[:])
                    i.then_inc(ket_mm, 1)
                e.wait_ge(ket_out, NT)
                e.wait_ge(p_out, 6)
                e.wait_ge(f_out, 1)

                def scores(t):
                    r = rows_of(t)
                    if t >= 2:
                        e.wait_ge(a_out, t - 1)
                    for h in range(H):
                        o, c = HD * (h % 2), h // 2
                        i = e.matmul(ps[0:r, 2 * (t % 2) + h % 2, c * P:c * P + r], KE[o:o + HD, c, t * P:t * P + r],
                                     QE[o:o + HD, c, t * P:t * P + r], start=True, stop=True)
                    i.then_inc(a_mm, 1)

                scores(0)
                for t in range(NT):
                    r, b, last_t = rows_of(t), t % 2, t == NT - 1
                    if not last_t:
                        scores(t + 1)
                        if t >= 1:
                            e.wait_ge(s_out, t)
                        for c in range(2):
                            i = e.matmul(ps[:, 6, c * P:c * P + P], keT[:, t, c * P:c * P + P], m.V[:, t, c * P:c * P + P],
                                         start=(c == 0), stop=(c == 1), skip_group_check=True)
                        i.then_inc(s_mm, 1)
                        e.wait_ge(s_sc, t + 1)
                    else:
                        e.wait_ge(ss_sc, 1)
                    if t >= 2:
                        e.wait_ge(o_out, t - 1)
                    for c in range(2):
                        if not last_t:
                            e.matmul(ps[:, 4 + b, c * P:c * P + P], Ssc[:, c, :], QE[:, c, t * P:t * P + P],
                                     start=(c == 0), stop=False, skip_group_check=True)
                        else:
                            for s in range(DEC_B):
                                o = c * P + DEC_L * s
                                e.matmul(ps[:, 4 + b, o:o + DEC_L], SSsc[:, c, s, :],
                                         QE[:, c, SEQ + DEC_L * s:SEQ + DEC_L * s + DEC_L],
                                         start=(c == 0 and s == 0), stop=False, skip_group_check=True)
                    e.wait_ge(a_out, t + 1)
                    for h in range(H):
                        o, c = HD * (h % 2), h // 2
                        i = e.matmul(ps[o:o + HD, 4 + b, c * P:c * P + r], m.V[0:r, t, h * HD:h * HD + HD],
                                     at[0:r, b, h % 2, c, 0:r], start=False, stop=True, skip_group_check=True)
                    i.then_inc(o_mm, 1)
                e.wait_ge(vm_ready, 1)
                e.wait_ge(turn_out, 1)
                e.wait_ge(s_out, NT - 1)
                for g in range(4):
                    c, b0 = g // 2, g % 2 * 4
                    if g >= 2:
                        e.wait_ge(vm_ready, g)
                    e.matmul(ps[:, 6 + g % 2, :].rearrange("p (b e) -> p b e", b=4), keT[0:NS, NT - 1, c * P:c * P + P],
                             vmask[:, b0:b0 + 4, c * P:c * P + P], start=True, stop=True).then_inc(s_mm, 1)
                e.wait_ge(a_out, NT)
                for i in range(len(norm_steps)):
                    norm_mean(e, i)


def fox(nc, m):
    ctx = ExitStack()
    sb = lambda name, shape: ctx.enter_context(nc.sbuf_tensor(name, shape, F32))
    sem = lambda name: ctx.enter_context(nc.semaphore(name))
    ps = m.ps
    R = DEC_L * H
    QG = 4
    NQ = NPG // QG
    F4 = slice(FROW, FROW + H)
    with ctx:
        ck = m.Z[:, ZQ:ZQ + 4, 0:SEQ]
        sc = [m.Z[:, z, 0:SEQ] for z in (ZG, ZG + 1, ZCA, ZCA + 1)]
        pT = m.Z[:, ZPU:ZPU + 2, 0:SEQ].rearrange("p b (k q) -> p b k q", q=P)
        kpg = sb("kpg", [P, 4, QG, W])
        vpg = sb("vpg", [P, NPG, W])
        kT = sb("kT", [P, 2, 2, QG * PAGE])
        lfp, cpg = sb("lfp", [P, PAGE * H]), sb("cpg", [P, H, PAGE])
        tot, carry = sb("page_totals", [P, H]), sb("page_carry", [P, H])
        cnew = sb("cnew", [NS, H])
        cdiag = sb("cdiag", [NS, NS, H])
        cq = sb("cq", [P, DEC_B, DEC_L, H])
        bias = sb("bias", [P, DEC_B, NPG, DEC_L, H])
        snew = sb("snew", [NS, DEC_B, DEC_L, H])
        nneg = sb("nneg", [NS, NS])
        qbd = sb("qbd", [P, 2, DEC_B, DEC_L, H])
        S = sb("S_fox", [P, 2, NPG + 1, R])
        cmax, csum = sb("cmax", [P, R]), sb("csum", [P, R])
        rmax, maxdiag = sb("rmax", [R, 1]), sb("maxdiag", [R, R])
        sinv, orow = sb("sinv", [R, 1]), sb("orow", [R, W])
        nmax, rsum, rinv, pmax = sb("nmax", [P, 4]), sb("rsum", [P, 4]), sb("rinv", [P, 4]), sb("pmax", [P, 4])
        ot = sb("ot", [P, 2, P])
        srow = sb("srow", [R, 2, QG * PAGE])
        b_q, b_s = ps[0:R, 7, :], ps[:, 7, 0:QG * R]
        b_max, b_bc = ps[0:R, 7, 256:384], ps[:, 7, 384:400]
        b_pv, b_sum, b_ot = ps[0:R, 7, 0:W], ps[0:R, 7, W:W + 1], ps[:, 7, 256:256 + 2 * R]

        lf_in, page_sums, sums_mm = (sem(n) for n in ("lf_in", "page_sums", "sums_mm"))
        ck_mm, ck_out, qbd_ready = (sem(n) for n in ("ck_mm", "ck_out", "qbd_ready"))
        p_sc, p_read, p_so, p_exp, p_tr, p_to, p_pv, p_oo = (sem("fox_" + n) for n in ("sc", "read", "so", "exp", "tr", "to", "pv", "oo"))
        k_in, v_in = [sem(f"k_in{i}") for i in range(4)], sem("v_in")
        k_tr, k_o0, k_o1 = sem("k_tr"), sem("k_o0"), sem("k_o1")
        s_q, s_qo, s_qt, s_ev, s_max, s_row, s_shift, s_exp, s_col, s_pv, s_div, s_small, s_out = (
            sem("samp_" + n) for n in ("q", "qo", "qt", "ev", "max", "row", "shift", "exp", "col", "pv", "div", "small", "out"))

        steps = [(i, h) for i in range(NT - 1) for h in range(H)]
        N = len(steps)
        assert N == DEC_B * NQ
        LAST = N + 6
        groups = lambda n: steps[n][0] // 4 + 1

        order23 = []
        for n in range(LAST):
            if 3 <= n < N + 3 and steps[n - 3][1] % 2:
                order23.append(("o", n - 3))
            if 2 <= n < N + 2:
                order23 += [("p", n - 2, g) for g in range(groups(n - 2))]
        turn23 = {k: i + 1 for i, k in enumerate(order23)}
        last_of = lambda n: turn23[("p", n, groups(n) - 1)]

        def sample_at(n, phase):
            b, rest = divmod(n - NQ - 1 - phase, NQ)
            return b if rest == 0 and 0 <= b < DEC_B else None

        with nc.Block() as block:

            @block.sync
            def _(e):
                pages = []

                def load_k(b):
                    for j in range(NQ):
                        for g in range(QG):
                            k = b * NPG + QG * j + g
                            pages.append(e.value_load(m.pages[0:1, k:k + 1], min_val=0, max_val=POOLPG - 1))
                            if g == 0 and b:
                                e.wait_ge(k_tr, NQ * b + j - 3)
                            e.dma_start(kpg[:, j, g, :].unsqueeze(1),
                                        m.cache_k[0, ds(pages[k], 1)].rearrange("a t h d -> t a (h d)")).then_inc(k_in[j], 16)

                def load_v(b):
                    if b:
                        e.wait_ge(s_pv, b)
                    for g in range(NPG):
                        e.dma_start(vpg[:, g, :].unsqueeze(1),
                                    m.cache_v[0, ds(pages[b * NPG + g], 1)].rearrange("a t h d -> t a (h d)")).then_inc(v_in, 16)

                load_k(0)
                for b in range(1, DEC_B):
                    load_k(b)
                    load_v(b - 1)
                load_v(DEC_B - 1)

            @block.gpsimd
            def _(e):
                e.indirect_dma_start(out=lfp[:], out_offset=None,
                                     in_=m.cache_logf[0].rearrange("n t h -> n (t h)"),
                                     in_offset=bass.IndirectOffsetOnAxis(ap=m.pages_col[:, 0:1], axis=0)).then_inc(lf_in, 16)
                e.memset(S[:], NEG)
                e.memset(qbd[:], 0.0)
                e.drain()
                for h in range(H):
                    o, c = HD * (h % 2), h // 2
                    e.tensor_copy(qbd[o:o + HD, c, :, :, h], m.Z[o:o + HD, ZFQ + c, SEQ:TOK].rearrange("p (b l) -> p b l", l=DEC_L))
                    e.drain()
                e.drain().then_inc(qbd_ready, 1)

            @block.scalar
            def _(e):
                for n in range(2 * H):
                    e.wait_ge(ck_mm, n + 1)
                    e.copy(ck[:, n // 2, n % 2 * 512:n % 2 * 512 + 512], ps[:, n % 4, :]).then_inc(ck_out, 1)
                for n in range(2):
                    e.activation(m.mixT[:, 4 + n, :], m.Z[:, ZCB + n, :], ACT.Silu, bias=m.ln_b[:, n:n + 1])
                for n in range(LAST):
                    if n < N:
                        e.wait_ge(k_tr, n + 1)
                        if n >= 2:
                            e.wait_ge(s_q, n - 1)
                        e.copy(kT[:, n % 2, 0, :], ps[:, 5, :]).then_inc(k_o0, 1)
                    if 3 <= n < N + 3 and steps[n - 3][1] % 2:
                        i, h = steps[n - 3]
                        k = turn23[("o", n - 3)]
                        e.wait_ge(p_tr, k)
                        e.copy(m.mixT[:, 2 + h // 2, i * P:i * P + P], ps[:, 2 + k % 2, 0:P]).then_inc(p_to, 1)
                    if 2 <= n < N + 2:
                        i, h = steps[n - 2]
                        for g in range(groups(n - 2)):
                            k = turn23[("p", n - 2, g)]
                            w = min(4, i + 1 - 4 * g)
                            e.wait_ge(p_tr, k)
                            if g == 0 and n >= 4:
                                e.wait_ge(p_pv, n - 3)
                            e.copy(pT[:, n % 2, 4 * g:4 * g + w, :], ps[:, 2 + k % 2, 0:w * P].rearrange("p (k q) -> p k q", q=P)).then_inc(p_to, 1)
                    if 1 <= n <= N:
                        e.wait_ge(s_q, n)
                        e.copy(srow[:, (n - 1) % 2, :], b_q).then_inc(s_qo, 1)
                    if n < N:
                        nk = (steps[n][0] + 1) * P
                        e.wait_ge(p_so, n + 1)
                        e.activation(sc[n % 4][:, 0:nk], sc[n % 4][:, 0:nk], ACT.Exp, bias=nmax[:, n % 4:n % 4 + 1],
                                     accum_out=rsum[:, n % 4:n % 4 + 1]).then_inc(p_exp, 1)
                    b = sample_at(n, 2)
                    if b is not None:
                        e.wait_ge(s_shift, b + 1)
                        e.activation(S[:, b % 2], S[:, b % 2], ACT.Exp).then_inc(s_exp, 1)

            @block.vector
            def _(e):
                e.wait_ge(lf_in, 16)
                for h in range(H):
                    e.tensor_tensor_scan(cpg[:, h, :], m.ones[:, 0:1].broadcast_to([P, PAGE]),
                                         lfp[:].rearrange("p (t h) -> p h t", h=H)[:, h, :], 0.0, ALU.mult, ALU.add)
                e.tensor_scalar(nneg[:], m.sampmask[:], -1.0, -NEG, ALU.add, ALU.mult)
                e.drain()
                e.tensor_copy(tot[:], cpg[:, :, PAGE - 1]).then_inc(page_sums, 1)
                e.wait_ge(sums_mm, 1)
                e.tensor_copy(carry[:], ps[:, 5, 0:H])
                e.tensor_copy(cnew[:], ps[0:NS, 5, H:2 * H])
                e.drain()
                for h in range(H):
                    e.tensor_scalar(cpg[:, h, :], cpg[:, h, :], carry[:, h:h + 1], None, ALU.add)
                e.tensor_tensor(cdiag[:], m.ident[0:NS, 0:NS].unsqueeze(2).broadcast_to([NS, NS, H]),
                                cnew[:].unsqueeze(1).broadcast_to([NS, NS, H]), ALU.mult)
                e.drain().then_inc(page_sums, 1)
                e.wait_ge(sums_mm, 2)
                e.tensor_copy(cq[:].rearrange("p b l h -> p (b l h)"), ps[:, 5, 0:P])
                e.drain()
                for h in range(H):
                    e.tensor_tensor(bias[:, :, :, :, h], cq[:, :, :, h].unsqueeze(2).broadcast_to([P, DEC_B, NPG, DEC_L]),
                                    ps[:, 6, h * P:(h + 1) * P].rearrange("p (b g) -> p b g", g=NPG).unsqueeze(3).broadcast_to([P, DEC_B, NPG, DEC_L]),
                                    ALU.subtract)
                rows = snew[:].rearrange("p b l h -> p (b l) h")
                e.tensor_tensor(rows, ps[0:NS, 5, P:2 * P].rearrange("p (t h) -> p t h", h=H),
                                cq[0:NS].rearrange("p b l h -> p (b l) h"), ALU.add)
                e.drain()
                e.tensor_tensor(rows, rows, cnew[:].unsqueeze(1).broadcast_to([NS, NS, H]), ALU.subtract)
                e.drain()
                e.tensor_tensor(rows, rows, nneg[:].unsqueeze(2).broadcast_to([NS, NS, H]), ALU.add)
                e.drain().then_inc(page_sums, 1)
                e.wait_ge(qbd_ready, 1)
                e.wait_ge(ck_out, 2 * H)
                def sample_steps(n):
                    b = sample_at(n, 4)
                    if b is not None:
                        e.wait_ge(s_small, 3 * b + 3)
                        for h in range(H):
                            o, c = HD * (h % 2), h // 2
                            mm = e.tensor_copy(m.mixT[o:o + HD, 2 + c, SEQ + DEC_L * b:SEQ + DEC_L * b + DEC_L],
                                               b_ot[o:o + HD, R * c:R * c + R].rearrange("p (q h) -> p h q", h=H)[:, h, :])
                        mm.then_inc(s_out, 1)
                    b = sample_at(n, 1)
                    if b is not None:
                        e.wait_ge(s_small, 3 * b + 1)
                        e.tensor_reduce(rmax[:], b_max, AX.X, ALU.max)
                        e.drain()
                        e.tensor_scalar(maxdiag[:], m.ident[0:R, 0:R], rmax[:], None, ALU.mult).then_inc(s_row, 1)
                    b = sample_at(n, 2)
                    if b is not None:
                        e.wait_ge(s_small, 3 * b + 2)
                        e.tensor_tensor(S[:, b % 2], S[:, b % 2], b_bc.unsqueeze(1).broadcast_to([P, NPG + 1, R]), ALU.subtract).then_inc(s_shift, 1)
                    if 2 <= n < N + 2:
                        b, j = (n - 2) // NQ, (n - 2) % NQ
                        e.wait_ge(s_qt, n - 1)
                        if j == 0 and b >= 2:
                            e.wait_ge(s_pv, b - 1)
                        e.tensor_tensor(S[:, b % 2, QG * j:QG * j + QG, :], b_s.rearrange("p (g r) -> p g r", r=R),
                                        bias[:, b, QG * j:QG * j + QG].rearrange("p g l h -> p g (l h)"), ALU.add).then_inc(s_ev, 1)
                    b = sample_at(n, 0)
                    if b is not None:
                        e.tensor_copy(S[0:NS, b % 2, NPG, :], snew[:, b].rearrange("p l h -> p (l h)"))
                        e.drain()
                        e.tensor_reduce(cmax[:], S[:, b % 2].rearrange("p g r -> p r g"), AX.X, ALU.max).then_inc(s_max, 1)

                for n in range(LAST):
                    if sample_at(n, 4) is None:
                        sample_steps(n)
                    if n < N:
                        i, h = steps[n]
                        nk, s = (i + 1) * P, sc[n % 4]
                        e.wait_ge(p_sc, n + 1)
                        if n >= 4:
                            e.wait_ge(p_tr, last_of(n - 4))
                        for g in range(groups(n)):
                            w = min(512, nk - 512 * g)
                            mm = e.scalar_tensor_tensor(out=s[:, 512 * g:512 * g + w], in0=ps[:, g, 0:w], scalar=m.lft[:, i, H + h:H + h + 1],
                                                        in1=ck[:, h, 512 * g:512 * g + w], op0=ALU.add, op1=ALU.subtract)
                        mm.then_inc(p_read, 1)
                        e.drain()
                        e.tensor_tensor(s[:, nk - P:nk], s[:, nk - P:nk], m.qmask[:], ALU.add)
                        e.drain()
                        e.tensor_reduce(pmax[:, n % 4:n % 4 + 1], s[:, 0:nk], AX.X, ALU.max)
                        e.drain()
                        if n >= 4:
                            e.wait_ge(p_exp, n - 3)
                        e.tensor_scalar(nmax[:, n % 4:n % 4 + 1], pmax[:, n % 4:n % 4 + 1], -1.0, None, ALU.mult).then_inc(p_so, 1)
                        e.wait_ge(k_tr, n + 1)
                        if n >= 2:
                            e.wait_ge(s_q, n - 1)
                        e.tensor_copy(kT[:, n % 2, 1, :], ps[:, 6, :]).then_inc(k_o1, 1)
                    if sample_at(n, 4) is not None:
                        sample_steps(n)
                    b = sample_at(n, 3)
                    if b is not None:
                        e.wait_ge(s_exp, b + 1)
                        e.tensor_reduce(csum[:], S[:, b % 2].rearrange("p g r -> p r g"), AX.X, ALU.add).then_inc(s_col, 1)
                    if 2 <= n < N + 2:
                        k = n - 2
                        i, h = steps[k]
                        e.wait_ge(p_exp, k + 1)
                        e.reciprocal(rinv[:, k % 4:k % 4 + 1], rsum[:, k % 4:k % 4 + 1])
                        e.drain()
                        e.wait_ge(p_pv, k + 1)
                        if k >= 4:
                            e.wait_ge(p_tr, turn23[("o", (k - 4) // 2 * 2 + 1)])
                        e.tensor_scalar(ot[:, k // 2 % 2, k % 2 * HD:k % 2 * HD + HD], ps[:, 4, k % 2 * HD:k % 2 * HD + HD],
                                        rinv[:, k % 4:k % 4 + 1], None, ALU.mult).then_inc(p_oo, 1)
                    b = sample_at(n, 3)
                    if b is not None:
                        e.wait_ge(s_pv, b + 1)
                        e.reciprocal(sinv[:], b_sum)
                        e.drain()
                        e.tensor_scalar(orow[:], b_pv, sinv[:], None, ALU.mult).then_inc(s_div, 1)

            @block.tensor
            def _(e):
                for n in range(2 * H):
                    h = n // 2
                    if n >= 4:
                        e.wait_ge(ck_out, n - 3)
                    e.matmul(ps[:, n % 4, :], m.ident[F4, FROW + h:FROW + h + 1].broadcast_to([H, P]),
                             m.CF[F4, n % 2 * 512:n % 2 * 512 + 512], start=True, stop=True).then_inc(ck_mm, 1)
                e.wait_ge(page_sums, 1)
                e.matmul(ps[:, 5, 0:H], m.carry[:], tot[:], start=True, stop=True)
                e.matmul(ps[0:NS, 5, H:2 * H], m.pagesel[:], tot[:], start=True, stop=False, skip_group_check=True)
                e.matmul(ps[0:NS, 5, H:2 * H], m.sampmask[:], m.lft[0:NS, NT - 1, 0:H], start=False, stop=True,
                         skip_group_check=True).then_inc(sums_mm, 1)
                e.wait_ge(page_sums, 2)
                e.wait_ge(qbd_ready, 1)
                for h in range(H):
                    e.transpose(ps[:, 6, h * P:(h + 1) * P], cpg[:, h, :], m.ident[:])
                e.matmul(ps[:, 5, 0:P], m.ones[0:NS, :], cdiag[:].rearrange("p t h -> p (t h)"), start=True, stop=True)
                for c in range(2):
                    mm = e.matmul(ps[0:NS, 5, P:2 * P], m.Z[:, ZFK + c, SEQ:TOK], qbd[:, c].rearrange("p b l h -> p (b l h)"),
                                  start=(c == 0), stop=(c == 1), skip_group_check=True)
                mm.then_inc(sums_mm, 1)
                e.wait_ge(page_sums, 3)
                e.wait_ge(ck_out, 2 * H)

                def sample_steps(n):
                    b = sample_at(n, 4)
                    if b is not None:
                        e.wait_ge(s_div, b + 1)
                        for c in range(2):
                            mm = e.transpose(b_ot[:, R * c:R * c + R], orow[:, c * P:c * P + P], m.ident[0:R, 0:R])
                        mm.then_inc(s_small, 1)
                    b = sample_at(n, 1)
                    if b is not None:
                        e.wait_ge(s_max, b + 1)
                        e.wait_ge(s_qo, min(n - 1, N))
                        e.transpose(b_max, cmax[:], m.ident[:]).then_inc(s_small, 1)
                    b = sample_at(n, 2)
                    if b is not None:
                        e.wait_ge(s_row, b + 1)
                        e.wait_ge(s_qo, min(n - 1, N))
                        e.matmul(b_bc, m.ones[0:R, :], maxdiag[:], start=True, stop=True).then_inc(s_small, 1)
                    if 2 <= n < N + 2:
                        e.wait_ge(s_qo, n - 1)
                        if sample_at(n, 1) is not None:
                            e.wait_ge(s_row, sample_at(n, 1) + 1)
                        if sample_at(n, 2) is not None:
                            e.wait_ge(s_shift, sample_at(n, 2) + 1)
                        if sample_at(n, 4) is not None:
                            e.wait_ge(s_out, sample_at(n, 4) + 1)
                        for g in range(QG):
                            mm = e.transpose(b_s[:, g * R:(g + 1) * R], srow[:, n % 2, g * PAGE:(g + 1) * PAGE], m.ident[0:R, 0:R])
                        mm.then_inc(s_qt, 1)

                for n in range(LAST):
                    if n < N:
                        i, h = steps[n]
                        o, c = HD * (h % 2), h // 2
                        if n >= 1:
                            e.wait_ge(p_read, n)
                        for g in range(groups(n)):
                            w = min(512, (i + 1) * P - 512 * g)
                            mm = e.matmul(ps[:, g, 0:w], m.Z[o:o + HD, ZFQ + c, i * P:i * P + P],
                                          m.Z[o:o + HD, ZFK + c, 512 * g:512 * g + w], start=True, stop=True)
                        mm.then_inc(p_sc, 1)
                    if sample_at(n, 4) is None:
                        sample_steps(n)
                    if n < N:
                        e.wait_ge(k_in[n % 4], 16 * QG * (n // 4 + 1))
                        if n >= 1:
                            e.wait_ge(k_o0, n)
                            e.wait_ge(k_o1, n)
                        for c in range(2):
                            for g in range(QG):
                                mm = e.transpose(ps[:, 5 + c, g * PAGE:(g + 1) * PAGE], kpg[:, n % 4, g, c * P:c * P + P], m.ident[:])
                        mm.then_inc(k_tr, 1)
                    if sample_at(n, 4) is not None:
                        sample_steps(n)
                    if 3 <= n < N + 3 and steps[n - 3][1] % 2:
                        k = turn23[("o", n - 3)]
                        e.wait_ge(p_oo, n - 2)
                        if k >= 3:
                            e.wait_ge(p_to, k - 2)
                        e.transpose(ps[:, 2 + k % 2, 0:P], ot[:, (n - 3) // 2 % 2, :], m.ident[:]).then_inc(p_tr, 1)
                    if 2 <= n < N + 2:
                        i, h = steps[n - 2]
                        e.wait_ge(p_exp, n - 1)
                        for g in range(groups(n - 2)):
                            k = turn23[("p", n - 2, g)]
                            if k >= 3:
                                e.wait_ge(p_to, k - 2)
                            for a in range(4 * g, min(4 * g + 4, i + 1)):
                                mm = e.transpose(ps[:, 2 + k % 2, (a - 4 * g) * P:(a - 4 * g + 1) * P], sc[(n - 2) % 4][:, a * P:a * P + P], m.ident[:])
                            mm.then_inc(p_tr, 1)
                    if 1 <= n <= N:
                        b = (n - 1) // NQ
                        e.wait_ge(k_o0, n)
                        e.wait_ge(k_o1, n)
                        if n >= 2:
                            e.wait_ge(s_ev, n - 1)
                        for c in range(2):
                            mm = e.matmul(b_q, qbd[:, c, b].rearrange("p l h -> p (l h)"), kT[:, (n - 1) % 2, c, :],
                                          start=(c == 0), stop=(c == 1))
                        mm.then_inc(s_q, 1)
                    if 2 <= n < N + 2:
                        i, h = steps[n - 2]
                        e.wait_ge(p_to, last_of(n - 2))
                        if n >= 3:
                            e.wait_ge(p_oo, n - 2)
                        for a in range(i + 1):
                            mm = e.matmul(ps[:, 4, n % 2 * HD:n % 2 * HD + HD], pT[:, n % 2, a, :], m.V[:, a, W + h * HD:W + (h + 1) * HD],
                                          start=(a == 0), stop=(a == i), skip_group_check=True)
                        mm.then_inc(p_pv, 1)
                    b = sample_at(n, 3)
                    if b is not None:
                        e.wait_ge(s_qo, min(n, N))
                        e.wait_ge(s_ev, min(n - 1, N))
                        e.wait_ge(s_shift, b + 1)
                        e.wait_ge(s_col, b + 1)
                        e.matmul(b_sum, csum[:], m.ones[:, 0:1], start=True, stop=True, skip_group_check=True)
                        e.wait_ge(v_in, 16 * NPG * (b + 1))
                        for g in range(NPG + 1):
                            values = vpg[:, g, :] if g < NPG else m.V[0:NS, NT - 1, W:2 * W]
                            mm = e.matmul(b_pv, S[0:P if g < NPG else NS, b % 2, g, :], values,
                                          start=(g == 0), stop=(g == NPG), skip_group_check=True)
                        mm.then_inc(s_pv, 1)


def out_projection(nc, m):
    ctx = ExitStack()
    sb = lambda name, shape: ctx.enter_context(nc.sbuf_tensor(name, shape, F32))
    sbr = lambda name, shape: ctx.enter_context(nc.sbuf_tensor(name, shape, F32R))
    sem = lambda name: ctx.enter_context(nc.semaphore(name))
    ps = m.ps
    NQ, QW = D // W, W
    with ctx:
        wo_at = next_address(nc)
        wo = sb("wo", [P, 3, KC, QW])
        wo_lo = nc.alloc_sbuf_tensor_at("wo_lo", [P, 3, KC, QW], F32R, offset=wo_at)
        mix_lo = nc.alloc_sbuf_tensor_at("mix_lo", [P, KC, TOK], F32R, offset=m.mixT_at)
        wo_hi, mix_hi = sbr("wo_hi", [P, 2, KC, QW]), sbr("mix_hi", [P, KC, TOK])
        h2 = sb("h2", [P, 2, D])
        h2T = sb("h2T", [P, 2, KC, P])
        junk = sb("junk2", [P, D])
        ssq, std, rstd = sb("ssq2", [P, 2]), sb("std2", [P, 2]), sb("rstd2", [P, 2])
        wo_in, x_in2, h2_sent = [sem(f"wo_in{i}") for i in range(3)], sem("c_x_in"), [sem(f"h2_sent{i}") for i in range(2)]
        wo_split, mix_hi_done, mix_split = sem("wo_split"), sem("mix_hi_done"), sem("mix_split")
        o_mm, x2_done, std_done, h2_done, h2_tr, h2T_out, lg_mm = (
            sem("c_" + n) for n in ("o_mm", "x2", "std", "h2", "h2_tr", "h2T_out", "lg_mm"))
        toks = lambda t: slice(t * P, t * P + rows_of(t))

        with nc.Block() as block:

            @block.sync
            def _(e):
                for q in range(NQ):
                    if q == 3:
                        e.wait_ge(o_mm, NT)
                    e.dma_start(wo[:, q % 3], m.w_out[0].rearrange("(k p) n -> p k n", p=P)[:, :, q * QW:(q + 1) * QW]).then_inc(wo_in[q % 3], 16)
                    if q == 1:
                        for t in range(NT):
                            src = m.x_prompt[0, t * P:(t + 1) * P, :] if t < NT - 1 else m.x_sample.rearrange("b l d -> (b l) d")
                            e.dma_start(m.x2[0:rows_of(t), t, :], src).then_inc(x_in2, 16)

            @block.gpsimd
            def _(e):
                e.memset(m.gidx[:], 0)
                e.drain()
                e.dma_start(m.slot_tok.rearrange("(p t) a -> p (t a)", t=SLOT_TILES), m.gidx[:]).then_inc(m.s_table, 16)
                for t in range(NT):
                    e.wait_ge(h2_done, t + 1)
                    e.dma_start(m.h2d[t * P:t * P + rows_of(t), :], h2[0:rows_of(t), t % 2, :]).then_inc(h2_sent[t % 2], 16)
                e.wait_ge(m.s_table, 16)
                e.wait_ge(m.s_zero_rows, 16 * (SLOT_TILES - 2 * LEAST_PAIRS))
                for i in range(2):
                    e.wait_ge(h2_sent[i], 16 * ((NT + 1 - i) // 2))

            @block.scalar
            def _(e):
                def split_wo(q):
                    e.wait_ge(wo_in[q % 3], 16 * (q // 3 + 1))
                    if q >= 2:
                        e.wait_ge(o_mm, NT * (q - 1))
                    e.copy(wo_hi[:, q % 2], wo[:, q % 3]).then_inc(mix_hi_done, 1)

                split_wo(0)
                for t in range(NT):
                    e.copy(mix_hi[:, :, toks(t)], m.mixT[:, :, toks(t)]).then_inc(mix_hi_done, 1)
                for q in range(1, NQ):
                    split_wo(q)
                for t in range(NT):
                    r, b = rows_of(t), t % 2
                    e.wait_ge(x2_done, NT * (NQ - 1) + t + 1)
                    e.activation(junk[0:r], m.x2[0:r, t, :], ACT.Square, scale=D ** -0.5, accum_out=ssq[0:r, b:b + 1])
                    e.drain()
                    e.activation(std[0:r, b:b + 1], ssq[0:r, b:b + 1], ACT.Sqrt, bias=m.eps[0:r, :]).then_inc(std_done, 1)

            @block.vector
            def _(e):
                e.memset(m.logits[:], 0.0)

                def low_wo(q):
                    e.wait_ge(mix_hi_done, 1 if q == 0 else 1 + NT + q)
                    e.tensor_tensor(wo_lo[:, q % 3], wo[:, q % 3], wo_hi[:, q % 2].bitcast(F32), ALU.subtract).then_inc(wo_split, 1)

                def add(q, t):
                    n, r = q * NT + t, rows_of(t)
                    e.wait_ge(o_mm, n + 1)
                    if n == 0:
                        e.wait_ge(x_in2, 16 * NT)
                    part = m.x2[0:r, t, q * QW:(q + 1) * QW]
                    e.tensor_tensor(part, part, ps[0:r, n % 4, 0:QW], ALU.add).then_inc(x2_done, 1)

                def low_mix(t):
                    e.wait_ge(mix_hi_done, t + 2)
                    e.tensor_tensor(mix_lo[:, :, toks(t)], m.mixT[:, :, toks(t)], mix_hi[:, :, toks(t)].bitcast(F32), ALU.subtract).then_inc(mix_split, 1)

                def tail(t):
                    r, b = rows_of(t), t % 2
                    e.wait_ge(h2_tr, t + 1)
                    if t >= 2:
                        e.wait_ge(lg_mm, t - 1)
                    for c in range(2):
                        i = e.tensor_tensor(h2T[:, b, 4 * c:4 * c + 4, 0:r], ps[:, 4 + c, :].rearrange("p (k t) -> p k t", k=4)[:, :, 0:r],
                                            m.g2[:, 4 * c:4 * c + 4].unsqueeze(2).broadcast_to([P, 4, r]), ALU.mult)
                    i.then_inc(h2T_out, 1)

                def logits(t):
                    r = rows_of(t)
                    e.wait_ge(lg_mm, t + 1)
                    e.tensor_tensor(m.logits[0:r, t, :], ps[0:r, 6 + t % 2, 0:NG + NE], m.rb[0:r, :], ALU.add)

                low_wo(0)
                low_mix(0)
                low_mix(1)
                for q in range(NQ - 1):
                    for t in range(NT):
                        if q == 0 and t + 2 < NT:
                            low_mix(t + 2)
                        add(q, t)
                        if t == NT // 2:
                            low_wo(q + 1)
                for t in range(NT):
                    add(NQ - 1, t)
                    r, b = rows_of(t), t % 2
                    e.wait_ge(std_done, t + 1)
                    e.reciprocal(rstd[0:r, b:b + 1], std[0:r, b:b + 1])
                    e.drain()
                    if t >= 2:
                        e.wait_ge(h2_tr, t - 1)
                        e.wait_ge(h2_sent[b], 16 * (t // 2))
                    e.tensor_scalar(h2[0:r, b, :], m.x2[0:r, t, :], rstd[0:r, b:b + 1], None, ALU.mult).then_inc(h2_done, 1)
                    tail(t)
                    if t:
                        logits(t - 1)
                logits(NT - 1)

            @block.tensor
            def _(e):
                def product(n):
                    q, t = n // NT, n % NT
                    r = rows_of(t)
                    if t == 0:
                        e.wait_ge(wo_split, q + 1)
                    if q == 0:
                        e.wait_ge(mix_split, t + 1)
                    if n >= 4:
                        e.wait_ge(x2_done, n - 3)
                    i = products(e, ps[0:r, n % 4, 0:QW], [(mix_hi[:, k, toks(t)], mix_lo[:, k, toks(t)], wo_hi[:, q % 2, k, :], wo_lo[:, q % 3, k, :])
                                                           for k in range(KC)])
                    i.then_inc(o_mm, 1)

                def logits(t):
                    r, b = rows_of(t), t % 2
                    e.wait_ge(h2T_out, t + 1)
                    for k in range(KC):
                        i = e.matmul(ps[0:r, 6 + b, 0:NG + NE], h2T[:, b, k, 0:r], m.wr[:, k, :], start=(k == 0), stop=(k == KC - 1))
                    i.then_inc(lg_mm, 1)

                first = (NQ - 1) * NT
                for n in range(first + 2):
                    product(n)
                for t in range(NT):
                    if t + 2 < NT:
                        product(first + t + 2)
                    r, b = rows_of(t), t % 2
                    e.wait_ge(h2_done, t + 1)
                    if t:
                        e.wait_ge(h2T_out, t)
                    for k in range(KC):
                        i = e.transpose(ps[:, 4 + k // 4, k % 4 * P:k % 4 * P + r], h2[0:r, b, k:D:KC], m.ident[0:r, 0:r])
                    i.then_inc(h2_tr, 1)
                    if t:
                        logits(t - 1)
                logits(NT - 1)


def route(nc, m):
    ctx = ExitStack()
    sb = lambda name, shape, dt=F32: ctx.enter_context(nc.sbuf_tensor(name, shape, dt))
    sem = lambda name: ctx.enter_context(nc.semaphore(name))
    ps = m.ps
    B3, B4 = [P, NT, NE], [P, NT, NG, NE // NG]
    with ctx:
        G, E = m.logits[:, :, 0:NG], m.logits[:, :, NG:NG + NE]
        gmax, gsum, gw = sb("gmax", [P, NT]), sb("gsum", [P, NT]), sb("gw", [P, NT])
        gx, gsel = sb("gx", [P, NT, NG]), sb("gsel", [P, NT, NG])
        em, wi, prio = sb("em", B3), sb("wi", B3), sb("prio", B3)
        oh = [sb("oh1", B3), sb("oh2", B3)]
        both, valid = sb("both", B3), sb("valid", [P, NT])
        top = [sb("top1", [P, NT]), sb("top2", [P, NT])]
        first = sb("first", [P, NT])
        ex, den = sb("ex", [P, NT]), sb("den", [P, NT])
        slot = sb("slot", B3)
        run = sb("run", [P, NT + 1, NE])
        ntile, incl, base = sb("ntile", [P, NE]), sb("incl", [P, NE]), sb("base", [P, NE])
        sf = sb("sf", [P, 2, NT])
        pos, pos2 = sb("pos", [P, 2, NT], I32), sb("pos2", [P, 2, NT], I32)
        te = sb("te", [1, SLOT_TILES, NE])
        tsum = sb("tsum", [1, SLOT_TILES])
        gdiff, exps, oh_done, cnt_mm, pos_done, sent, tiles_known = (
            sem("r_" + n) for n in ("gdiff", "exps", "oh", "cnt_mm", "pos", "sent", "tiles"))

        with nc.Block() as block:

            @block.sync
            def _(e):
                e.wait_ge(tiles_known, 1)
                x = e.value_load(m.tile_exp[0:1, 0:1], min_val=0, max_val=NE - 1)
                e.dma_start(m.wg[:, 0].unsqueeze(1), m.exp_w_gate[0, ds(x, 1)].rearrange("a (p k) n -> p a k n", k=KC)).then_inc(m.gu_in[0], 16)
                e.dma_start(m.wu[:, 0].unsqueeze(1), m.exp_w_up[0, ds(x, 1)].rearrange("a (p k) n -> p a k n", k=KC)).then_inc(m.gu_in[0], 16)
                e.dma_start(m.wd[:, 0].unsqueeze(1), m.exp_w_down[0, ds(x, 1)].rearrange("a (p k) n -> p a k n", k=DE // P)).then_inc(m.dn_in[0], 16)

            @block.scalar
            def _(e):
                e.wait_ge(gdiff, 1)
                e.activation(gx[:], gx[:], ACT.Exp).then_inc(exps, 1)
                e.wait_ge(gdiff, 2)
                e.activation(ex[:], ex[:], ACT.Exp).then_inc(exps, 1)

            @block.vector
            def _(e):
                bc = lambda x, n: x[:].unsqueeze(2).broadcast_to([P, NT, n])

                def pick(src, mx, out, n, pr):
                    e.tensor_tensor(wi[:, :, 0:n], src, bc(mx, n), ALU.is_equal)
                    e.drain()
                    e.tensor_tensor(wi[:, :, 0:n], wi[:, :, 0:n], pr, ALU.mult)
                    e.drain()
                    e.tensor_reduce(first[:], wi[:, :, 0:n], AX.X, ALU.max)
                    e.drain()
                    e.tensor_tensor(out, wi[:, :, 0:n], bc(first, n), ALU.is_equal)
                    e.drain()

                e.tensor_scalar(prio[:], m.exp_id[:], -1.0, float(NE), ALU.mult, ALU.add)
                e.tensor_scalar(valid[:], m.tok_id[:], float(TOK), None, ALU.is_lt)
                e.tensor_reduce(gmax[:], G, AX.X, ALU.max)
                e.drain()
                e.tensor_tensor(gx[:], G, bc(gmax, NG), ALU.subtract).then_inc(gdiff, 1)
                pick(G, gmax, gsel[:], NG, prio[:, :, 0:NG])
                e.tensor_scalar(gsel[:], gsel[:], -1.0, -NEG, ALU.add, ALU.mult)
                e.drain()
                e.tensor_tensor(em[:].rearrange("p t (g k) -> p t g k", g=NG), E.rearrange("p t (g k) -> p t g k", g=NG),
                                gsel[:].unsqueeze(3).broadcast_to(B4), ALU.add)
                e.drain()
                e.tensor_reduce(top[0][:], em[:], AX.X, ALU.max)
                e.drain()
                pick(em[:], top[0], oh[0][:], NE, prio[:])
                e.scalar_tensor_tensor(out=em[:], in0=oh[0][:], scalar=NEG, in1=em[:], op0=ALU.mult, op1=ALU.add)
                e.drain()
                e.tensor_reduce(top[1][:], em[:], AX.X, ALU.max)
                e.drain()
                e.tensor_tensor(ex[:], top[1][:], top[0][:], ALU.subtract).then_inc(gdiff, 1)
                pick(em[:], top[1], oh[1][:], NE, prio[:])
                e.tensor_tensor(both[:], oh[0][:], oh[1][:], ALU.add)
                e.drain()
                e.tensor_tensor(both[:], both[:], bc(valid, NE), ALU.mult).then_inc(oh_done, 1)
                e.wait_ge(exps, 2)
                e.tensor_reduce(gsum[:], gx[:], AX.X, ALU.add)
                e.tensor_scalar(den[:], ex[:], 1.0, None, ALU.add)
                e.drain()
                e.tensor_tensor(den[:], den[:], gsum[:], ALU.mult)
                e.drain()
                e.reciprocal(m.gate[:, 0, :], den[:])
                e.drain()
                e.tensor_tensor(m.gate[:, 1, :], m.gate[:, 0, :], ex[:], ALU.mult)
                e.wait_ge(cnt_mm, 1)
                e.memset(run[:, 0, :], 0.0)
                e.memset(ntile[:], 0.0)
                e.drain()
                for t in range(NT):
                    e.tensor_tensor(run[:, t + 1, :], run[:, t, :], ps[:, 1, t * NE:(t + 1) * NE], ALU.add)
                    e.drain()
                for j in range(NT):
                    e.scalar_tensor_tensor(out=ntile[:], in0=run[:, NT, :], scalar=float(P * j), in1=ntile[:], op0=ALU.is_gt, op1=ALU.add)
                    e.drain()
                e.tensor_tensor_scan(incl[:], m.ones[:, 0:NE], ntile[:], 0.0, ALU.mult, ALU.add)
                e.drain()
                e.tensor_tensor(te[:], m.tile_id[0:1].unsqueeze(2).broadcast_to([1, SLOT_TILES, NE]),
                                incl[0:1].unsqueeze(1).broadcast_to([1, SLOT_TILES, NE]), ALU.is_ge)
                e.drain()
                e.tensor_reduce(tsum[:], te[:], AX.X, ALU.add)
                e.drain()
                e.tensor_scalar(m.tile_exp[:], tsum[:], float(NE - 1), None, ALU.min).then_inc(tiles_known, 1)
                e.tensor_tensor(base[:], incl[:], ntile[:], ALU.subtract)
                e.tensor_tensor(slot[:], ps[:, 0, 0:NT * NE].rearrange("p (t n) -> p t n", n=NE), run[:, 0:NT, :], ALU.add)
                e.drain()
                e.scalar_tensor_tensor(out=slot[:], in0=base[:].unsqueeze(1).broadcast_to(B3), scalar=float(P), in1=slot[:],
                                       op0=ALU.mult, op1=ALU.add)
                e.drain()
                for c in range(2):
                    e.tensor_tensor(em[:], oh[c][:], slot[:], ALU.mult)
                    e.drain()
                    e.tensor_reduce(sf[:, c, :], em[:], AX.X, ALU.add)
                    e.drain()
                e.tensor_copy(m.slots[:], sf[:])
                e.drain()
                e.tensor_scalar(pos[:], m.slots[:], P - 1, 5, ALU.bitwise_and, ALU.logical_shift_left)
                e.tensor_scalar(pos2[:], m.slots[:], 7, None, ALU.logical_shift_right)
                e.drain()
                e.tensor_tensor(pos[:], pos[:], pos2[:], ALU.add).then_inc(pos_done, 1)
                e.tensor_scalar(m.more_pairs[:], incl[0:1, NE - 1:NE], 1.0 - 2 * LEAST_PAIRS, 0.0, ALU.add, ALU.max)
                e.drain()
                e.tensor_scalar(m.more_pairs[:], m.more_pairs[:], 1, None, ALU.logical_shift_right)

            @block.tensor
            def _(e):
                e.wait_ge(oh_done, 1)
                rhs = both[:].rearrange("p t n -> p (t n)")
                e.matmul(ps[:, 0, 0:NT * NE], m.strict[:], rhs, start=True, stop=True)
                e.matmul(ps[:, 1, 0:NT * NE], m.ones[:], rhs, start=True, stop=True).then_inc(cnt_mm, 1)

            @block.gpsimd
            def _(e):
                e.wait_ge(pos_done, 1)
                for t in range(NT):
                    r = rows_of(t)
                    for c in range(2):
                        e.indirect_dma_start(out=m.slot_tok, out_offset=bass.IndirectOffsetOnAxis(ap=pos[0:r, c, t:t + 1], axis=0),
                                             in_=m.tok_id[0:r, t:t + 1], in_offset=None).then_inc(sent, 16)
                e.wait_ge(sent, 16 * 2 * NT)
                e.dma_start(m.gidx[:], m.slot_tok.rearrange("(p t) a -> p (t a)", t=SLOT_TILES)).then_inc(sent, 16)
                e.wait_ge(sent, 16 * (2 * NT + 1))


def experts(nc, m):
    ctx = ExitStack()
    sb = lambda name, shape, dt=F32: ctx.enter_context(nc.sbuf_tensor(name, shape, dt))
    sem = lambda name: ctx.enter_context(nc.semaphore(name))
    ps = m.ps
    KE = DE // P
    S = SLOT_TILES
    with ctx:
        wg, wu, wd = m.wg, m.wu, m.wd
        hg, hgT = sb("hg", [P, 2, D]), sb("hgT", [P, 2, KC, P])
        gcol = [sb(f"gcol{i}", [P, 1], I32) for i in range(2)]
        sg, he, heT = sb("sg", [P, 2, DE]), sb("he", [P, 2, DE]), sb("heT", [P, 2, KE, P])
        yo = sb("yo", [P, 2, D])
        landed = sb("landed", [1, 2])
        pair = lambda n: [sem(f"{n}{i}") for i in range(2)]
        gu_in, dn_in, hg_in, y_sent = m.gu_in, m.dn_in, pair("hg_in"), pair("y_sent")
        t_mm, t_out, gu_mm, silu, he_done, he_mm, he_out, d_mm, y_a, y_v = (
            sem("e_" + n) for n in ("t_mm", "t_out", "gu_mm", "silu", "he", "he_mm", "he_out", "d_mm", "y_a", "y_v"))


        def pairs(e):
            return e.value_load(m.more_pairs[0:1, 0:1], min_val=0, max_val=S // 2 - LEAST_PAIRS) + LEAST_PAIRS

        with nc.Block() as block:

            @block.sync
            def _(e):
                def load(s, b, first=False):
                    x = e.value_load(m.tile_exp[0:1, ds(s, 1)], min_val=0, max_val=NE - 1)
                    if not first:
                        e.wait_ge(gu_mm, s - 1)
                    for to, of in ((wg, m.exp_w_gate), (wu, m.exp_w_up)):
                        e.dma_start(to[:, b].unsqueeze(1), of[0, ds(x, 1)].rearrange("a (p k) n -> p a k n", k=KC)).then_inc(gu_in[b], 16)
                    if not first:
                        e.wait_ge(d_mm, s - 1)
                    e.dma_start(wd[:, b].unsqueeze(1), m.exp_w_down[0, ds(x, 1)].rearrange("a (p k) n -> p a k n", k=KE)).then_inc(dn_in[b], 16)

                load(1, 1, True)
                with e.Fori(1, pairs(e)) as j:
                    load(2 * j, 0)
                    load(2 * j + 1, 1)

            @block.gpsimd
            def _(e):
                def gather(s, b, first=False):
                    if not first:
                        e.wait_ge(t_mm, s - 1)
                    e.tensor_copy(gcol[b][:], m.gidx[:, ds(s, 1)])
                    e.drain()
                    e.indirect_dma_start(out=hg[:, b, :], out_offset=None, in_=m.h2d,
                                         in_offset=bass.IndirectOffsetOnAxis(ap=gcol[b][:, 0:1], axis=0)).then_inc(hg_in[b], 16)

                gather(0, 0, True)
                gather(1, 1, True)
                with e.Fori(1, pairs(e)) as j:
                    gather(2 * j, 0)
                    gather(2 * j + 1, 1)

            @block.scalar
            def _(e):
                def act_silu(s, b):
                    e.wait_ge(gu_mm, s + 1)
                    e.activation(sg[:, b, :], ps[:, 2 * b, :], ACT.Silu).then_inc(silu, 1)

                def step(s, b, j, last=False):
                    e.wait_ge(he_mm, s + 1)
                    e.copy(heT[:, b], ps[:, 2 * b, :].rearrange("p (k t) -> p k t", k=KE)).then_inc(he_out, 1)
                    e.wait_ge(d_mm, s + 1)
                    if not (isinstance(j, int) and j == 0):
                        e.wait_ge(y_sent[b], 16 * j)
                    e.copy(yo[:, b, 0:512], ps[:, 6, :]).then_inc(y_a, 1)
                    e.wait_ge(y_a, s + 1)
                    e.wait_ge(y_v, s + 1)
                    e.dma_start(m.yd[ds(s * P, P), :], yo[:, b, :]).then_inc(y_sent[b], 16)
                    if not last:
                        act_silu(s + 2, b)

                act_silu(0, 0)
                act_silu(1, 1)
                step(0, 0, 0)
                step(1, 1, 0)
                n = pairs(e)
                with e.Fori(1, n - 1) as j:
                    step(2 * j, 0, j)
                    step(2 * j + 1, 1, j)
                step(2 * n - 2, 0, n - 1, True)
                step(2 * n - 1, 1, n - 1, True)
                for i in range(2):
                    e.wait_ge(y_sent[i], 16 * n)
                    e.copy(landed[0:1, i:i + 1], m.eps[0:1, :])

            @block.vector
            def _(e):
                def turn_out(s, b, first=False):
                    e.wait_ge(t_mm, s + 1)
                    if not first:
                        e.wait_ge(gu_mm, s - 1)
                    for c in range(2):
                        i = e.tensor_tensor(hgT[:, b, 4 * c:4 * c + 4, :], ps[:, 4 + c, :].rearrange("p (k t) -> p k t", k=4),
                                            m.g2[:, 4 * c:4 * c + 4].unsqueeze(2).broadcast_to([P, 4, P]), ALU.mult)
                    i.then_inc(t_out, 1)

                def make_he(s, b):
                    e.wait_ge(silu, s + 1)
                    e.tensor_tensor(he[:, b, :], sg[:, b, :], ps[:, 2 * b + 1, :], ALU.mult).then_inc(he_done, 1)

                def step(s, b, j, last=False):
                    if not last:
                        turn_out(s + 2, b)
                    e.wait_ge(d_mm, s + 1)
                    if not (isinstance(j, int) and j == 0):
                        e.wait_ge(y_sent[b], 16 * j)
                    e.tensor_copy(yo[:, b, 512:], ps[:, 7, :]).then_inc(y_v, 1)
                    if not last:
                        make_he(s + 2, b)

                for s in range(2):
                    turn_out(s, s, True)
                    make_he(s, s)
                step(0, 0, 0)
                step(1, 1, 0)
                n = pairs(e)
                with e.Fori(1, n - 1) as j:
                    step(2 * j, 0, j)
                    step(2 * j + 1, 1, j)
                step(2 * n - 2, 0, n - 1, True)
                step(2 * n - 1, 1, n - 1, True)

            @block.tensor
            def _(e):
                def turn(s, b, j):
                    e.wait_ge(hg_in[b], 16 * j + 16)
                    if not (isinstance(s, int) and s == 0):
                        e.wait_ge(t_out, s)
                    for k in range(KC):
                        i = e.transpose(ps[:, 4 + k // 4, k % 4 * P:k % 4 * P + P], hg[:, b, k:D:KC], m.ident[:])
                    i.then_inc(t_mm, 1)

                def gate_up(s, b, j):
                    e.wait_ge(t_out, s + 1)
                    e.wait_ge(gu_in[b], 32 * j + 32)
                    for n, w in enumerate((wg, wu)):
                        for k in range(KC):
                            i = e.matmul(ps[:, 2 * b + n, :], hgT[:, b, k, :], w[:, b, k, :], start=(k == 0), stop=(k == KC - 1))
                    i.then_inc(gu_mm, 1)

                def step(s, b, j, last=False):
                    e.wait_ge(he_done, s + 1)
                    for k in range(KE):
                        i = e.transpose(ps[:, 2 * b, k * P:k * P + P], he[:, b, k:DE:KE], m.ident[:])
                    i.then_inc(he_mm, 1)
                    if not last:
                        turn(s + 2, b, j + 1)
                    e.wait_ge(he_out, s + 1)
                    e.wait_ge(dn_in[b], 16 * j + 16)
                    if not (isinstance(s, int) and s == 0):
                        e.wait_ge(y_a, s)
                        e.wait_ge(y_v, s)
                    for n in range(2):
                        for k in range(KE):
                            i = e.matmul(ps[:, 6 + n, :], heT[:, b, k, :], wd[:, b, k, n * 512:(n + 1) * 512],
                                         start=(k == 0), stop=(k == KE - 1))
                    i.then_inc(d_mm, 1)
                    if not last:
                        gate_up(s + 2, b, j + 1)

                for s in range(2):
                    turn(s, s, 0)
                    gate_up(s, s, 0)
                step(0, 0, 0)
                step(1, 1, 0)
                n = pairs(e)
                with e.Fori(1, n - 1) as j:
                    step(2 * j, 0, j)
                    step(2 * j + 1, 1, j)
                step(2 * n - 2, 0, n - 1, True)
                step(2 * n - 1, 1, n - 1, True)


def combine(nc, m):
    NB = 3
    ctx = ExitStack()
    sem = lambda name: ctx.enter_context(nc.semaphore(name))
    with ctx:
        yr = ctx.enter_context(nc.sbuf_tensor("yr", [P, 2 * NB, D], F32))
        rows_in, done, sent = [sem(f"rows_in{i}") for i in range(NB)], sem("y_done2"), sem("y_out")

        with nc.Block() as block:

            @block.gpsimd
            def _(e):
                for t in range(NT):
                    r = rows_of(t)
                    for c in range(2):
                        b = 2 * (t % NB) + c
                        if t >= NB:
                            e.wait_ge(done, t - NB + 1)
                        e.indirect_dma_start(out=yr[0:r, b, :], out_offset=None, in_=m.yd,
                                             in_offset=bass.IndirectOffsetOnAxis(ap=m.slots[0:r, c, t:t + 1], axis=0)).then_inc(rows_in[t % NB], 16)

            @block.vector
            def _(e):
                for t in range(NT):
                    r = rows_of(t)
                    for c in range(2):
                        b = 2 * (t % NB) + c
                        e.wait_ge(rows_in[t % NB], 32 * (t // NB + 1))
                        i = e.scalar_tensor_tensor(out=m.x2[0:r, t, :], in0=yr[0:r, b, :], scalar=m.gate[0:r, c, t:t + 1],
                                                   in1=m.x2[0:r, t, :], op0=ALU.mult, op1=ALU.add)
                        if c == 0:
                            e.drain()
                    i.then_inc(done, 1)

            @block.sync
            def _(e):
                for t in range(NT):
                    e.wait_ge(done, t + 1)
                    to = m.y_prompt[0, t * P:(t + 1) * P, :] if t < NT - 1 else m.y_sample.rearrange("b l d -> (b l) d")
                    e.dma_start(to, m.x2[0:rows_of(t), t, :]).then_inc(sent, 16)
                e.wait_ge(sent, 16 * NT)


OUTS = [("y_prompt", (1, SEQ, D)), ("y_sample", (DEC_B, DEC_L, D)),
        ("k_prompt", (1, 1, SEQ, H, HD)), ("v_prompt", (1, 1, SEQ, H, HD)), ("logf_prompt", (1, 1, SEQ, H)),
        ("k_sample", (1, DEC_B, DEC_L, H, HD)), ("v_sample", (1, DEC_B, DEC_L, H, HD)), ("logf_sample", (1, DEC_B, DEC_L, H)),
        ("gla_prompt", (1, 1, H, HD, HD)), ("gla_sample", (1, DEC_B, H, HD, HD)),
        ("conv_prompt", (1, 1, TAPS - 1, W)), ("conv_sample", (1, DEC_B, TAPS - 1, W)),
        ("pool_prompt", (1, 1, PMAX - 1, W)), ("pool_sample", (1, DEC_B, PMAX - 1, W))]


def program(nc, m):
    ctx = ExitStack()
    sb = lambda name, shape, dt=F32: ctx.enter_context(nc.sbuf_tensor(name, shape, dt))
    with ctx:
        m.ps = ctx.enter_context(nc.psum_tensor("ps", [P, 8, 512], F32))
        m.s_param, m.s_zero_rows = (ctx.enter_context(nc.semaphore(n)) for n in ("s_param", "s_zero_rows"))
        m.ident, m.ones, m.headmean, m.chmean = sb("ident", [P, P]), sb("ones", [P, P]), sb("headmean", [P, P]), sb("chmean", [P, P])
        m.causal, m.strict, m.qmask = sb("causal", [P, P]), sb("strict", [P, P]), sb("qmask", [P, P])
        m.sampmask = sb("sampmask", [NS, NS])
        m.eps = sb("eps", [P, 1])
        m.carry, m.pagesel = sb("carry", [P, P]), sb("pagesel", [P, NS])
        m.reset, m.poolw = sb("reset", [P, TOK]), sb("poolw", [P, 2, P])
        m.tok_id = sb("tok_id", [P, NT], I32)
        m.exp_id_i, m.exp_id = sb("exp_id_i", [P, NT, NE], I32), sb("exp_id", [P, NT, NE])
        m.tile_id_i, m.tile_id = sb("tile_id_i", [P, SLOT_TILES], I32), sb("tile_id", [P, SLOT_TILES])
        m.count_i, m.count = sb("count_i", [P, PMAX], I32), sb("count", [P, PMAX])
        m.g1, m.g2 = sb("g1", [P, KC]), sb("g2", [P, KC])
        m.gla_g, m.gla_b, m.cb, m.ln_g, m.ln_b, m.pscale = (sb(n, [P, 2]) for n in ("gla_g", "gla_b", "cb", "ln_g", "ln_b", "pscale"))
        m.fqg, m.fkg, m.fb = sb("fqg", [P, 1]), sb("fkg", [P, 1]), sb("fb", [FROW + H, 1])
        m.wa2, m.tapw = sb("wa2", [RANK, W]), sb("tapw", [TAPS, W])
        m.wr, m.rb = sb("wr", [P, KC, NG + NE]), sb("rb", [P, NG + NE])
        m.pages, m.pages_col = sb("pages", [1, P], I32), sb("pages_col", [P, 1], I32)
        m.fqg8 = sb("fqg8", [P, 1])
        m.CF, m.lft = sb("CF", [FROW + H, TOK]), sb("lft", [P, NT, 2 * H])
        m.x_in = [ctx.enter_context(nc.semaphore(f"x_in{i}")) for i in range(4)]
        m.wv_in = ctx.enter_context(nc.semaphore("wv_in"))
        m.mixT_at = next_address(nc)
        m.mixT = sb("mixT", [P, KC, TOK])
        m.Z_at = next_address(nc)
        with (nc.sbuf_tensor("Z", [P, 16, TOK], F32) as m.Z, nc.sbuf_tensor("ZS", [FROW + H, TOK], F32) as m.ZS,
              nc.sbuf_tensor("V", [P, NT, 2 * W], F32) as m.V):
            m.xt = [m.Z[:, z, 0:D] for z in (ZG, ZG + 1, ZCB, ZCB + 1)]
            m.wv = m.Z[:, ZFQ:ZFQ + 4, :].rearrange("p z t -> p (z t)")[:, 0:KC * 2 * W].rearrange("p (k n) -> p k n", k=KC)
            constants(nc, m)
            projections(nc, m)
            gla_pool_norms(nc, m)
            fox(nc, m)
        m.s_table = ctx.enter_context(nc.semaphore("s_table"))
        m.x2 = sb("x2", [P, NT, D])
        m.logits = sb("logits", [P, NT, NG + NE])
        m.gate, m.slots = sb("gate", [P, 2, NT]), sb("slots", [P, 2, NT], I32)
        m.gidx, m.tile_exp = sb("gidx", [P, SLOT_TILES], I32), sb("tile_exp", [1, SLOT_TILES], I32)
        m.more_pairs = sb("more_pairs", [1, 1], I32)
        out_projection(nc, m)
        m.wg, m.wu = sb("wg", [P, 2, KC, DE]), sb("wu", [P, 2, KC, DE])
        m.wd = m.mixT[:].rearrange("p k t -> p (k t)")[:, 0:2 * DE // P * D].rearrange("p (b k n) -> p b k n", b=2, k=DE // P)
        m.gu_in, m.dn_in = ([ctx.enter_context(nc.semaphore(f"{n}{i}")) for i in range(2)] for n in ("gu_in", "dn_in"))
        route(nc, m)
        experts(nc, m)
        combine(nc, m)


def build(nc, arrays):
    m = Memory()
    m.x_prompt, m.x_sample, m.cache_k, m.cache_v = arrays["x_prompt"], arrays["x_sample"], arrays["cache_k"], arrays["cache_v"]
    m.cache_logf, m.page_table, m.state_gla, m.state_conv = arrays["cache_logf"], arrays["page_table"], arrays["state_gla"], arrays["state_conv"]
    m.state_pool, m.norm1_g, m.w_in, m.gla_w_a2 = arrays["state_pool"], arrays["norm1_g"], arrays["w_in"], arrays["gla_w_a2"]
    m.gla_b_a, m.gla_norm_g, m.fox_b_f, m.fox_q_norm_g = arrays["gla_b_a"], arrays["gla_norm_g"], arrays["fox_b_f"], arrays["fox_q_norm_g"]
    m.fox_k_norm_g, m.conv_w, m.conv_b, m.conv_ln_g = arrays["fox_k_norm_g"], arrays["conv_w"], arrays["conv_b"], arrays["conv_ln_g"]
    m.conv_ln_b, m.pool_w, m.pool_scale, m.w_out = arrays["conv_ln_b"], arrays["pool_w"], arrays["pool_scale"], arrays["w_out"]
    m.norm2_g, m.router_wg, m.router_bg, m.router_we = arrays["norm2_g"], arrays["router_wg"], arrays["router_bg"], arrays["router_we"]
    m.router_be, m.exp_w_gate, m.exp_w_up, m.exp_w_down = arrays["router_be"], arrays["exp_w_gate"], arrays["exp_w_up"], arrays["exp_w_down"]
    m.y_prompt, m.y_sample, m.k_prompt, m.v_prompt = arrays["y_prompt"], arrays["y_sample"], arrays["k_prompt"], arrays["v_prompt"]
    m.logf_prompt, m.k_sample, m.v_sample, m.logf_sample = arrays["logf_prompt"], arrays["k_sample"], arrays["v_sample"], arrays["logf_sample"]
    m.gla_prompt, m.gla_sample, m.conv_prompt, m.conv_sample = arrays["gla_prompt"], arrays["gla_sample"], arrays["conv_prompt"], arrays["conv_sample"]
    m.pool_prompt, m.pool_sample = arrays["pool_prompt"], arrays["pool_sample"]
    m.h2d = nc.dram_tensor("normed_rows", (TOK, D), F32, kind="Internal").ap()
    m.slot_tok = nc.dram_tensor("slot_tokens", (SLOT_TILES * P, 1), I32, kind="Internal").ap()
    m.yd = nc.dram_tensor("slot_rows", (SLOT_TILES * P, D), F32, kind="Internal").ap()
    program(nc, m)


def kernel(**inputs):
    import numpy as np
    import concourse.bacc as bacc
    from concourse.bass_utils import run_bass_kernel_spmd

    nc = bacc.Bacc("TRN2", target_bir_lowering=False, num_devices=1)
    arrays, handles = {}, {}
    for name, a in inputs.items():
        arrays["in_" + name] = np.ascontiguousarray(a)
        handles[name] = nc.dram_tensor("in_" + name, arrays["in_" + name].shape, mybir.dt.from_np(arrays["in_" + name].dtype),
                                       kind="ExternalInput").ap()
    for name, shape in OUTS:
        handles[name] = nc.dram_tensor("out_" + name, shape, F32, kind="ExternalOutput").ap()
    build(nc, handles)
    r = run_bass_kernel_spmd(nc, [arrays], core_ids=[0])
    return tuple(r.results[0]["out_" + name] for name, _ in OUTS)
```
